# Optimizing a Trainium2 kernel written in Bass

```python
import math
import jax, jax.numpy as jnp
from jax import lax
import numpy as np

D_MODEL = 1024
BATCH = 1
SEQ = 256
DEPTH = 2

D_MIX = D_MODEL
HEAD_DIM = 64
N_Q_HEADS = 8
N_KV_HEADS = 2
GQA_GROUP = N_Q_HEADS // N_KV_HEADS
D_ATTN = N_Q_HEADS * HEAD_DIM
D_KV = N_KV_HEADS * HEAD_DIM
WINDOW = 128
ATT_BLOCK = 128
N_BUCKETS = 32
MAX_DISTANCE = 128
D_CONV = D_MIX // 4
CONV_WIDTH = 3
D_SGU = D_MIX // 4
SGU_GROUPS = 4
SGU_GROUP_DIM = D_SGU // SGU_GROUPS
SGU_CHUNK = 128
IN_SPLITS = (D_ATTN, D_KV, D_KV, D_CONV, D_CONV, D_CONV, D_SGU, D_SGU)
D_IN = D_ATTN + 2 * D_KV + 3 * D_CONV + 2 * D_SGU
PEER_HEADS = 8
PEER_TOPK = 16
N_KEYS = 128
N_EXPERTS = N_KEYS * N_KEYS
PEER_QDIM = 256
PEER_HALF = PEER_QDIM // 2
PEER_TOKEN_BLOCK = 128
EPS = 1e-6
NEG_INF = -1e30


def rms_norm(x, g):
    xf = x.astype(jnp.float32)
    y = xf * lax.rsqrt(jnp.mean(xf * xf, axis=-1, keepdims=True) + EPS)
    return (y * g.astype(jnp.float32)).astype(x.dtype)

def t5_causal_bucket(dist):
    max_exact = N_BUCKETS // 2
    d = jnp.maximum(dist, 0)
    log_ratio = jnp.log(jnp.maximum(d, 1).astype(jnp.float32) / max_exact) / math.log(MAX_DISTANCE / max_exact)
    large = max_exact + (log_ratio * (N_BUCKETS - max_exact)).astype(jnp.int32)
    large = jnp.minimum(large, N_BUCKETS - 1)
    return jnp.where(d < max_exact, d, large)

def sliding_window_attention(q, k, v, sink, rel_bias):
    B, S = q.shape[0], q.shape[1]
    nb = S // ATT_BLOCK
    qb = q.reshape(B, nb, ATT_BLOCK, N_KV_HEADS, GQA_GROUP, HEAD_DIM)
    kb = k.reshape(B, nb, ATT_BLOCK, N_KV_HEADS, HEAD_DIM)
    vb = v.reshape(B, nb, ATT_BLOCK, N_KV_HEADS, HEAD_DIM)

    def with_prev(t):
        prev = jnp.pad(t[:, :-1], ((0, 0), (1, 0), (0, 0), (0, 0), (0, 0)))
        return jnp.concatenate([prev, t], axis=2)

    kw, vw = with_prev(kb), with_prev(vb)
    logits = jnp.einsum('bnqkgd,bnskd->bnkgqs', qb, kw,
                        preferred_element_type=jnp.float32) * (HEAD_DIM ** -0.5)
    q_idx = jnp.arange(ATT_BLOCK)[:, None]
    s_idx = jnp.arange(2 * ATT_BLOCK)[None, :]
    dist = q_idx + ATT_BLOCK - s_idx
    in_window = (dist >= 0) & (dist < WINDOW)
    blk = jnp.arange(nb)[:, None, None]
    key_exists = (blk * ATT_BLOCK + s_idx[None] - ATT_BLOCK) >= 0
    mask = in_window[None] & key_exists
    bias = rel_bias.astype(jnp.float32)[t5_causal_bucket(dist)]
    bias = bias.transpose(2, 0, 1).reshape(N_KV_HEADS, GQA_GROUP, ATT_BLOCK, 2 * ATT_BLOCK)
    logits = jnp.where(mask[None, :, None, None], logits + bias, NEG_INF)
    sink_l = sink.astype(jnp.float32).reshape(1, 1, N_KV_HEADS, GQA_GROUP, 1, 1)
    m = jnp.maximum(jnp.max(logits, axis=-1, keepdims=True), sink_l)
    p = jnp.exp(logits - m)
    p = p / (jnp.sum(p, axis=-1, keepdims=True) + jnp.exp(sink_l - m))
    out = jnp.einsum('bnkgqs,bnskd->bnqkgd', p.astype(v.dtype), vw)
    return out.reshape(B, S, D_ATTN)

def short_conv_mixer(b_gate, c_gate, h, conv_w):
    S = h.shape[1]
    z = c_gate * h
    zp = jnp.pad(z, ((0, 0), (CONV_WIDTH - 1, 0), (0, 0)))
    conv = zp[:, 0:S] * conv_w[0]
    for j in range(1, CONV_WIDTH):
        conv = conv + zp[:, j:j + S] * conv_w[j]
    return b_gate * conv

def chunked_spatial_gating(u, v, w_s, b_s):
    B, S = u.shape[0], u.shape[1]
    nc = S // SGU_CHUNK
    vf = v.astype(jnp.float32).reshape(B, S, SGU_GROUPS, SGU_GROUP_DIM)
    mu = jnp.mean(vf, axis=-1, keepdims=True)
    var = jnp.mean(jnp.square(vf - mu), axis=-1, keepdims=True)
    vn = ((vf - mu) * lax.rsqrt(var + EPS)).astype(v.dtype)
    vn = vn.reshape(B, nc, SGU_CHUNK, SGU_GROUPS, SGU_GROUP_DIM)
    causal = jnp.tril(jnp.ones((SGU_CHUNK, SGU_CHUNK), dtype=w_s.dtype))
    w = w_s * causal[None]
    mixed = jnp.einsum('gts,bnsgc->bntgc', w, vn) + b_s.T[None, None, :, :, None]
    return u * mixed.reshape(B, S, D_SGU)

def peer_ffn(h, w_pq, sub_keys, expert_down, expert_up):
    B, S, D = h.shape
    tokens = h.reshape(-1, PEER_TOKEN_BLOCK, D)

    def block(t):
        T = t.shape[0]
        q = (t @ w_pq).reshape(T, PEER_HEADS, 2, PEER_HALF)
        s = jnp.einsum('thpk,hpnk->thpn', q, sub_keys, preferred_element_type=jnp.float32)
        top_s, top_i = lax.top_k(s, PEER_TOPK)
        cand_s = top_s[:, :, 0, :, None] + top_s[:, :, 1, None, :]
        cand_i = top_i[:, :, 0, :, None] * N_KEYS + top_i[:, :, 1, None, :]
        best_s, best_pos = lax.top_k(cand_s.reshape(T, PEER_HEADS, PEER_TOPK * PEER_TOPK), PEER_TOPK)
        experts = jnp.take_along_axis(cand_i.reshape(T, PEER_HEADS, PEER_TOPK * PEER_TOPK), best_pos, axis=-1)
        gate = jax.nn.softmax(best_s, axis=-1)
        u = expert_down[experts]
        act = jax.nn.gelu(jnp.einsum('td,thkd->thk', t, u, preferred_element_type=jnp.float32),
                          approximate=False)
        wgt = (gate * act).astype(t.dtype)
        vv = expert_up[experts]
        return jnp.einsum('thk,thkd->td', wgt, vv)

    return lax.map(block, tokens).reshape(B, S, D)

def hybrid_layer(x, c_act, rel_bias, w_ada, b_ada, norm1_g, norm2_g, w_in, q_norm_g, k_norm_g,
                 attn_sink, conv_w, sgu_w, sgu_b, out_norm_g, w_out, peer_wq, peer_sub_keys,
                 peer_down, peer_up):
    B, S = x.shape[0], x.shape[1]
    mod = (c_act @ w_ada + b_ada)[:, None, :]
    sh1, sc1, g1, sh2, sc2, g2 = jnp.split(mod, 6, axis=-1)
    h = rms_norm(x, norm1_g) * (1 + sc1) + sh1
    proj = h @ w_in
    split_pts = [int(i) for i in np.cumsum(IN_SPLITS)[:-1]]
    q, k, v, cb, cc, ch, su, sv = jnp.split(proj, split_pts, axis=-1)
    q = rms_norm(q.reshape(B, S, N_Q_HEADS, HEAD_DIM), q_norm_g)
    k = rms_norm(k.reshape(B, S, N_KV_HEADS, HEAD_DIM), k_norm_g)
    v = v.reshape(B, S, N_KV_HEADS, HEAD_DIM)
    y_attn = sliding_window_attention(q, k, v, attn_sink, rel_bias)
    y_conv = short_conv_mixer(cb, cc, ch, conv_w)
    y_sgu = chunked_spatial_gating(su, sv, sgu_w, sgu_b)
    ga, gc, gs = jnp.split(out_norm_g, [D_ATTN, D_ATTN + D_CONV])
    merged = jnp.concatenate([rms_norm(y_attn, ga), rms_norm(y_conv, gc), rms_norm(y_sgu, gs)], axis=-1)
    x = x + g1 * (merged @ w_out)
    h2 = rms_norm(x, norm2_g) * (1 + sc2) + sh2
    x = x + g2 * peer_ffn(h2, peer_wq, peer_sub_keys, peer_down, peer_up)
    return x

def first_inputs(seed: int = 0) -> dict:
    key = jax.random.key(seed)
    ks = jax.random.split(key, 20)
    f32 = jnp.float32
    nrm = lambda k, shape, s: jax.random.normal(k, shape, f32) * s
    return {
        "x": nrm(ks[0], (BATCH, SEQ, D_MODEL), 1.0),
        "c": nrm(ks[1], (BATCH, D_MODEL), 1.0),
        "rel_bias": nrm(ks[2], (N_BUCKETS, N_Q_HEADS), 0.5),
        "w_ada": nrm(ks[3], (DEPTH, D_MODEL, 6 * D_MODEL), 0.5 * D_MODEL ** -0.5),
        "b_ada": nrm(ks[4], (DEPTH, 6 * D_MODEL), 0.02),
        "norm1_g": 1.0 + nrm(ks[5], (DEPTH, D_MODEL), 0.02),
        "norm2_g": 1.0 + nrm(ks[6], (DEPTH, D_MODEL), 0.02),
        "w_in": nrm(ks[7], (DEPTH, D_MODEL, D_IN), D_MODEL ** -0.5),
        "q_norm_g": 1.0 + nrm(ks[8], (DEPTH, HEAD_DIM), 0.02),
        "k_norm_g": 1.0 + nrm(ks[9], (DEPTH, HEAD_DIM), 0.02),
        "attn_sink": nrm(ks[10], (DEPTH, N_Q_HEADS), 0.5),
        "conv_w": nrm(ks[11], (DEPTH, CONV_WIDTH, D_CONV), CONV_WIDTH ** -0.5),
        "sgu_w": nrm(ks[12], (DEPTH, SGU_GROUPS, SGU_CHUNK, SGU_CHUNK), SGU_CHUNK ** -0.5),
        "sgu_b": 1.0 + nrm(ks[13], (DEPTH, SGU_GROUPS, SGU_CHUNK), 0.02),
        "out_norm_g": 1.0 + nrm(ks[14], (DEPTH, D_MIX), 0.02),
        "w_out": nrm(ks[15], (DEPTH, D_MIX, D_MODEL), D_MIX ** -0.5),
        "peer_wq": nrm(ks[16], (DEPTH, D_MODEL, PEER_HEADS * PEER_QDIM), D_MODEL ** -0.5),
        "peer_sub_keys": nrm(ks[17], (DEPTH, PEER_HEADS, 2, N_KEYS, PEER_HALF), PEER_HALF ** -0.5),
        "peer_down": nrm(ks[18], (DEPTH, N_EXPERTS, D_MODEL), D_MODEL ** -0.5),
        "peer_up": nrm(ks[19], (DEPTH, N_EXPERTS, D_MODEL), 0.5 * PEER_HEADS ** -0.5),
    }

def first_block(x, c, rel_bias, w_ada, b_ada, norm1_g, norm2_g, w_in, q_norm_g, k_norm_g, attn_sink,
              conv_w, sgu_w, sgu_b, out_norm_g, w_out, peer_wq, peer_sub_keys, peer_down, peer_up):
    c_act = jax.nn.silu(c)
    for l in range(DEPTH):
        x = hybrid_layer(x, c_act, rel_bias, w_ada[l], b_ada[l], norm1_g[l], norm2_g[l], w_in[l],
                         q_norm_g[l], k_norm_g[l], attn_sink[l], conv_w[l], sgu_w[l], sgu_b[l],
                         out_norm_g[l], w_out[l], peer_wq[l], peer_sub_keys[l], peer_down[l], peer_up[l])
    return x


CHUNK = 64
N_MIXERS = 2
N_GLA_LAYERS = (DEPTH + 1) // 2
N_LRU_LAYERS = DEPTH // 2

GLA_HEADS = 4
GLA_DK = D_MODEL // 2 // GLA_HEADS
GLA_DV = D_MODEL // GLA_HEADS
GLA_QK = GLA_HEADS * GLA_DK
GLA_VD = GLA_HEADS * GLA_DV
GLA_GATE_RANK = 16
GLA_GATE_TAU = 16.0
GLA_IN = 2 * GLA_QK + 2 * GLA_VD + GLA_GATE_RANK

LRU_WIDTH = D_MODEL
LRU_BLOCKS = 4
LRU_BLOCK_W = LRU_WIDTH // LRU_BLOCKS
CONV_W = 4
LRU_C = 8.0

N_EXPERTS_2 = 16
N_GROUPS = 4
EXPERTS_PER_GROUP = N_EXPERTS_2 // N_GROUPS
TOP_K = 2
D_EXPERT = 512


def rmsnorm(x, g):
    x32 = x.astype(jnp.float32)
    inv = lax.rsqrt(jnp.mean(x32 * x32, axis=-1, keepdims=True) + EPS)
    return (x32 * inv).astype(x.dtype) * g

def modulate(h, shift, scale):
    return h * (1 + scale[:, None]) + shift[:, None]

def gla_mixer(h, w_in, w_gate_up, b_gate, norm_g, w_out):
    B, S, _ = h.shape
    N = S // CHUNK
    proj = h @ w_in
    q, k, v, g, a_lr = jnp.split(
        proj, [GLA_QK, 2 * GLA_QK, 2 * GLA_QK + GLA_VD, 2 * GLA_QK + 2 * GLA_VD], axis=-1)
    log_a = jax.nn.log_sigmoid((a_lr @ w_gate_up + b_gate).astype(jnp.float32)) / GLA_GATE_TAU

    def chunked(t, d):
        return t.reshape(B, N, CHUNK, GLA_HEADS, d)

    q = chunked(q, GLA_DK) * (GLA_DK ** -0.5)
    k = chunked(k, GLA_DK)
    v = chunked(v, GLA_DV)
    cum = jnp.cumsum(chunked(log_a, GLA_DK), axis=2)
    total = cum[:, :, -1]
    k_dec = k * jnp.exp(total[:, :, None] - cum).astype(k.dtype)
    gamma = jnp.exp(total).astype(h.dtype)

    def step(s_prev, xs):
        qn, kn, vn, gn = xs
        inter = jnp.einsum('bchk,bhkv->bchv', qn * gn[:, None], s_prev)
        scores = jnp.einsum('bchk,bshk->bhcs', qn, kn)
        intra = jnp.einsum('bhcs,bshv->bchv', scores, vn)
        s_new = gn[..., None] * s_prev + jnp.einsum('bshk,bshv->bhkv', kn, vn)
        return s_new, inter + intra

    s0 = jnp.zeros((B, GLA_HEADS, GLA_DK, GLA_DV), h.dtype)
    xs = (jnp.moveaxis(q, 1, 0), jnp.moveaxis(k_dec, 1, 0),
          jnp.moveaxis(v, 1, 0), jnp.moveaxis(gamma, 1, 0))
    _, o = lax.scan(step, s0, xs)
    o = jnp.moveaxis(o, 0, 1).reshape(B, S, GLA_HEADS, GLA_DV)
    o = rmsnorm(o, norm_g) * jax.nn.silu(g).reshape(B, S, GLA_HEADS, GLA_DV)
    return o.reshape(B, S, GLA_VD) @ w_out

def lru_mixer(h, w_in, conv_w, conv_b, w_r, b_r, w_i, b_i, lam, w_out):
    B, S, _ = h.shape
    proj = h @ w_in
    gate_br, xb = jnp.split(proj, 2, axis=-1)
    xp = jnp.pad(xb, ((0, 0), (CONV_W - 1, 0), (0, 0)))
    xc = conv_b + sum(xp[:, j:j + S] * conv_w[j] for j in range(CONV_W))
    xg = xc.reshape(B, S, LRU_BLOCKS, LRU_BLOCK_W)
    r = jax.nn.sigmoid(jnp.einsum('bshi,hij->bshj', xg, w_r) + b_r).reshape(B, S, LRU_WIDTH)
    i = jax.nn.sigmoid(jnp.einsum('bshi,hij->bshj', xg, w_i) + b_i).reshape(B, S, LRU_WIDTH)
    log_a = (-LRU_C * r.astype(jnp.float32)) * jax.nn.softplus(-lam.astype(jnp.float32))
    a = jnp.exp(log_a)
    mult = jnp.sqrt(-jnp.expm1(2.0 * log_a))
    b = (xc * i).astype(jnp.float32) * mult

    def combine(left, right):
        a1, b1 = left
        a2, b2 = right
        return a1 * a2, a2 * b1 + b2

    _, hs = lax.associative_scan(combine, (a, b), axis=1)
    y = hs.astype(h.dtype) * jax.nn.gelu(gate_br)
    return y @ w_out

def grouped_moe(h, router_w, router_bias, w_gate, w_up, w_down):
    B, S, D = h.shape
    t = h.reshape(-1, D)
    scores = jax.nn.sigmoid((t @ router_w).astype(jnp.float32))
    sel = scores + router_bias.astype(jnp.float32)
    grouped = sel.reshape(-1, N_GROUPS, EXPERTS_PER_GROUP)
    group_score = lax.top_k(grouped, TOP_K)[0].sum(-1)
    grp = jnp.argmax(group_score, axis=-1)
    in_group = jnp.take_along_axis(grouped, grp[:, None, None], axis=1)[:, 0]
    _, local = lax.top_k(in_group, TOP_K)
    expert_idx = grp[:, None] * EXPERTS_PER_GROUP + local
    w = jnp.take_along_axis(scores, expert_idx, axis=1)
    w = w / jnp.sum(w, axis=-1, keepdims=True)
    combine = jnp.sum(jax.nn.one_hot(expert_idx, N_EXPERTS_2, dtype=jnp.float32) * w[..., None], axis=1)
    combine = combine.astype(t.dtype)
    out = jnp.zeros_like(t)
    for e in range(N_EXPERTS_2):
        he = jax.nn.silu(t @ w_gate[e]) * (t @ w_up[e])
        out = out + combine[:, e:e + 1] * (he @ w_down[e])
    return out.reshape(B, S, D)

def second_inputs(seed: int = 0) -> dict:
    key = jax.random.key(seed)
    ks = iter(jax.random.split(key, 40))
    f32 = jnp.float32

    def nrm(shape, scale):
        return jax.random.normal(next(ks), shape, f32) * scale

    def gain(shape):
        return 1.0 + nrm(shape, 0.05)

    D = D_MODEL
    p = {}
    p["x"] = nrm((BATCH, SEQ, D), 1.0)
    p["c"] = nrm((BATCH, D), 1.0)
    p["gla_w_in"] = nrm((N_GLA_LAYERS, D, GLA_IN), D ** -0.5)
    p["gla_w_gate_up"] = nrm((N_GLA_LAYERS, GLA_GATE_RANK, GLA_QK), GLA_GATE_RANK ** -0.5)
    p["gla_b_gate"] = nrm((N_GLA_LAYERS, GLA_QK), 0.1)
    p["gla_norm_g"] = gain((N_GLA_LAYERS, GLA_DV))
    p["gla_w_out"] = nrm((N_GLA_LAYERS, GLA_VD, D), GLA_VD ** -0.5)
    p["lru_w_in"] = nrm((N_LRU_LAYERS, D, 2 * LRU_WIDTH), D ** -0.5)
    p["lru_conv_w"] = nrm((N_LRU_LAYERS, CONV_W, LRU_WIDTH), CONV_W ** -0.5)
    p["lru_conv_b"] = nrm((N_LRU_LAYERS, LRU_WIDTH), 0.02)
    p["lru_w_r"] = nrm((N_LRU_LAYERS, LRU_BLOCKS, LRU_BLOCK_W, LRU_BLOCK_W), LRU_BLOCK_W ** -0.5)
    p["lru_b_r"] = nrm((N_LRU_LAYERS, LRU_BLOCKS, LRU_BLOCK_W), 0.02)
    p["lru_w_i"] = nrm((N_LRU_LAYERS, LRU_BLOCKS, LRU_BLOCK_W, LRU_BLOCK_W), LRU_BLOCK_W ** -0.5)
    p["lru_b_i"] = nrm((N_LRU_LAYERS, LRU_BLOCKS, LRU_BLOCK_W), 0.02)
    u = jax.random.uniform(next(ks), (N_LRU_LAYERS, LRU_WIDTH), f32, 0.9, 0.999)
    a_base = u ** (1.0 / LRU_C)
    p["lru_lambda"] = jnp.log(a_base) - jnp.log1p(-a_base)
    p["lru_w_out"] = nrm((N_LRU_LAYERS, LRU_WIDTH, D), LRU_WIDTH ** -0.5)
    p["router_w"] = nrm((D, N_EXPERTS_2), D ** -0.5)
    p["router_bias"] = nrm((N_EXPERTS_2,), 0.01)
    p["moe_w_gate"] = nrm((DEPTH, N_EXPERTS_2, D, D_EXPERT), D ** -0.5)
    p["moe_w_up"] = nrm((DEPTH, N_EXPERTS_2, D, D_EXPERT), D ** -0.5)
    p["moe_w_down"] = nrm((DEPTH, N_EXPERTS_2, D_EXPERT, D), D_EXPERT ** -0.5)
    p["norm_mix_g"] = gain((DEPTH, D))
    p["norm_ffn_g"] = gain((DEPTH, D))
    p["ada_w"] = nrm((DEPTH, D, 6 * D), 0.5 * D ** -0.5)
    p["ada_b"] = nrm((DEPTH, 6 * D), 0.02)
    p["final_norm_g"] = gain((D,))
    return p

def second_block(x, c, gla_w_in, gla_w_gate_up, gla_b_gate, gla_norm_g, gla_w_out,
              lru_w_in, lru_conv_w, lru_conv_b, lru_w_r, lru_b_r, lru_w_i, lru_b_i,
              lru_lambda, lru_w_out, router_w, router_bias, moe_w_gate, moe_w_up,
              moe_w_down, norm_mix_g, norm_ffn_g, ada_w, ada_b, final_norm_g):
    cond = jax.nn.silu(c)
    for i in range(DEPTH):
        sh1, sc1, g1, sh2, sc2, g2 = jnp.split(cond @ ada_w[i] + ada_b[i], 6, axis=-1)
        h = modulate(rmsnorm(x, norm_mix_g[i]), sh1, sc1)
        j = i // N_MIXERS
        if i % N_MIXERS == 0:
            mix = gla_mixer(h, gla_w_in[j], gla_w_gate_up[j], gla_b_gate[j],
                            gla_norm_g[j], gla_w_out[j])
        else:
            mix = lru_mixer(h, lru_w_in[j], lru_conv_w[j], lru_conv_b[j], lru_w_r[j],
                            lru_b_r[j], lru_w_i[j], lru_b_i[j], lru_lambda[j], lru_w_out[j])
        x = x + g1[:, None] * mix
        h = modulate(rmsnorm(x, norm_ffn_g[i]), sh2, sc2)
        x = x + g2[:, None] * grouped_moe(h, router_w, router_bias,
                                          moe_w_gate[i], moe_w_up[i], moe_w_down[i])
    return rmsnorm(x, final_norm_g)


def setup_inputs(seed=0):
    out = dict(first_inputs(seed))
    for name, value in second_inputs(seed + 1).items():
        if name != "x":
            out[name + "_2"] = value
    return out


def reference(
    x, c, rel_bias, w_ada, b_ada, norm1_g, norm2_g, w_in, q_norm_g, k_norm_g, attn_sink, conv_w,
    sgu_w, sgu_b, out_norm_g, w_out, peer_wq, peer_sub_keys, peer_down, peer_up, c_2,
    gla_w_in_2, gla_w_gate_up_2, gla_b_gate_2, gla_norm_g_2, gla_w_out_2, lru_w_in_2,
    lru_conv_w_2, lru_conv_b_2, lru_w_r_2, lru_b_r_2, lru_w_i_2, lru_b_i_2, lru_lambda_2,
    lru_w_out_2, router_w_2, router_bias_2, moe_w_gate_2, moe_w_up_2, moe_w_down_2,
    norm_mix_g_2, norm_ffn_g_2, ada_w_2, ada_b_2, final_norm_g_2,
):
    x = first_block(
        x, c, rel_bias, w_ada, b_ada, norm1_g, norm2_g, w_in, q_norm_g, k_norm_g, attn_sink,
        conv_w, sgu_w, sgu_b, out_norm_g, w_out, peer_wq, peer_sub_keys, peer_down, peer_up,
    )
    return second_block(
        x, c_2, gla_w_in_2, gla_w_gate_up_2, gla_b_gate_2, gla_norm_g_2, gla_w_out_2,
        lru_w_in_2, lru_conv_w_2, lru_conv_b_2, lru_w_r_2, lru_b_r_2, lru_w_i_2, lru_b_i_2,
        lru_lambda_2, lru_w_out_2, router_w_2, router_bias_2, moe_w_gate_2, moe_w_up_2,
        moe_w_down_2, norm_mix_g_2, norm_ffn_g_2, ada_w_2, ada_b_2, final_norm_g_2,
    )


_drawn_inputs = setup_inputs


def setup_inputs(seed=0):
    import zlib

    import numpy as np

    out = dict(_drawn_inputs(seed))
    spreads = {}
    factors = {'norm2_g': 3.172,
     'q_norm_g': 4.447,
     'k_norm_g': 3.824,
     'attn_sink': 12.035,
     'sgu_b': 13.806,
     'lru_b_r_2': 30.224,
     'lru_b_i_2': 8.0,
     'gla_b_gate_2': 3.655,
     'gla_norm_g_2': 3.745}
    for name, (base, spread) in spreads.items():
        noise = np.random.default_rng([zlib.crc32(name.encode()), seed]).standard_normal(out[name].shape)
        drawn = base * np.exp(spread * noise) if base else spread * noise
        out[name] = __import__('jax').numpy.asarray(drawn.astype(out[name].dtype))
    for name, factor in factors.items():
        out[name] = (out[name] * factor).astype(out[name].dtype)
    return out
```

```python
from contextlib import ExitStack

import numpy as np

import concourse.bass as bass
from concourse import mybir

P = 128
D = 1024
KT = D // P
T = 256
TB = T // P
DEPTH = 2
LAYERS = 2 * DEPTH
EPS = 1e-6
NEG = -1e30

F32 = mybir.dt.float32
BF16 = mybir.dt.bfloat16
U32 = mybir.dt.uint32
ALU = mybir.AluOpType
ACT = mybir.ActivationFunctionType
AX = mybir.AxisListType.X

HEADS, KVH, HD = 8, 2, 64
BUCKETS, MAX_DIST = 32, 128
PH, TOPK, NKEYS = 8, 16, 128
EXPERTS, FE = 16, 512
GH, GDK, GDV, CHUNK, GRANK = 4, 128, 256, 64, 16
CONV2 = 4

SLOT = 16 * P
RING = 4
BANKS = 4
ADA_RING = 3
QUARTERS = 4
QT_TILES = NKEYS // QUARTERS
QT_SLOTS = QT_TILES // 2
GROUP = 512 // QT_TILES
EXP_SLOTS = 6


def plan():
    slot, unit, s, u = {}, {}, 0, 0

    def stage(name, slots, units):
        nonlocal s, u
        slot[name], unit[name] = s, u
        s += slots
        u += units

    for l in range(LAYERS):
        stage(("mod", l), 0, 1)
        stage(("norm", 2 * l), 0, 1)
        if l < DEPTH:
            stage(("q", l), 2, 2)
            stage(("kv", l), 1, 1)
            stage(("sgu", l), 2, 2)
            stage(("conv", l), 3, 3)
            stage(("qkT", l), 0, 3)
            stage(("scores", l), 0, 6)
            stage(("conv_sum", l), 0, 1)
            stage(("mix", l), 0, 1)
            stage(("PT", l), 0, 6)
            stage(("PV", l), 0, 2)
            stage(("sguT", l), 0, 1)
            stage(("attnT", l), 0, 2)
        elif l == DEPTH:
            stage(("gq", l), 2, 2)
            stage(("alr", l), 0, 1)
            stage(("z", l), 0, 2)
            stage(("gk", l), 2, 2)
            stage(("gv", l), 4, 4)
            stage(("gg", l), 4, 4)
            stage(("decay", l), 0, 2)
            stage(("gamma", l), 0, 1)
            stage(("kvs", l), 0, 8)
            stage(("oT", l), 0, 4)
        else:
            stage(("lru_g", l), 4, 4)
            stage(("lru_x", l), 4, 4)
            stage(("lru_r", l), 1, 4)
            stage(("lru_i", l), 1, 4)
        stage(("out", l), 4, 4)
        stage(("norm", 2 * l + 1), 0, 1)
        if l < DEPTH:
            stage(("pq", l), 8, 8)
            stage(("keys", l), 1, 8)
            stage(("down", l, 0), QT_SLOTS, QT_SLOTS)
            stage(("idxT", l), 0, 2)
            stage(("down", l, 1), QT_SLOTS, 2 * QT_SLOTS)
            stage(("up", l, 0), QT_SLOTS, QT_SLOTS)
            stage(("down", l, 2), QT_SLOTS, QT_SLOTS)
            stage(("up", l, 1), QT_SLOTS, QT_SLOTS)
            stage(("down", l, 3), QT_SLOTS, QT_SLOTS)
            stage(("up", l, 2), QT_SLOTS, QT_SLOTS)
            stage(("up", l, 3), QT_SLOTS, 0)
        else:
            stage(("router", l), 0, 1)
            stage(("combT", l), 0, 1)
            stage(("comb", l), 0, 8)
            stage(("experts", l), EXPERTS * EXP_SLOTS, EXPERTS * 4)
    stage(("norm", 2 * LAYERS), 0, 1)
    slot["end"] = s
    assert s % RING == 0
    return slot, unit


SLOT_OF, UNIT_OF = plan()

COLS = {}


def _cols():
    n = 0
    for name, w in (
        [("c", 8), ("c2", 8), ("final_g", 8)]
        + [((k, l), w) for l in range(LAYERS) for k, w in (("b_ada", 48), ("g1", 8), ("g2", 8))]
        + [((k, l), w) for l in range(DEPTH)
           for k, w in (("gq", 1), ("gk", 1), ("cw", 6), ("og", 8), ("sb", 4), ("sink", 8))]
        + [("lcw", 32), ("lcb", 8), ("lbr", 8), ("lbi", 8), ("lam", 8), ("rw", 128), ("rb", 16)]
    ):
        COLS[name] = (n, w)
        n += w
    COLS["end"] = (n, 0)


_cols()
NCOLS = COLS["end"][0]

ROOM = 26624
ACT0, ACT1, TOP = 0, 8192, 16384
MT, SQ = ACT1, ACT1 + 2048
L1 = dict(bias=0, sgw=2048, qk=2560, v=3840, suv=4096, cb=5120, cc=5632, z=6144, yc=6660, kT=7172,
          vn=7428, lg=12288, pp=14336, pT=16384, qT=19456, ya=20480, ys=21504, sq2=22016, sq3=22528,
          rc=23552, tmp=23808)
FIRST_CONST = 2560
GLA_CONST = 512 + 256 + 512 + 128
L2 = dict(bg=0, ng=512, wgu=768, wa=1280, qT=1408, k=2432, v=3456, gs=5504, alr=7552,
          lg=12288, e=13312, kd=14336, az=15360, S=16384, o=18432, osq=20480, gam=22528, zz=22560)
L3 = dict(gate=0, xp=2048, xc=4120, r=24576, i=12288, a=14336, t=16384, m=18432, b=20480, hs=22528)
MOE = dict(cb=16384, he=0, si=2048, cT=20480)


def program(nc, x, w, ada, small, first_const, gla_const, out):
    with ExitStack() as ctx:
        def sb(name, shape, dt=F32):
            return ctx.enter_context(nc.sbuf_tensor(name, shape, dt))

        def sem(name):
            return ctx.enter_context(nc.semaphore(name))

        ring = sb("ring", [P, RING, SLOT])
        ada_ring = sb("ada_ring", [P, ADA_RING, D])
        ada_sum = sb("ada_sum", [P, 6 * D])
        xT = sb("xT", [P, KT, T])
        hT = sb("hT", [P, KT, T])
        arena = sb("arena", [P, ROOM])
        cols = sb("cols", [P, NCOLS])
        mod = sb("mod", [P, 48])
        gain = sb("gain", [P, 2, KT])
        cact = sb("cact", [P, 2, KT])
        rstd = sb("rstd", [P, T])
        ident = sb("ident", [P, P])
        iota = sb("iota", [P, P])
        ones = sb("ones", [P, P])
        one = sb("one", [P, 1])
        zeros = sb("zeros", [P, 512], BF16)
        st = sb("st", [P, 6, 32])
        tv = sb("tv", [P, 16, TOPK])
        ti = sb("ti", [P, 16, TOPK], U32)
        tf = sb("tf", [P, 16, TOPK])
        bv = sb("bv", [P, PH, TOPK])
        bp = sb("bp", [P, 3, PH * TOPK], U32)
        bf = sb("bf", [P, 2, PH * TOPK])
        pick = sb("pick", [P, 3, TB, P])
        pickT = sb("pickT", [P, 3, T])
        psr = sb("psr", [P, 16])
        sel = tf[:, :, :].rearrange("p (r a) k -> p r (a k)", a=2)
        seli = ti[:, 0:2, 0:8]
        later = sb("later", [P, P])
        chunk_of = sb("chunk_of", [P, 2])

        unit = [ctx.enter_context(nc.psum_tensor(f"unit{i}", [P, 512], F32)) for i in range(BANKS)]
        acc = [ctx.enter_context(nc.psum_tensor(f"acc{i}", [P, 512], F32)) for i in range(4)]

        slot_landed = [sem(f"slot_landed{i}") for i in range(RING)]
        slot_read = [sem(f"slot_read{i}") for i in range(RING)]
        ada_landed = [sem(f"ada_landed{i}") for i in range(ADA_RING)]
        ada_read = [sem(f"ada_read{i}") for i in range(ADA_RING)]
        unit_full = [sem(f"unit_full{i}") for i in range(BANKS)]
        unit_taken = [sem(f"unit_taken{i}") for i in range(BANKS)]
        dve_step, act_step, pool_step = sem("dve_step"), sem("act_step"), sem("pool_step")
        x_landed, cols_landed, const_landed = sem("x_landed"), sem("cols_landed"), sem("const_landed")
        consts_made = sem("consts_made")
        c_ready = sem("c_ready")
        x_ready, sq_ready, std_ready, h_ready = (
            sem("x_ready"), sem("sq_ready"), sem("std_ready"), sem("h_ready"))
        acc_full, o_full = sem("acc_full"), sem("o_full")
        bias_masked = sem("bias_masked")
        qk_var, qk_std, qk_ready = sem("qk_var"), sem("qk_std"), sem("qk_ready")
        yc_ready, yc_sq, yc_std = sem("yc_ready"), sem("yc_sq"), sem("yc_std")
        vn_var, vn_std, vn_ready = sem("vn_var"), sem("vn_std"), sem("vn_ready")
        lg_ready, exp_done = sem("lg_ready"), sem("exp_done")
        ys_var, ys_std, ys_ready = sem("ys_var"), sem("ys_std"), sem("ys_ready")
        ya_var, ya_std, ya_ready = sem("ya_var"), sem("ya_std"), sem("ya_ready")
        m_ready = sem("m_ready")
        best_ready, gate_exp, pick_ready = sem("best_ready"), sem("gate_exp"), sem("pick_ready")
        hot_ready = sem("hot_ready")
        z_ready, soft_done, la_ready, kd_ready = (
            sem("z_ready"), sem("soft_done"), sem("la_ready"), sem("kd_ready"))
        o_var, o_std, o_ready = sem("o_var"), sem("o_std"), sem("o_ready")
        xc_ready, lam_abs, lam_exp, lam_ready = sem("xc_ready"), sem("lam_abs"), sem("lam_exp"), sem("lam_ready")
        tanh_done, m_sq, m_root = sem("tanh_done"), sem("m_sq"), sem("m_root")
        comb_ready, he_ready = sem("comb_ready"), sem("he_ready")
        stored = sem("stored")

        def room(at, *shape):
            n = int(np.prod(shape))
            v = arena[:, at:at + n]
            if len(shape) == 2:
                v = v.rearrange("p (a b) -> p a b", b=shape[1])
            elif len(shape) == 3:
                v = v.rearrange("p (a b c) -> p a b c", b=shape[1], c=shape[2])
            return v

        def col(name, i=None):
            at, n = COLS[name]
            return cols[:, at:at + n] if i is None else cols[:, at + i:at + i + 1]

        mT = room(MT, KT, T)
        sq = room(SQ, KT, T)

        class Steps:

            def __init__(self, eng, s):
                self.eng, self.sem, self.n, self.base = eng, s, 0, 0

            def __call__(self, ins):
                self.n += 1
                ins.then_inc(self.sem, 1)

            def sync(self, back=0):
                self.eng.wait_ge(self.sem, self.base + (self.n - back))

            def enter(self, it, per):
                self.base, self.per, self.at = it * per, per, self.n

            def leave(self, times):
                assert self.n - self.at == self.per, self.n - self.at
                self.base = 0
                self.n = self.at + self.per * times

        def upto(base, it, step):
            return base if it is None else it * step + base

        def wait_full(eng, u, it=None, per=0):
            eng.wait_ge(unit_full[u % BANKS], upto(u // BANKS + 1, it, per // BANKS))

        def wait_taken(eng, u, it=None, per=0):
            eng.wait_ge(unit_taken[u % BANKS], upto(u // BANKS + 1, it, per // BANKS))

        def bank(u):
            return unit[u % BANKS]

        block = ctx.enter_context(nc.Block())

        @block.sync
        def _(sp):
            sp.dma_start(cols[:, :], small).then_inc(cols_landed, 16)
            sp.dma_start(xT[:, :, :], x.rearrange("(k p) t -> p k t", p=P)).then_inc(x_landed, 16)
            for s in range(RING):
                sp.dma_start(ring[:, s, :], w[s]).then_inc(slot_landed[s], 16)
            with sp.Fori(1, SLOT_OF["end"] // RING) as it:
                for s in range(RING):
                    sp.wait_ge(slot_read[s], it)
                    sp.dma_start(ring[:, s, :], w[it * RING + s]).then_inc(slot_landed[s], 16)
            sp.wait_ge(h_ready, 2 * LAYERS + 1)
            sp.dma_start(out.rearrange("(k p) t -> p k t", p=P), hT[:, :, :]).then_inc(stored, 16)
            sp.wait_ge(stored, 16)

        @block.gpsimd
        def _(pool):
            g = nc.gpsimd
            steps = Steps(pool, pool_step)

            def ada_load(lo, hi):
                flat = ada.rearrange("l a p d -> (l a) p d")
                if lo == 0:
                    for s in range(ADA_RING):
                        pool.dma_start(ada_ring[:, s, :], flat[s]).then_inc(ada_landed[s], 16)
                    lo = ADA_RING
                with pool.Fori(lo // ADA_RING, hi // ADA_RING) as it:
                    for s in range(ADA_RING):
                        pool.wait_ge(ada_read[s], it)
                        pool.dma_start(ada_ring[:, s, :], flat[it * ADA_RING + s]).then_inc(
                            ada_landed[s], 16)

            steps(g.memset(ident[:, :], 0.0))
            steps(g.memset(later[:, :], 1.0 / 16.0))
            steps(g.memset(chunk_of[:, :], 1.0 / 16.0))
            steps(g.memset(ones[:, :], 1.0 / D))
            steps(g.memset(one[:, :], 1.0))
            steps(g.iota(iota[:, :], pattern=[[1, P]], base=0, channel_multiplier=0,
                         allow_small_or_imprecise_dtypes=True))
            steps.sync()
            steps(g.affine_select(out=ident[:, :], in_=ident[:, :], compare_op=ALU.not_equal,
                                  fill=1.0, base=0, pattern=[[-1, P]], channel_multiplier=1))
            steps(g.affine_select(out=later[:, :], in_=later[:, :], compare_op=ALU.is_gt,
                                  fill=0.0, base=0, pattern=[[-1, P]], channel_multiplier=1))
            steps(g.affine_select(out=chunk_of[:, 0:1], in_=chunk_of[:, 0:1], compare_op=ALU.is_ge,
                                  fill=0.0, base=CHUNK - 1, pattern=[[0, 1]], channel_multiplier=-1))
            steps(g.affine_select(out=chunk_of[:, 1:2], in_=chunk_of[:, 1:2], compare_op=ALU.is_ge,
                                  fill=0.0, base=-CHUNK, pattern=[[0, 1]], channel_multiplier=1))
            steps.sync()
            steps(g.memset(later[CHUNK:P, 0:CHUNK], 0.0))
            steps.sync()
            g.memset(zeros[:, :], 0.0).then_inc(consts_made, 1)

            def first_masks(l):
                pool.wait_ge(const_landed, 16 * (l + 1))
                b = room(L1["bias"], HEADS, T)
                steps(g.affine_select(out=b, in_=b, compare_op=ALU.is_ge, fill=NEG, base=P,
                                      pattern=[[0, HEADS], [-1, T]], channel_multiplier=1))
                steps.sync()
                steps(g.affine_select(out=b, in_=b, compare_op=ALU.is_gt, fill=NEG, base=0,
                                      pattern=[[0, HEADS], [1, T]], channel_multiplier=-1))
                steps.sync()
                wv = room(L1["sgw"], 4, P)
                g.affine_select(out=wv, in_=wv, compare_op=ALU.is_ge, fill=0.0, base=0,
                                pattern=[[0, 4], [1, P]], channel_multiplier=-1).then_inc(bias_masked, 1)

            pool.dma_start(arena[:, 0:FIRST_CONST], first_const[0]).then_inc(const_landed, 16)
            ada_load(0, 48)
            first_masks(0)
            for l in range(1, LAYERS):
                ada_load(48 * l, 48 * (l + 1))
                pool.wait_ge(x_ready, 2 * l)
                if l < DEPTH:
                    pool.dma_start(arena[:, 0:FIRST_CONST], first_const[l]).then_inc(const_landed, 16)
                    first_masks(l)
                elif l == DEPTH:
                    pool.dma_start(arena[:, 0:GLA_CONST], gla_const).then_inc(const_landed, 16)

        @block.tensor
        def _(pe):
            mm = nc.tensor.matmul

            def open_bank(u, it=None, per=0):
                if u >= BANKS:
                    wait_taken(pe, u - BANKS, it, per)

            def slot_mms(n, mms, it=None, ends=()):
                pe.wait_ge(slot_landed[n % RING], upto(16 * (n // RING + 1), it, 16))
                ends = dict(ends)
                for i, (o, a, b, start, stop) in enumerate(mms):
                    ins = mm(o, a, b, start=start, stop=stop, skip_group_check=True)
                    if i == 0 and n > 0:
                        ins.then_inc(slot_read[(n - 1) % RING], 1)
                    if i in ends:
                        ins.then_inc(ends[i], 1)

            def tile(n, i):
                return ring[:, n % RING, i * P:(i + 1) * P]

            def feature_slot(n, u, act, it=None, per=0):
                open_bank(u, it, per)
                mms = [(bank(u)[:, j * T:(j + 1) * T], tile(n, j * KT + k), act[:, k, :], k == 0, k == KT - 1)
                       for j in range(2) for k in range(KT)]
                slot_mms(n, mms, it, {15: unit_full[u % BANKS]})

            def token_slots(n, u, act):
                for b in range(TB):
                    open_bank(u + b)
                for s in range(2):
                    mms = [(bank(u + b)[:, :], act[:, 4 * s + k, b * P:(b + 1) * P],
                            ring[:, (n + s) % RING, k * 512:(k + 1) * 512], s + k == 0, s == 1 and k == 3)
                           for b in range(TB) for k in range(4)]
                    slot_mms(n + s, mms, None,
                             {3: unit_full[u % BANKS], 7: unit_full[(u + 1) % BANKS]} if s else {})

            def transposes(u, srcs):
                open_bank(u)
                for i, a in enumerate(srcs):
                    ins = nc.tensor.transpose(bank(u)[:, i * P:(i + 1) * P], a, ident[:, :])
                ins.then_inc(unit_full[u % BANKS], 1)

            def norm(i):
                pe.wait_ge(sq_ready, i + 1)
                u = UNIT_OF["norm", i]
                open_bank(u)
                for k in range(KT):
                    ins = mm(bank(u)[:, 0:T], ones[:, :], sq[:, k, :], start=k == 0, stop=k == KT - 1)
                ins.then_inc(unit_full[u % BANKS], 1)

            def mods(l):
                for s in range(ADA_RING):
                    pe.wait_ge(ada_read[s], (l + 1) * (48 // ADA_RING))
                u = UNIT_OF["mod", l]
                open_bank(u)
                for i in range(48):
                    ins = mm(bank(u)[:, i:i + 1], ada_sum[:, i * P:(i + 1) * P], one[:, :],
                             start=True, stop=True)
                ins.then_inc(unit_full[u % BANKS], 1)

            def out_proj(l):
                pe.wait_ge(m_ready, l + 1)
                for s in range(4):
                    feature_slot(SLOT_OF["out", l] + s, UNIT_OF["out", l] + s, mT)

            def clear_acc():
                for b in range(4):
                    mm(acc[b][:, :], zeros[:, 0:P], zeros[:, :], start=True, stop=False,
                       skip_group_check=True)

            def first_mixer(l):
                pe.wait_ge(h_ready, 2 * l + 1)
                token_slots(SLOT_OF["q", l], UNIT_OF["q", l], hT)
                n, u = SLOT_OF["kv", l], UNIT_OF["kv", l]
                open_bank(u)
                slot_mms(n, [(bank(u)[:, b * 256:(b + 1) * 256], hT[:, k, b * P:(b + 1) * P],
                              ring[:, n % RING, k * 256:(k + 1) * 256], k == 0, k == KT - 1)
                             for b in range(TB) for k in range(KT)], None, {15: unit_full[u % BANKS]})
                token_slots(SLOT_OF["sgu", l], UNIT_OF["sgu", l], hT)
                for s in range(3):
                    feature_slot(SLOT_OF["conv", l] + s, UNIT_OF["conv", l] + s, hT)
                qk = room(L1["qk"], TB, 640)
                pe.wait_ge(qk_ready, l + 1)
                u = UNIT_OF["qkT", l]
                transposes(u, [qk[:, b, 512:640] for b in range(TB)])
                for b in range(TB):
                    transposes(u + 1 + b, [qk[:, b, i * P:(i + 1) * P] for i in range(4)])
                qT, kT = room(L1["qT"], TB, 4, P), room(L1["kT"], T)
                u = UNIT_OF["scores", l]
                wait_taken(pe, UNIT_OF["qkT", l])
                for b in range(TB):
                    wait_taken(pe, UNIT_OF["qkT", l] + 1 + b)
                    nk = P * (b + 1)
                    per = 512 // nk
                    for c in range(HEADS // per):
                        open_bank(u)
                        for h in range(per):
                            j, i = divmod(c * per + h, 4)
                            ins = mm(bank(u)[:, h * nk:(h + 1) * nk], qT[64 * j:64 * j + 64, b, i, :],
                                     kT[64 * j:64 * j + 64, 0:nk], start=True, stop=True)
                        ins.then_inc(unit_full[u % BANKS], 1)
                        u += 1
                u = UNIT_OF["conv_sum", l]
                pe.wait_ge(yc_sq, l + 1)
                open_bank(u)
                s2 = room(L1["sq2"], 2, T)
                for k in range(2):
                    ins = mm(bank(u)[:, 0:T], ones[:, :], s2[:, k, :], start=k == 0, stop=k == 1)
                ins.then_inc(unit_full[u % BANKS], 1)
                u = UNIT_OF["mix", l]
                pe.wait_ge(vn_ready, l + 1)
                pe.wait_ge(bias_masked, l + 1)
                open_bank(u)
                sgw, vn = room(L1["sgw"], 4, P), room(L1["vn"], TB, 256)
                for b in range(TB):
                    for g in range(4):
                        ins = mm(bank(u)[:, b * 256 + g * 64:b * 256 + (g + 1) * 64], sgw[:, g, :],
                                 vn[:, b, g * 64:(g + 1) * 64], start=True, stop=True)
                ins.then_inc(unit_full[u % BANKS], 1)
                pp, pT = room(L1["pp"], HEADS, T), room(L1["pT"], 24, P)
                v = room(L1["v"], TB, P)
                u = UNIT_OF["PT", l]
                for b in range(TB):
                    pe.wait_ge(exp_done, 2 * l + b + 1)
                    flat = [pp[:, h, s * P:(s + 1) * P] for h in range(HEADS) for s in range(b + 1)]
                    for c in range(2 * (b + 1)):
                        transposes(u, flat[4 * c:4 * c + 4])
                        u += 1
                u = UNIT_OF["PV", l]
                for b in range(TB):
                    for c in range(2 * (b + 1)):
                        wait_taken(pe, UNIT_OF["PT", l] + 2 * b + c)
                    open_bank(u)
                    for h in range(HEADS):
                        for s in range(b + 1):
                            ins = mm(bank(u)[:, h * 64:(h + 1) * 64],
                                     pT[:, 8 * b + h * (b + 1) + s, :],
                                     v[:, s, h // 4 * 64:(h // 4 + 1) * 64], start=s == 0, stop=s == b)
                    ins.then_inc(unit_full[u % BANKS], 1)
                    u += 1
                ys, ya = room(L1["ys"], TB, 256), room(L1["ya"], TB, 512)
                pe.wait_ge(ys_ready, l + 1)
                transposes(UNIT_OF["sguT", l], [ys[:, b, i * P:(i + 1) * P] for i in range(2) for b in range(TB)])
                pe.wait_ge(ya_ready, l + 1)
                for b in range(TB):
                    transposes(UNIT_OF["attnT", l] + b, [ya[:, b, i * P:(i + 1) * P] for i in range(4)])

            ohi = room(TOP + 4096, GROUP, P)
            ohj = room(TOP + 6144, GROUP, QT_TILES)

            def gates(u, count, it, per):
                open_bank(u, it, per)
                pe.wait_ge(hot_ready, count)
                for t in range(GROUP):
                    ins = mm(bank(u)[:, t * QT_TILES:(t + 1) * QT_TILES], ohi[:, t, :], ohj[:, t, :],
                             start=True, stop=True)
                ins.then_inc(unit_full[u % BANKS], 1)

            def down(l, q):
                n, u = SLOT_OF["down", l, q], UNIT_OF["down", l, q]
                per = 2 if q == 1 else 1
                with pe.Fori(0, QT_SLOTS // RING) as it:
                    for s in range(RING):
                        feature_slot(n + s, u + s * per, hT, it, RING * per)
                        if q == 1:
                            gates(u + s * per + 1, it * RING + (QT_SLOTS * QUARTERS * l + s + 1), it, RING * per)

            def up(l, q):
                n, u = SLOT_OF["up", l, q], UNIT_OF["up", l, q]
                act_q = arena[:, (q % 2) * 8192:(q % 2 + 1) * 8192]
                gu, gper = ((UNIT_OF["down", l, 1] + 1, 2) if q == 0 else (UNIT_OF["up", l, q - 1], 1))
                last = gu + (QT_SLOTS - 1) * gper
                for c in range(BANKS):
                    if last - c * gper >= gu:
                        wait_taken(pe, last - c * gper)
                with pe.Fori(0, QT_SLOTS // RING) as it:
                    for s in range(RING):
                        mms = [(acc[d // 2][:, (d % 2) * T:(d % 2 + 1) * T], tile(n + s, j * KT + d),
                                act_q[:, bass.ds(it * (RING * 512) + (s * 2 + j) * T, T)], False, False)
                               for j in range(2) for d in range(KT)]
                        slot_mms(n + s, mms, it)
                        if q < 3:
                            gates(u + s, it * RING + (QT_SLOTS * (QUARTERS * l + q + 1) + s + 1), it, RING)

            def peer(l):
                pe.wait_ge(h_ready, 2 * l + 2)
                for s in range(8):
                    feature_slot(SLOT_OF["pq", l] + s, UNIT_OF["pq", l] + s, hT)
                n, u = SLOT_OF["keys", l], UNIT_OF["keys", l]
                qT = room(ACT1, 16, T)
                for b in range(BANKS):
                    wait_taken(pe, UNIT_OF["pq", l] + 7 - b)
                pe.wait_ge(slot_landed[n % RING], 16 * (n // RING + 1))
                for b in range(TB):
                    for c in range(4):
                        open_bank(u)
                        for i in range(4):
                            g = 4 * c + i
                            ins = mm(bank(u)[:, i * P:(i + 1) * P], qT[:, g, b * P:(b + 1) * P], tile(n, g),
                                     start=True, stop=True)
                            if b + c + i == 0:
                                ins.then_inc(slot_read[(n - 1) % RING], 1)
                        ins.then_inc(unit_full[u % BANKS], 1)
                        u += 1
                clear_acc()
                down(l, 0)
                pe.wait_ge(pick_ready, l + 1)
                u = UNIT_OF["idxT", l]
                transposes(u, [pick[:, a, b, :] for a in range(2) for b in range(TB)])
                transposes(u + 1, [pick[:, 2, b, :] for b in range(TB)])
                down(l, 1)
                up(l, 0)
                down(l, 2)
                up(l, 1)
                down(l, 3)
                up(l, 2)
                up(l, 3)
                end_acc()

            def end_acc():
                for b in range(4):
                    ins = mm(acc[b][:, :], zeros[:, 0:P], zeros[:, :], start=False, stop=True,
                             skip_group_check=True)
                ins.then_inc(acc_full, 1)

            def gla(l):
                pe.wait_ge(h_ready, 2 * l + 1)
                for s in range(2):
                    feature_slot(SLOT_OF["gq", l] + s, UNIT_OF["gq", l] + s, hT)
                pe.wait_ge(const_landed, 16 * (DEPTH + 1))
                wa = room(L2["wa"], KT, GRANK)
                u = UNIT_OF["alr", l]
                open_bank(u)
                for k in range(KT):
                    ins = mm(bank(u)[0:GRANK, 0:T], wa[:, k, :], hT[:, k, :], start=k == 0, stop=k == KT - 1)
                ins.then_inc(unit_full[u % BANKS], 1)
                wait_taken(pe, u)
                alr = arena[0:GRANK, L2["alr"]:L2["alr"] + T]
                u = UNIT_OF["z", l]
                for b in range(TB):
                    open_bank(u + b)
                    mm(bank(u + b)[:, :], alr[:, b * P:(b + 1) * P],
                       arena[0:GRANK, L2["wgu"]:L2["wgu"] + 512], start=True, stop=True).then_inc(
                           unit_full[(u + b) % BANKS], 1)
                token_slots(SLOT_OF["gk", l], UNIT_OF["gk", l], hT)
                for c in range(2):
                    token_slots(SLOT_OF["gv", l] + 2 * c, UNIT_OF["gv", l] + 2 * c, hT)
                for c in range(2):
                    token_slots(SLOT_OF["gg", l] + 2 * c, UNIT_OF["gg", l] + 2 * c, hT)
                la = room(L2["zz"], TB, 512)
                pe.wait_ge(la_ready, 1)
                u = UNIT_OF["decay", l]
                for b in range(TB):
                    open_bank(u + b)
                    mm(bank(u + b)[:, :], later[:, :], la[:, b, :], start=True, stop=True).then_inc(
                        unit_full[(u + b) % BANKS], 1)
                u = UNIT_OF["gamma", l]
                open_bank(u)
                for h in range(GH):
                    for b in range(TB):
                        ins = mm(bank(u)[:, h * 4 + 2 * b:h * 4 + 2 * b + 2], la[:, b, h * GDK:(h + 1) * GDK],
                                 chunk_of[:, :], start=True, stop=True)
                ins.then_inc(unit_full[u % BANKS], 1)
                kd, v = room(L2["kd"], TB, 512), room(L2["v"], TB, 1024)
                S, qT = room(L2["S"], 2, GH, GDV), room(L2["qT"], GH, T)
                pe.wait_ge(kd_ready, 1)
                u = UNIT_OF["kvs", l]

                def kvs(c):
                    b, r = c // 2, CHUNK * (c % 2)
                    for a in range(2):
                        open_bank(u + 2 * c + a)
                        for h in range(2 * a, 2 * a + 2):
                            ins = mm(bank(u + 2 * c + a)[:, (h % 2) * GDV:(h % 2 + 1) * GDV],
                                     kd[r:r + CHUNK, b, h * GDK:(h + 1) * GDK],
                                     v[r:r + CHUNK, b, h * GDV:(h + 1) * GDV], start=True, stop=True)
                        ins.then_inc(unit_full[(u + 2 * c + a) % BANKS], 1)

                def outs(c):
                    b, r = c // 2, CHUNK * (c % 2)
                    wait_taken(pe, u + 2 * c)
                    wait_taken(pe, u + 2 * c + 1)
                    for h in range(GH):
                        ins = mm(acc[2 * b + h // 2][r:r + CHUNK, (h % 2) * GDV:(h % 2 + 1) * GDV],
                                 qT[:, h, c * CHUNK:(c + 1) * CHUNK], S[:, c % 2, h, :],
                                 start=True, stop=True, skip_group_check=True)
                    ins.then_inc(o_full, 1)

                kvs(0)
                for c in range(T // CHUNK):
                    if c + 1 < T // CHUNK:
                        kvs(c + 1)
                    outs(c)
                o = room(L2["o"], TB, 1024)
                pe.wait_ge(o_ready, 1)
                u = UNIT_OF["oT", l]
                for b in range(TB):
                    for c in range(2):
                        transposes(u, [o[:, b, (4 * c + i) * P:(4 * c + i + 1) * P] for i in range(4)])
                        u += 1

            def lru(l):
                pe.wait_ge(h_ready, 2 * l + 1)
                for name in ("lru_g", "lru_x"):
                    for s in range(4):
                        feature_slot(SLOT_OF[name, l] + s, UNIT_OF[name, l] + s, hT)
                xc = room(L3["xc"], KT, T)
                pe.wait_ge(xc_ready, 1)
                for name in ("lru_r", "lru_i"):
                    n, u = SLOT_OF[name, l], UNIT_OF[name, l]
                    mms, ends = [], {}
                    pe.wait_ge(slot_landed[n % RING], 16 * (n // RING + 1))
                    for blk in range(4):
                        open_bank(u + blk)
                        for j in range(2):
                            for k in range(2):
                                ins = mm(bank(u + blk)[:, j * T:(j + 1) * T], tile(n, blk * 4 + j * 2 + k),
                                         xc[:, 2 * blk + k, :], start=k == 0, stop=k == 1)
                                if blk + j + k == 0:
                                    ins.then_inc(slot_read[(n - 1) % RING], 1)
                        ins.then_inc(unit_full[(u + blk) % BANKS], 1)

            def moe(l):
                pe.wait_ge(h_ready, 2 * l + 2)
                u = UNIT_OF["router", l]
                at, _ = COLS["rw"]
                open_bank(u)
                for b in range(TB):
                    for k in range(KT):
                        ins = mm(bank(u)[:, b * 16:(b + 1) * 16], hT[:, k, b * P:(b + 1) * P],
                                 cols[:, at + 16 * k:at + 16 * (k + 1)], start=k == 0, stop=k == KT - 1)
                ins.then_inc(unit_full[u % BANKS], 1)
                pe.wait_ge(comb_ready, l - DEPTH + 1)
                u = UNIT_OF["combT", l]
                open_bank(u)
                for b in range(TB):
                    ins = nc.tensor.transpose(bank(u)[0:16, b * P:(b + 1) * P], sel[:, 7, b * 16:(b + 1) * 16],
                                              ident[:, :])
                ins.then_inc(unit_full[u % BANKS], 1)
                wait_taken(pe, u)
                cT = arena[0:16, MOE["cT"]:MOE["cT"] + T]
                u = UNIT_OF["comb", l]
                for e in range(EXPERTS):
                    if e % 2 == 0:
                        open_bank(u)
                    ins = mm(bank(u)[:, (e % 2) * T:(e % 2 + 1) * T], ident[0:16, e:e + 1].broadcast_to([16, P]), cT,
                             start=True, stop=True)
                    if e % 2:
                        ins.then_inc(unit_full[u % BANKS], 1)
                        u += 1
                clear_acc()
                n, u = SLOT_OF["experts", l], UNIT_OF["experts", l]
                he = room(MOE["he"], 4, T)
                with pe.Fori(0, EXPERTS // 2) as it:
                    for e in range(2):
                        m, ue = n + EXP_SLOTS * e, u + 4 * e
                        its = 3
                        for s in range(4):
                            open_bank(ue + s, it, 8)
                            mms = [(bank(ue + s)[:, j * T:(j + 1) * T], tile(m + s, j * KT + k), hT[:, k, :],
                                    k == 0, k == KT - 1) for j in range(2) for k in range(KT)]
                            pe.wait_ge(slot_landed[(m + s) % RING], it * (16 * its) + 16 * ((m + s) // RING + 1))
                            for i, (o, a, b, start, stop) in enumerate(mms):
                                ins = mm(o, a, b, start=start, stop=stop)
                                if i == 0:
                                    ins.then_inc(slot_read[(m + s - 1) % RING], 1)
                            ins.then_inc(unit_full[(ue + s) % BANKS], 1)
                        for s in range(2):
                            pe.wait_ge(he_ready, it * 4 + (2 * EXPERTS * (l - DEPTH) + 2 * e + s + 1))
                            pe.wait_ge(slot_landed[(m + 4 + s) % RING],
                                       it * (16 * its) + 16 * ((m + 4 + s) // RING + 1))
                            for j in range(2):
                                for d in range(KT):
                                    ins = mm(acc[d // 2][:, (d % 2) * T:(d % 2 + 1) * T],
                                             tile(m + 4 + s, j * KT + d), he[:, 2 * s + j, :],
                                             start=False, stop=False, skip_group_check=True)
                                    if j + d == 0:
                                        ins.then_inc(slot_read[(m + 3 + s) % RING], 1)
                end_acc()

            pe.wait_ge(consts_made, 1)
            pe.wait_ge(cols_landed, 16)
            for l in range(LAYERS):
                mods(l)
                norm(2 * l)
                (first_mixer if l < DEPTH else gla if l == DEPTH else lru)(l)
                out_proj(l)
                norm(2 * l + 1)
                (peer if l < DEPTH else moe)(l)
            norm(2 * LAYERS)

        @block.scalar
        def _(act):
            steps = Steps(act, act_step)
            af = nc.scalar.activation

            def take(u, o, i, func=ACT.Copy, it=None, per=0, **kw):
                wait_full(act, u, it, per)
                af(o, i, func, **kw).then_inc(unit_taken[u % BANKS], 1)

            def norm(i):
                if i:
                    act.wait_ge(x_ready, i)
                else:
                    act.wait_ge(x_landed, 16)
                af(sq, xT[:, :, :], ACT.Square).then_inc(sq_ready, 1)
                wait_taken(act, UNIT_OF["norm", i])
                af(rstd[:, :], rstd[:, :], ACT.Sqrt).then_inc(std_ready, 1)

            def first_mixer(l):
                qk, v = room(L1["qk"], TB, 640), room(L1["v"], TB, P)
                for b in range(TB):
                    u = UNIT_OF["q", l] + b
                    take(u, qk[:, b, 0:512], bank(u)[:, :])
                u = UNIT_OF["kv", l]
                kv = bank(u)[:, :].rearrange("p (b c) -> p b c", b=TB)
                wait_full(act, u)
                steps(af(qk[:, :, 512:640], kv[:, :, 0:P], ACT.Copy))
                take(u, v, kv[:, :, P:2 * P])
                suv = room(L1["suv"], TB, 512)
                for b in range(TB):
                    u = UNIT_OF["sgu", l] + b
                    take(u, suv[:, b, :], bank(u)[:, :])
                for i, name in enumerate(("cb", "cc")):
                    u = UNIT_OF["conv", l] + i
                    take(u, room(L1[name], 512), bank(u)[:, :])
                act.wait_ge(qk_var, l + 1)
                af(st[:, 0, 0:20], st[:, 0, 0:20], ACT.Sqrt).then_inc(qk_std, 1)
                act.wait_ge(vn_var, l + 1)
                af(st[:, 2, 0:8], st[:, 2, 0:8], ACT.Sqrt).then_inc(vn_std, 1)
                act.wait_ge(yc_ready, l + 1)
                af(room(L1["sq2"], 512), room(L1["yc"], 512), ACT.Square).then_inc(yc_sq, 1)
                pp, pT = room(L1["pp"], HEADS, T), room(L1["pT"], 24, P)
                for b in range(TB):
                    nk = P * (b + 1)
                    lg = room((SQ, L1["lg"])[b], HEADS, T)
                    act.wait_ge(lg_ready, 2 * l + b + 1)
                    if b:
                        wait_full(act, UNIT_OF["PT", l] + 1)
                    for h in range(HEADS):
                        steps(af(pp[:, h, 0:nk], lg[:, h, 0:nk], ACT.Exp, bias=st[:, 3, 8 * b + h:8 * b + h + 1],
                                 accum_out=st[:, 4, 8 * b + h:8 * b + h + 1]))
                    af(st[:, 5, 8 * b:8 * b + 8], st[:, 5, 8 * b:8 * b + 8], ACT.Exp).then_inc(exp_done, 1)
                    for c in range(2 * (b + 1)):
                        u = UNIT_OF["PT", l] + 2 * b + c
                        k = 8 * b + 4 * c
                        take(u, pT[:, k:k + 4, :], bank(u)[:, :].rearrange("p (a b) -> p a b", b=P))
                wait_taken(act, UNIT_OF["conv_sum", l])
                af(room(L1["rc"], T), room(L1["rc"], T), ACT.Sqrt).then_inc(yc_std, 1)
                act.wait_ge(ys_var, l + 1)
                af(st[:, 1, 20:22], st[:, 1, 20:22], ACT.Sqrt).then_inc(ys_std, 1)
                act.wait_ge(ya_var, l + 1)
                af(st[:, 1, 24:26], st[:, 1, 24:26], ACT.Sqrt).then_inc(ya_std, 1)

            def gelus(l, q):
                u, per = UNIT_OF["down", l, q], 2 if q == 1 else 1
                act_q = arena[:, (q % 2) * 8192:(q % 2 + 1) * 8192]
                with act.Fori(0, QT_SLOTS // RING) as it:
                    for s in range(RING):
                        take(u + s * per, act_q[:, bass.ds(it * (RING * 512) + s * 512, 512)],
                             bank(u + s * per)[:, :], ACT.Gelu, it, RING * per)

            def peer(l):
                qT = room(ACT1, 16, T)
                for s in range(8):
                    u = UNIT_OF["pq", l] + s
                    take(u, qT[:, 2 * s:2 * s + 2, :], bank(u)[:, :].rearrange("p (a b) -> p a b", b=T))
                S = room(TOP, TB, 16 * P)
                for b in range(TB):
                    for c in range(4):
                        u = UNIT_OF["keys", l] + 4 * b + c
                        take(u, S[:, b, c * 512:(c + 1) * 512], bank(u)[:, :])
                gelus(l, 0)
                for b in range(TB):
                    act.wait_ge(best_ready, 2 * l + b + 1)
                    af(pick[:, 2, b, :], pick[:, 2, b, :], ACT.Exp).then_inc(gate_exp, 1)
                for q in range(1, QUARTERS):
                    gelus(l, q)

            def gla(l):
                qT = room(L2["qT"], GH, T)
                for s in range(2):
                    u = UNIT_OF["gq", l] + s
                    take(u, qT[:, 2 * s:2 * s + 2, :], bank(u)[:, :].rearrange("p (a b) -> p a b", b=T),
                         scale=float(GDK) ** -0.5)
                u = UNIT_OF["alr", l]
                take(u, arena[0:GRANK, L2["alr"]:L2["alr"] + T], bank(u)[0:GRANK, 0:T])
                e = room(L2["e"], 1024)
                act.wait_ge(z_ready, 1)
                steps(af(e, e, ACT.Exp, scale=-1.0))
                steps.sync()
                af(e, e, ACT.Ln, bias=1.0).then_inc(soft_done, 1)
                k, v, gs = room(L2["k"], TB, 512), room(L2["v"], TB, 1024), room(L2["gs"], TB, 1024)
                for b in range(TB):
                    u = UNIT_OF["gk", l] + b
                    take(u, k[:, b, :], bank(u)[:, :])
                for name, o, f in (("gv", v, ACT.Copy), ("gg", gs, ACT.Silu)):
                    for c in range(2):
                        for b in range(TB):
                            u = UNIT_OF[name, l] + 2 * c + b
                            take(u, o[:, b, c * 512:(c + 1) * 512], bank(u)[:, :], f)
                for b in range(TB):
                    u = UNIT_OF["decay", l] + b
                    take(u, room(L2["lg"], TB, 512)[:, b, :], bank(u)[:, :], ACT.Exp)
                u = UNIT_OF["gamma", l]
                take(u, room(L2["gam"], 16), bank(u)[:, 0:16], ACT.Exp)
                act.wait_ge(o_var, 1)
                af(st[:, 0, 0:8], st[:, 0, 0:8], ACT.Sqrt).then_inc(o_std, 1)

            def lru(l):
                gate = room(L3["gate"], KT, T)
                act.wait_ge(lam_abs, 1)
                af(st[:, 0, 0:8], st[:, 0, 8:16], ACT.Exp, scale=-1.0).then_inc(lam_exp, 1)
                for s in range(4):
                    u = UNIT_OF["lru_g", l] + s
                    take(u, gate[:, 2 * s:2 * s + 2, :], bank(u)[:, :].rearrange("p (a b) -> p a b", b=T),
                         ACT.Gelu_apprx_tanh)
                xp = room(L3["xp"], KT, T + CONV2 - 1)
                for s in range(4):
                    u = UNIT_OF["lru_x", l] + s
                    take(u, xp[:, 2 * s:2 * s + 2, CONV2 - 1:], bank(u)[:, :].rearrange("p (a b) -> p a b", b=T))
                for name, o, bias in (("lru_r", "r", "lbr"), ("lru_i", "i", "lbi")):
                    ov = room(L3[o], KT, T)
                    for blk in range(4):
                        u = UNIT_OF[name, l] + blk
                        wait_full(act, u)
                        steps(af(ov[:, 2 * blk, :], bank(u)[:, 0:T], ACT.Sigmoid, bias=col(bias, 2 * blk)))
                        take(u, ov[:, 2 * blk + 1, :], bank(u)[:, T:2 * T], ACT.Sigmoid, bias=col(bias, 2 * blk + 1))
                r, t, a = room(L3["r"], KT, T), room(L3["t"], KT, T), room(L3["a"], KT, T)
                act.wait_ge(lam_ready, 1)
                for b in range(4):
                    wait_taken(act, UNIT_OF["lru_r", l] + b)
                steps.sync()
                for k in range(KT):
                    steps(af(t[:, k, :], r[:, k, :], ACT.Tanh, scale=st[:, 1, k:k + 1]))
                for k in range(KT):
                    ins = af(a[:, k, :], r[:, k, :], ACT.Exp, scale=st[:, 1, k:k + 1])
                    if k < KT - 1:
                        steps(ins)
                ins.then_inc(tanh_done, 1)
                act.wait_ge(m_sq, 1)
                af(room(L3["m"], 2048), room(L3["m"], 2048), ACT.Sqrt).then_inc(m_root, 1)

            def moe(l):
                u = UNIT_OF["router", l]
                take(u, sel[:, 0, :], bank(u)[:, 0:32], ACT.Sigmoid)
                u = UNIT_OF["combT", l]
                take(u, arena[0:16, MOE["cT"]:MOE["cT"] + T], bank(u)[0:16, 0:T])
                cb = room(MOE["cb"], EXPERTS, T)
                for c in range(8):
                    u = UNIT_OF["comb", l] + c
                    take(u, cb[:, 2 * c:2 * c + 2, :], bank(u)[:, :].rearrange("p (a b) -> p a b", b=T))
                si = room(MOE["si"], 2, 512)
                u = UNIT_OF["experts", l]
                with act.Fori(0, EXPERTS // 2) as it:
                    for e in range(2):
                        for s in range(2):
                            ug = u + 4 * e + 2 * s
                            wait_taken(act, ug - 3, it, 8)
                            take(ug, si[:, s, :], bank(ug)[:, :], ACT.Silu, it, 8)

            act.wait_ge(cols_landed, 16)
            af(cact[:, :, :], cols[:, 0:16].rearrange("p (a b) -> p a b", b=KT), ACT.Silu).then_inc(c_ready, 1)
            for l in range(LAYERS):
                norm(2 * l)
                (first_mixer if l < DEPTH else gla if l == DEPTH else lru)(l)
                norm(2 * l + 1)
                (peer if l < DEPTH else moe)(l)
            norm(2 * LAYERS)

        @block.vector
        def _(dve):
            v = nc.vector
            steps = Steps(dve, dve_step)
            ts, tt, stt = v.tensor_scalar, v.tensor_tensor, v.scalar_tensor_tensor

            def spread(a, axis, shape):
                return a.unsqueeze(axis).broadcast_to(shape)

            def took(ins, u):
                ins.then_inc(unit_taken[u % BANKS], 1)

            def ada_turn(l, it, pieces):
                c = cact[:, l // DEPTH, :]
                for first in range(0, pieces, ADA_RING):
                    for k in range(KT):
                        for i in range(ADA_RING):
                            if k == 0:
                                dve.wait_ge(ada_landed[i], it * (16 * pieces // ADA_RING)
                                            + 16 * (16 * l + first // ADA_RING + 1))
                            o = ada_sum[:, bass.ds(it * (pieces * P) + (first + i) * P, P)]
                            a = ada_ring[:, i, k * P:(k + 1) * P]
                            if k == 0:
                                ins = ts(o, a, c[:, 0:1], None, ALU.mult)
                            else:
                                steps.sync(2 if k < KT - 1 else 2 - i)
                                ins = stt(o, a, c[:, k:k + 1], o, ALU.mult, ALU.add)
                            if k < KT - 1:
                                steps(ins)
                            else:
                                ins.then_inc(ada_read[i], 1)

            def ada_loop(l):
                with dve.Fori(0, 48 // ADA_RING) as it:
                    steps.enter(it, ADA_RING * (KT - 1))
                    ada_turn(l, it, ADA_RING)
                steps.leave(48 // ADA_RING)

            def mods(l):
                u = UNIT_OF["mod", l]
                wait_full(dve, u)
                if l:
                    dve.wait_ge(x_ready, 2 * l)
                took(tt(mod[:, :], bank(u)[:, 0:48], col(("b_ada", l)), ALU.add), u)
                wait_taken(dve, u)
                steps(stt(gain[:, 0, :], mod[:, 8:16], 1.0, col(("g1", l)), ALU.add, ALU.mult))
                steps(stt(gain[:, 1, :], mod[:, 32:40], 1.0, col(("g2", l)), ALU.add, ALU.mult))
                steps.sync()

            def norm(i):
                u = UNIT_OF["norm", i]
                wait_full(dve, u)
                took(ts(rstd[:, :], bank(u)[:, 0:T], EPS, None, ALU.add), u)
                dve.wait_ge(std_ready, i + 1)
                steps(v.reciprocal(rstd[:, :], rstd[:, :]))
                steps.sync()
                steps(tt(hT[:, :, :], xT[:, :, :], spread(rstd[:, :], 1, [P, KT, T]), ALU.mult))
                steps.sync()
                for k in range(KT):
                    if i < 2 * LAYERS:
                        sh = (i % 2) * 24 + k
                        ins = ts(hT[:, k, :], hT[:, k, :], gain[:, i % 2, k:k + 1], mod[:, sh:sh + 1],
                                 ALU.mult, ALU.add)
                    else:
                        ins = ts(hT[:, k, :], hT[:, k, :], col("final_g", k), None, ALU.mult)
                    if k < KT - 1:
                        steps(ins)
                ins.then_inc(h_ready, 1)

            def residual(l):
                for s in range(4):
                    u = UNIT_OF["out", l] + s
                    wait_full(dve, u)
                    for j in range(2):
                        d = 2 * s + j
                        ins = stt(xT[:, d, :], bank(u)[:, j * T:(j + 1) * T], mod[:, 16 + d:17 + d],
                                  xT[:, d, :], ALU.mult, ALU.add)
                        if j:
                            took(ins, u)
                        else:
                            steps(ins)
                for s in range(4):
                    wait_taken(dve, UNIT_OF["out", l] + s)
                v.memset(psr[:, 15:16], 0.0).then_inc(x_ready, 1)

            def acc_residual(l):
                dve.wait_ge(acc_full, l + 1)
                for d in range(KT):
                    ins = stt(xT[:, d, :], acc[d // 2][:, (d % 2) * T:(d % 2 + 1) * T],
                              mod[:, 40 + d:41 + d], xT[:, d, :], ALU.mult, ALU.add)
                    if d < KT - 1:
                        steps(ins)
                ins.then_inc(x_ready, 1)

            def var(o, i, scale):
                return ts(o, i, scale, EPS, ALU.mult, ALU.add)

            def first_mixer(l):
                qk, suv = room(L1["qk"], TB, 640), room(L1["suv"], TB, 512)
                s3 = room(L1["sq3"], 1024)
                og = col(("og", l))
                wait_taken(dve, UNIT_OF["q", l])
                wait_taken(dve, UNIT_OF["q", l] + 1)
                wait_taken(dve, UNIT_OF["kv", l])
                qsq = room(SQ, TB * 640)
                qf = room(L1["qk"], TB * 640)
                steps(tt(qsq, qf, qf, ALU.mult))
                steps.sync()
                rs = st[:, 0, 0:20]
                steps(v.tensor_reduce(rs, room(SQ, 20, HD), AX, ALU.add))
                steps.sync()
                var(rs, rs, 1.0 / HD).then_inc(qk_var, 1)
                for b in range(TB):
                    wait_taken(dve, UNIT_OF["sgu", l] + b)
                vn = room(L1["vn"], TB, 256)
                vn3 = room(L1["vn"], TB * 4, 64)
                mu = st[:, 2, 8:16]
                for b in range(TB):
                    steps(v.tensor_reduce(st[:, 2, 8 + 4 * b:12 + 4 * b],
                                          suv[:, b, 256:512].rearrange("p (g c) -> p g c", c=64), AX, ALU.add))
                steps.sync()
                steps(ts(mu, mu, 1.0 / 64, None, ALU.mult))
                steps.sync()
                for b in range(TB):
                    steps(tt(vn[:, b, :].rearrange("p (g c) -> p g c", c=64),
                             suv[:, b, 256:512].rearrange("p (g c) -> p g c", c=64),
                             spread(st[:, 2, 8 + 4 * b:12 + 4 * b], 2, [P, 4, 64]), ALU.subtract))
                steps.sync()
                vf = room(L1["vn"], 512)
                steps(tt(s3[:, 0:512], vf, vf, ALU.mult))
                steps.sync()
                steps(v.tensor_reduce(st[:, 2, 0:8], room(L1["sq3"], 8, 64), AX, ALU.add))
                steps.sync()
                var(st[:, 2, 0:8], st[:, 2, 0:8], 1.0 / 64).then_inc(vn_var, 1)
                dve.wait_ge(qk_std, l + 1)
                steps(v.reciprocal(rs, rs))
                steps.sync()
                q3 = room(L1["qk"], 20, HD)
                tt(q3, q3, spread(rs, 2, [P, 20, HD]), ALU.mult).then_inc(qk_ready, 1)
                dve.wait_ge(vn_std, l + 1)
                steps(v.reciprocal(st[:, 2, 0:8], st[:, 2, 0:8]))
                steps.sync()
                tt(vn3, vn3, spread(st[:, 2, 0:8], 2, [P, 8, 64]), ALU.mult).then_inc(vn_ready, 1)
                z, cc = room(L1["z"], 2, T + 2), room(L1["cc"], 2, T)
                yc, cb = room(L1["yc"], 2, T), room(L1["cb"], 2, T)
                steps(v.memset(z[:, :, 0:2], 0.0))
                u = UNIT_OF["conv", l]
                wait_taken(dve, u)
                wait_taken(dve, u + 1)
                wait_full(dve, u + 2)
                took(tt(z[:, :, 2:], cc, bank(u + 2)[:, :].rearrange("p (a b) -> p a b", b=T), ALU.mult), u + 2)
                wait_taken(dve, u + 2)
                steps.sync()
                for j in range(3):
                    for k in range(2):
                        w_j = col(("cw", l), 2 * j + k)
                        if j == 0:
                            steps(ts(yc[:, k, :], z[:, k, 0:T], w_j, None, ALU.mult))
                        else:
                            steps.sync(1)
                            steps(stt(yc[:, k, :], z[:, k, j:j + T], w_j, yc[:, k, :], ALU.mult, ALU.add))
                steps.sync()
                tt(yc, yc, cb, ALU.mult).then_inc(yc_ready, 1)
                u = UNIT_OF["qkT", l]
                wait_full(dve, u)
                took(ts(room(L1["kT"], T), bank(u)[:, 0:T], col(("gk", l)), None, ALU.mult), u)
                for b in range(TB):
                    wait_full(dve, u + 1 + b)
                    took(ts(room(L1["qT"], TB, 512)[:, b, :], bank(u + 1 + b)[:, :], col(("gq", l)),
                            float(HD) ** -0.5, ALU.mult, ALU.mult), u + 1 + b)
                dve.wait_ge(bias_masked, l + 1)
                bias = room(L1["bias"], HEADS, T)
                sink = col(("sink", l))
                u = UNIT_OF["scores", l]
                for b in range(TB):
                    nk = P * (b + 1)
                    per = 512 // nk
                    lg = room((SQ, L1["lg"])[b], HEADS, T)
                    for c in range(HEADS // per):
                        wait_full(dve, u)
                        took(tt(lg[:, c * per:(c + 1) * per, 0:nk],
                                bank(u)[:, :].rearrange("p (h s) -> p h s", s=nk),
                                bias[:, c * per:(c + 1) * per, T - nk:T], ALU.add), u)
                        u += 1
                    for c in range(min(BANKS, HEADS // per)):
                        wait_taken(dve, u - 1 - c)
                    top = st[:, 2, 16 + 8 * b:24 + 8 * b]
                    steps(v.tensor_reduce(top, lg[:, :, 0:nk], AX, ALU.max))
                    steps.sync()
                    steps(tt(top, top, sink, ALU.max))
                    steps.sync()
                    steps(tt(st[:, 5, 8 * b:8 * b + 8], sink, top, ALU.subtract))
                    ts(st[:, 3, 8 * b:8 * b + 8], top, -1.0, None, ALU.mult).then_inc(lg_ready, 1)
                u = UNIT_OF["conv_sum", l]
                wait_full(dve, u)
                took(ts(room(L1["rc"], T), bank(u)[:, 0:T], float(D) / 256, EPS, ALU.mult, ALU.add), u)
                u = UNIT_OF["mix", l]
                wait_full(dve, u)
                ys = room(L1["ys"], TB, 256)
                for b in range(TB):
                    ins = tt(ys[:, b, :].rearrange("p (g c) -> p g c", c=64),
                             bank(u)[:, b * 256:(b + 1) * 256].rearrange("p (g c) -> p g c", c=64),
                             spread(col(("sb", l)), 2, [P, 4, 64]), ALU.add)
                    if b:
                        took(ins, u)
                    else:
                        steps(ins)
                wait_taken(dve, u)
                steps(tt(ys, ys, suv[:, :, 0:256], ALU.mult))
                steps.sync()
                for b in range(TB):
                    steps(v.tensor_tensor_reduce(out=s3[:, b * 256:(b + 1) * 256], in0=ys[:, b, :],
                                                 in1=ys[:, b, :], scale=1.0, scalar=0.0, op0=ALU.mult,
                                                 op1=ALU.add, accum_out=st[:, 1, 20 + b:21 + b]))
                steps.sync()
                var(st[:, 1, 20:22], st[:, 1, 20:22], 1.0 / 256).then_inc(ys_var, 1)
                ya = room(L1["ya"], TB, 512)
                for b in range(TB):
                    dve.wait_ge(exp_done, 2 * l + b + 1)
                    den = st[:, 4, 8 * b:8 * b + 8]
                    steps(tt(den, den, st[:, 5, 8 * b:8 * b + 8], ALU.add))
                    steps.sync()
                    steps(v.reciprocal(den, den))
                    steps.sync()
                    u = UNIT_OF["PV", l] + b
                    wait_full(dve, u)
                    took(tt(ya[:, b, :].rearrange("p (h c) -> p h c", c=64),
                            bank(u)[:, :].rearrange("p (h c) -> p h c", c=64),
                            spread(den, 2, [P, HEADS, 64]), ALU.mult), u)
                    wait_taken(dve, u)
                    steps(v.tensor_tensor_reduce(out=s3[:, 0:512], in0=ya[:, b, :],
                                                 in1=ya[:, b, :], scale=1.0, scalar=0.0, op0=ALU.mult,
                                                 op1=ALU.add, accum_out=st[:, 1, 24 + b:25 + b]))
                    steps.sync()
                var(st[:, 1, 24:26], st[:, 1, 24:26], 1.0 / 512).then_inc(ya_var, 1)
                dve.wait_ge(ys_std, l + 1)
                steps(v.reciprocal(st[:, 1, 20:22], st[:, 1, 20:22]))
                steps.sync()
                tt(ys, ys, spread(st[:, 1, 20:22], 2, [P, TB, 256]), ALU.mult).then_inc(ys_ready, 1)
                dve.wait_ge(ya_std, l + 1)
                steps(v.reciprocal(st[:, 1, 24:26], st[:, 1, 24:26]))
                steps.sync()
                tt(ya, ya, spread(st[:, 1, 24:26], 2, [P, TB, 512]), ALU.mult).then_inc(ya_ready, 1)
                rc = room(L1["rc"], T)
                dve.wait_ge(yc_std, l + 1)
                steps(v.reciprocal(rc, rc))
                steps.sync()
                for k in range(2):
                    steps(stt(mT[:, 4 + k, :], yc[:, k, :], og[:, 4 + k:5 + k], rc, ALU.mult, ALU.mult))
                u = UNIT_OF["sguT", l]
                wait_full(dve, u)
                took(tt(mT[:, 6:8, :], bank(u)[:, :].rearrange("p (a b) -> p a b", b=T),
                        spread(og[:, 6:8], 2, [P, 2, T]), ALU.mult), u)
                for b in range(TB):
                    u = UNIT_OF["attnT", l] + b
                    wait_full(dve, u)
                    took(tt(mT[:, 0:4, b * P:(b + 1) * P], bank(u)[:, :].rearrange("p (a b) -> p a b", b=P),
                            spread(og[:, 0:4], 2, [P, 4, P]), ALU.mult), u)
                v.memset(psr[:, 14:15], 0.0).then_inc(m_ready, 1)

            def best(b, l):
                S = room(TOP, TB, 16, P)
                work = room(TOP + 8192, 16, P)
                for c in range(4):
                    wait_taken(dve, UNIT_OF["keys", l] + 4 * b + c)
                for g in range(16):
                    steps(v.max(tv[:, g, 0:8], S[:, b, g, :]))
                steps.sync()
                for g in range(16):
                    steps(v.max_index(ti[:, g, 0:8], tv[:, g, 0:8], S[:, b, g, :]))
                    steps(v.match_replace(work[:, g, :], tv[:, g, 0:8], S[:, b, g, :], -3e38))
                steps.sync()
                for g in range(16):
                    steps(v.max(tv[:, g, 8:16], work[:, g, :]))
                steps.sync()
                for g in range(16):
                    steps(v.max_index(ti[:, g, 8:16], tv[:, g, 8:16], work[:, g, :]))
                steps.sync()
                steps(v.tensor_copy(tf[:, :, :], ti[:, :, :]))
                cand = room(TOP + 6144, PH, TOPK * TOPK)
                c4 = cand.rearrange("p h (a b) -> p h a b", b=TOPK)
                half = tv[:, :, :].rearrange("p (h s) a -> p h s a", s=2)
                steps(tt(c4, half[:, :, 0, :].unsqueeze(3).broadcast_to([P, PH, TOPK, TOPK]),
                         half[:, :, 1, :].unsqueeze(2).broadcast_to([P, PH, TOPK, TOPK]), ALU.add))
                steps.sync()
                bp3 = bp[:, 0, :].rearrange("p (h k) -> p h k", k=TOPK)
                for h in range(PH):
                    steps(v.max(bv[:, h, 0:8], cand[:, h, :]))
                steps.sync()
                for h in range(PH):
                    steps(v.max_index(bp3[:, h, 0:8], bv[:, h, 0:8], cand[:, h, :]))
                steps.sync()
                for h in range(PH):
                    steps(v.match_replace(cand[:, h, :], bv[:, h, 0:8], cand[:, h, :], -3e38))
                steps.sync()
                for h in range(PH):
                    steps(v.max(bv[:, h, 8:16], cand[:, h, :]))
                steps.sync()
                for h in range(PH):
                    steps(v.max_index(bp3[:, h, 8:16], bv[:, h, 8:16], cand[:, h, :]))
                g3 = pick[:, 2, b, :].rearrange("p (h k) -> p h k", k=TOPK)
                tt(g3, bv[:, :, :], bv[:, :, 0:1].broadcast_to([P, PH, TOPK]), ALU.subtract).then_inc(best_ready, 1)
                steps.sync()
                steps(ts(bp[:, 1, :], bp[:, 0, :], 4, None, ALU.logical_shift_right))
                steps(ts(bp[:, 2, :], bp[:, 0, :], TOPK - 1, None, ALU.bitwise_and))
                steps.sync()
                steps(v.tensor_copy(bf[:, :, :], bp[:, 1:3, :]))
                steps.sync()
                tfh = tf[:, :, :].rearrange("p (h s) a -> p h s a", s=2)
                eq = room(TOP + 8192, PH, TOPK, TOPK)
                for s in range(2):
                    steps(tt(eq, iota[:, 0:TOPK].unsqueeze(1).broadcast_to([P, PH * TOPK, TOPK]).rearrange(
                        "p (h k) a -> p h k a", h=PH),
                        bf[:, s, :].rearrange("p (h k) -> p h k", h=PH).unsqueeze(3).broadcast_to(
                            [P, PH, TOPK, TOPK]), ALU.is_equal))
                    steps.sync()
                    steps(tt(eq, eq, tfh[:, :, s, :].unsqueeze(2).broadcast_to([P, PH, TOPK, TOPK]), ALU.mult))
                    steps.sync()
                    steps(v.tensor_reduce(pick[:, s, b, :], eq.rearrange("p h k a -> p (h k) a"), AX, ALU.add))
                    steps.sync()
                dve.wait_ge(gate_exp, 2 * l + b + 1)
                steps(v.tensor_reduce(psr[:, 0:8], g3, AX, ALU.add))
                steps.sync()
                steps(v.reciprocal(psr[:, 0:8], psr[:, 0:8]))
                steps.sync()
                steps(tt(g3, g3, spread(psr[:, 0:8], 2, [P, PH, TOPK]), ALU.mult))
                steps.sync()

            ohi = room(TOP + 4096, GROUP, P)
            ohj = room(TOP + 6144, GROUP, QT_TILES)

            def gates(l, q):
                act_q = arena[:, (q % 2) * 8192:(q % 2 + 1) * 8192].rearrange("p (j t) -> p t j", t=T)
                u, per = (UNIT_OF["down", l, 1] + 1, 2) if q == 0 else (UNIT_OF["up", l, q - 1], 1)
                uq, pq = UNIT_OF["down", l, q], 2 if q == 1 else 1
                for c in range(BANKS):
                    wait_taken(dve, uq + (QT_SLOTS - 1 - c) * pq)
                with dve.Fori(0, QT_SLOTS // RING) as it:
                    for s in range(RING):
                        for t in range(GROUP):
                            at = it * (RING * GROUP) + (s * GROUP + t)
                            ts(ohi[:, t, :], iota[:, :], pickT[:, 0, bass.ds(at, 1)], None, ALU.is_equal)
                            ins = ts(ohj[:, t, :], iota[:, q * QT_TILES:(q + 1) * QT_TILES],
                                     pickT[:, 1, bass.ds(at, 1)], pickT[:, 2, bass.ds(at, 1)],
                                     ALU.is_equal, ALU.mult)
                        ins.then_inc(hot_ready, 1)
                        ug = u + s * per
                        wait_full(dve, ug, it, RING * per)
                        a = act_q[:, bass.ds(it * (RING * GROUP) + s * GROUP, GROUP), :]
                        took(tt(a, a, bank(ug)[:, :].rearrange("p (t j) -> p t j", j=QT_TILES), ALU.mult), ug)

            def peer(l):
                for b in range(TB):
                    best(b, l)
                v.memset(psr[:, 13:14], 0.0).then_inc(pick_ready, 1)
                u = UNIT_OF["idxT", l]
                wait_full(dve, u)
                took(v.tensor_copy(pickT[:, 0:2, :], bank(u)[:, :].rearrange("p (a b) -> p a b", b=T)), u)
                wait_full(dve, u + 1)
                took(v.tensor_copy(pickT[:, 2, :], bank(u + 1)[:, 0:T]), u + 1)
                wait_taken(dve, u)
                wait_taken(dve, u + 1)
                gates(l, 0)
                gates(l, 1)
                ada_loop(l + 1)
                gates(l, 2)
                gates(l, 3)
                acc_residual(l)

            def gla(l):
                zz, e = room(L2["zz"], TB, 512), room(L2["e"], TB, 512)
                dve.wait_ge(const_landed, 16 * (DEPTH + 1))
                u = UNIT_OF["z", l]
                for b in range(TB):
                    wait_full(dve, u + b)
                    took(tt(zz[:, b, :], bank(u + b)[:, :], room(L2["bg"], 512), ALU.add), u + b)
                for b in range(TB):
                    wait_taken(dve, u + b)
                stt(e, zz, -1.0, zz, ALU.mult, ALU.max).then_inc(z_ready, 1)
                steps(ts(zz, zz, 0.0, None, ALU.min))
                dve.wait_ge(soft_done, 1)
                steps.sync()
                tt(zz, zz, e, ALU.subtract).then_inc(la_ready, 1)
                gs = room(L2["gs"], TB * GH, GDV)
                for i in range(4):
                    wait_taken(dve, UNIT_OF["gg", l] + i)
                steps(tt(gs, gs, spread(room(L2["ng"], GDV), 1, [P, TB * GH, GDV]), ALU.mult))
                kd = room(L2["kd"], 1024)
                for b in range(TB):
                    wait_taken(dve, UNIT_OF["decay", l] + b)
                    wait_taken(dve, UNIT_OF["gk", l] + b)
                tt(kd, room(L2["k"], 1024), room(L2["lg"], 1024), ALU.mult).then_inc(kd_ready, 1)
                S, gam = room(L2["S"], 2, GH, GDV), room(L2["gam"], 16)
                wait_taken(dve, UNIT_OF["gamma", l])
                u = UNIT_OF["kvs", l]
                for c in range(T // CHUNK):
                    if c >= 2:
                        dve.wait_ge(o_full, c - 1)
                    for a in range(2):
                        ua = u + 2 * c + a
                        wait_full(dve, ua)
                        if c == 0:
                            took(v.tensor_copy(S[:, 0, 2 * a:2 * a + 2, :],
                                               bank(ua)[:, :].rearrange("p (a b) -> p a b", b=GDV)), ua)
                        else:
                            for h in range(2 * a, 2 * a + 2):
                                ins = stt(S[:, c % 2, h, :], S[:, (c - 1) % 2, h, :],
                                          gam[:, 4 * h + c:4 * h + c + 1],
                                          bank(ua)[:, (h % 2) * GDV:(h % 2 + 1) * GDV], ALU.mult, ALU.add)
                                if h % 2:
                                    took(ins, ua)
                                else:
                                    steps(ins)
                    wait_taken(dve, u + 2 * c)
                    wait_taken(dve, u + 2 * c + 1)
                o, osq = room(L2["o"], TB, 1024), room(L2["osq"], 2048)
                of = room(L2["o"], 2048)
                for b in range(TB):
                    dve.wait_ge(o_full, 2 * b + 2)
                    for a in range(2):
                        steps(v.tensor_copy(o[:, b, a * 512:(a + 1) * 512], acc[2 * b + a][:, :]))
                steps.sync()
                steps(tt(osq, of, of, ALU.mult))
                steps.sync()
                rs = st[:, 0, 0:8]
                steps(v.tensor_reduce(rs, room(L2["osq"], 8, GDV), AX, ALU.add))
                steps.sync()
                var(rs, rs, 1.0 / GDV).then_inc(o_var, 1)
                steps(tt(of, of, room(L2["gs"], 2048), ALU.mult))
                dve.wait_ge(o_std, 1)
                steps(v.reciprocal(rs, rs))
                steps.sync()
                o3 = room(L2["o"], 8, GDV)
                tt(o3, o3, spread(rs, 2, [P, 8, GDV]), ALU.mult).then_inc(o_ready, 1)
                u = UNIT_OF["oT", l]
                for b in range(TB):
                    for c in range(2):
                        wait_full(dve, u)
                        took(v.tensor_copy(mT[:, 4 * c:4 * c + 4, b * P:(b + 1) * P],
                                           bank(u)[:, :].rearrange("p (a b) -> p a b", b=P)), u)
                        u += 1
                v.memset(psr[:, 14:15], 0.0).then_inc(m_ready, 1)

            def lru(l):
                lam, s, s2, p = col("lam"), st[:, 2, 0:8], st[:, 2, 8:16], st[:, 2, 16:24]
                stt(st[:, 0, 8:16], lam, -1.0, lam, ALU.mult, ALU.max).then_inc(lam_abs, 1)
                xp = room(L3["xp"], KT, T + CONV2 - 1)
                steps(v.memset(xp[:, :, 0:CONV2 - 1], 0.0))
                dve.wait_ge(lam_exp, 1)
                steps(ts(s, st[:, 0, 0:8], 2.0, None, ALU.add))
                steps.sync()
                steps(v.reciprocal(s, s))
                steps.sync()
                steps(tt(s, s, st[:, 0, 0:8], ALU.mult))
                steps.sync()
                steps(tt(s2, s, s, ALU.mult))
                steps.sync()
                steps(ts(p, s2, 1.0 / 15, 1.0 / 13, ALU.mult, ALU.add))
                for n in (11, 9, 7, 5, 3, 1):
                    steps.sync()
                    steps(tt(p, p, s2, ALU.mult))
                    steps.sync()
                    steps(ts(p, p, 1.0 / n, None, ALU.add))
                steps.sync()
                steps(tt(p, p, s, ALU.mult))
                steps(ts(s2, lam, -1.0, 0.0, ALU.mult, ALU.max))
                steps.sync()
                steps(stt(p, p, 2.0, s2, ALU.mult, ALU.add))
                steps.sync()
                ts(st[:, 1, 0:8], p, -8.0, None, ALU.mult).then_inc(lam_ready, 1)
                xc = room(L3["xc"], KT, T)
                for i in range(4):
                    wait_taken(dve, UNIT_OF["lru_x", l] + i)
                for j in range(CONV2):
                    for k in range(KT):
                        w_j = col("lcw", 8 * j + k)
                        if j == 0:
                            steps(ts(xc[:, k, :], xp[:, k, 0:T], w_j, col("lcb", k), ALU.mult, ALU.add))
                        else:
                            steps.sync(KT - 1)
                            ins = stt(xc[:, k, :], xp[:, k, j:j + T], w_j, xc[:, k, :], ALU.mult, ALU.add)
                            if j == CONV2 - 1 and k == KT - 1:
                                ins.then_inc(xc_ready, 1)
                            else:
                                steps(ins)
                a, i_, t, m = (room(L3[n], 2048) for n in ("a", "i", "t", "m"))
                b_, hs = room(L3["b"], KT, T), room(L3["hs"], KT, T)
                dve.wait_ge(xc_ready, 1)
                for n in range(4):
                    wait_taken(dve, UNIT_OF["lru_i", l] + n)
                steps(tt(room(L3["b"], 2048), room(L3["xc"], 2048), i_, ALU.mult))
                dve.wait_ge(tanh_done, 1)
                steps(ts(m, t, -1.0, 1.0, ALU.mult, ALU.add))
                steps.sync()
                steps(v.reciprocal(m, m))
                steps.sync()
                steps(stt(m, t, -2.0, m, ALU.mult, ALU.mult))
                steps.sync()
                ts(m, m, 1e-34, None, ALU.max).then_inc(m_sq, 1)
                dve.wait_ge(m_root, 1)
                steps(tt(room(L3["b"], 2048), room(L3["b"], 2048), m, ALU.mult))
                steps.sync()
                a3 = room(L3["a"], KT, T)
                for k in range(KT):
                    steps(v.tensor_tensor_scan(hs[:, k, :], a3[:, k, :], b_[:, k, :], 0.0, ALU.mult, ALU.add))
                steps.sync()
                for n in range(4):
                    wait_taken(dve, UNIT_OF["lru_g", l] + n)
                tt(mT, hs, room(L3["gate"], KT, T), ALU.mult).then_inc(m_ready, 1)

            def route(l):
                u = UNIT_OF["router", l]
                wait_taken(dve, u)
                scores, biased = sel[:, 0, :], sel[:, 1, :]
                steps(tt(biased.rearrange("p (b e) -> p b e", b=TB), scores.rearrange("p (b e) -> p b e", b=TB),
                         spread(col("rb"), 1, [P, TB, EXPERTS]), ALU.add))
                steps.sync()
                x4 = biased.rearrange("p (g e) -> p g e", e=4)
                r2, r3 = sel[:, 2, :], sel[:, 3, :]
                for i, (e, op) in enumerate(((0, ALU.max), (0, ALU.min), (2, ALU.max), (2, ALU.min))):
                    steps(tt(r2[:, 8 * i:8 * i + 8], x4[:, :, e], x4[:, :, e + 1], op))
                steps.sync()
                steps(tt(r3[:, 0:8], r2[:, 0:8], r2[:, 16:24], ALU.max))
                steps(tt(r3[:, 8:16], r2[:, 0:8], r2[:, 16:24], ALU.min))
                steps(tt(r3[:, 16:24], r2[:, 8:16], r2[:, 24:32], ALU.max))
                steps(v.memset(sel[:, 4, 0:16], NEG))
                steps.sync()
                steps(tt(r3[:, 24:32], r3[:, 8:16], r3[:, 16:24], ALU.max))
                steps.sync()
                gs = sel[:, 4, 0:16].rearrange("p (b e) -> p b e", b=TB)
                steps(tt(gs[:, :, 0:4], r3[:, 0:8].rearrange("p (b e) -> p b e", b=TB),
                         r3[:, 24:32].rearrange("p (b e) -> p b e", b=TB), ALU.add))
                steps.sync()
                top = sel[:, 5, :]
                for b in range(TB):
                    steps(v.max(top[:, 8 * b:8 * b + 8], gs[:, b, :]))
                steps.sync()
                for b in range(TB):
                    steps(v.max_index(seli[:, b, :], top[:, 8 * b:8 * b + 8], gs[:, b, :]))
                steps.sync()
                steps(v.tensor_copy(top[:, 16:18], seli[:, :, 0]))
                steps.sync()
                pickg = sel[:, 6, :]
                for b in range(TB):
                    steps(ts(pickg[:, 4 * b:4 * b + 4], iota[:, 0:4], top[:, 16 + b:17 + b], None, ALU.is_equal))
                steps.sync()
                steps(ts(pickg[:, 8:16], pickg[:, 0:8], 1.0, -NEG, ALU.subtract, ALU.mult))
                steps(tt(r2.rearrange("p (g e) -> p g e", e=4), x4, spread(pickg[:, 0:8], 2, [P, 8, 4]), ALU.mult))
                steps.sync()
                steps(tt(r2.rearrange("p (g e) -> p g e", e=4), r2.rearrange("p (g e) -> p g e", e=4),
                         spread(pickg[:, 8:16], 2, [P, 8, 4]), ALU.add))
                steps.sync()
                for b in range(TB):
                    steps(v.max(top[:, 8 * b:8 * b + 8], r2[:, 16 * b:16 * b + 16]))
                steps.sync()
                for b in range(TB):
                    steps(v.max_index(seli[:, b, :], top[:, 8 * b:8 * b + 8], r2[:, 16 * b:16 * b + 16]))
                steps.sync()
                steps(v.tensor_copy(top[:, 16:20].rearrange("p (b e) -> p b e", b=TB), seli[:, :, 0:2]))
                steps.sync()
                for b in range(TB):
                    steps(ts(r3[:, 16 * b:16 * b + 16], iota[:, 0:16], top[:, 16 + 2 * b:17 + 2 * b], None,
                             ALU.is_equal))
                steps.sync()
                for b in range(TB):
                    steps(stt(r3[:, 16 * b:16 * b + 16], iota[:, 0:16], top[:, 17 + 2 * b:18 + 2 * b],
                              r3[:, 16 * b:16 * b + 16], ALU.is_equal, ALU.add))
                steps.sync()
                steps(tt(r3, r3, scores, ALU.mult))
                steps.sync()
                r3b = r3.rearrange("p (b e) -> p b e", b=TB)
                steps(v.tensor_reduce(top[:, 20:22], r3b, AX, ALU.add))
                steps.sync()
                steps(v.reciprocal(top[:, 20:22], top[:, 20:22]))
                steps.sync()
                tt(sel[:, 7, :].rearrange("p (b e) -> p b e", b=TB), r3b,
                   spread(top[:, 20:22], 2, [P, TB, EXPERTS]), ALU.mult).then_inc(comb_ready, 1)

            def moe(l):
                route(l)
                for c in range(BANKS):
                    wait_taken(dve, UNIT_OF["comb", l] + 7 - c)
                u = UNIT_OF["experts", l]
                he, si = room(MOE["he"], 2, 512), room(MOE["si"], 2, 512)
                cb = arena[:, MOE["cb"]:MOE["cb"] + EXPERTS * T]
                with dve.Fori(0, EXPERTS // 2) as it:
                    if l + 1 < LAYERS:
                        steps.enter(it, 6 * (KT - 1))
                    for e in range(2):
                        for s in range(2):
                            ug = u + 4 * e + 2 * s
                            wait_taken(dve, ug, it, 8)
                            wait_full(dve, ug + 1, it, 8)
                            took(tt(he[:, s, :], si[:, s, :], bank(ug + 1)[:, :], ALU.mult), ug + 1)
                            wait_taken(dve, ug + 1, it, 8)
                            h2 = he[:, s, :].rearrange("p (a b) -> p a b", b=T)
                            c = cb[:, bass.ds(it * (2 * T) + e * T, T)]
                            tt(h2, h2, spread(c, 1, [P, 2, T]), ALU.mult).then_inc(he_ready, 1)
                    if l + 1 < LAYERS:
                        ada_turn(l + 1, it, 6)
                if l + 1 < LAYERS:
                    steps.leave(EXPERTS // 2)
                acc_residual(l)

            dve.wait_ge(consts_made, 1)
            dve.wait_ge(cols_landed, 16)
            dve.wait_ge(x_landed, 16)
            dve.wait_ge(c_ready, 1)
            ada_loop(0)
            for l in range(LAYERS):
                mods(l)
                norm(2 * l)
                (first_mixer if l < DEPTH else gla if l == DEPTH else lru)(l)
                residual(l)
                norm(2 * l + 1)
                (peer if l < DEPTH else moe)(l)
            norm(2 * LAYERS)


def _t5_buckets():
    d = np.arange(P)
    exact = BUCKETS // 2
    ratio = np.log(np.maximum(d, 1).astype(np.float32) / np.float32(exact)) / np.float32(
        np.log(MAX_DIST / exact))
    large = np.minimum(exact + (ratio * np.float32(BUCKETS - exact)).astype(np.int32), BUCKETS - 1)
    return np.where(d < exact, d, large)


def _tiles(a):
    n = a.shape[1] // 256
    return a.reshape(KT, P, n, 2, P).transpose(2, 1, 3, 0, 4).reshape(n, P, SLOT)


def _rows(a):
    m = a.shape[1] // 512
    return a.reshape(2, 4, P, m, 512).transpose(3, 0, 2, 1, 4).reshape(2 * m, P, SLOT)


def _stream(i):
    w = np.empty((SLOT_OF["end"], P, SLOT), np.float32)

    def put(name, a):
        w[SLOT_OF[name]:SLOT_OF[name] + len(a)] = a

    q_order = np.concatenate([np.arange(HD) + HD * ((h % 2) * 4 + h // 2) for h in range(HEADS)])
    for l in range(DEPTH):
        a = i["w_in"][l]
        put(("q", l), _rows(a[:, q_order]))
        put(("kv", l), a[:, 512:768].reshape(KT, P, 256).transpose(1, 0, 2).reshape(1, P, SLOT))
        put(("sgu", l), _rows(a[:, 1536:2048]))
        put(("conv", l), _tiles(a[:, 768:1536]))
        put(("out", l), _tiles(i["w_out"][l]))
        put(("pq", l), _tiles(i["peer_wq"][l]))
        put(("keys", l), i["peer_sub_keys"][l].transpose(3, 0, 1, 2).reshape(1, P, SLOT))
        down = i["peer_down"][l].reshape(P, 64, 2, KT, P).transpose(1, 4, 2, 3, 0).reshape(64, P, SLOT)
        up = i["peer_up"][l].reshape(P, 64, SLOT).transpose(1, 0, 2)
        for q in range(QUARTERS):
            put(("down", l, q), down[q * QT_SLOTS:(q + 1) * QT_SLOTS])
            put(("up", l, q), up[q * QT_SLOTS:(q + 1) * QT_SLOTS])
        m = DEPTH + l
        gate, up_, dn = i["moe_w_gate_2"][l], i["moe_w_up_2"][l], i["moe_w_down_2"][l]
        ex = np.empty((EXPERTS, EXP_SLOTS, P, SLOT), np.float32)
        for e in range(EXPERTS):
            ex[e, 0:4:2] = _tiles(gate[e])
            ex[e, 1:4:2] = _tiles(up_[e])
            ex[e, 4:6] = dn[e].reshape(2, 2, P, D).transpose(0, 2, 1, 3).reshape(2, P, SLOT)
        put(("experts", m), ex.reshape(EXPERTS * EXP_SLOTS, P, SLOT))
    l = DEPTH
    a = i["gla_w_in_2"][0]
    put(("gq", l), _tiles(a[:, 0:512]))
    put(("gk", l), _rows(a[:, 512:1024]))
    put(("gv", l), _rows(a[:, 1024:2048]))
    put(("gg", l), _rows(a[:, 2048:3072]))
    put(("out", l), _tiles(i["gla_w_out_2"][0]))
    l = DEPTH + 1
    a = i["lru_w_in_2"][0]
    put(("lru_g", l), _tiles(a[:, 0:D]))
    put(("lru_x", l), _tiles(a[:, D:2 * D]))
    for name, key in (("lru_r", "lru_w_r_2"), ("lru_i", "lru_w_i_2")):
        put((name, l), i[key][0].reshape(4, 2, P, 2, P).transpose(2, 0, 3, 1, 4).reshape(1, P, SLOT))
    put(("out", l), _tiles(i["lru_w_out_2"][0]))
    return w


def _ada(i):
    a = np.concatenate([i["w_ada"], i["ada_w_2"]])
    return np.ascontiguousarray(a.reshape(LAYERS, KT, P, 48, P).transpose(0, 3, 2, 1, 4).reshape(
        LAYERS, 48, P, D))


def _small(i):
    t = np.zeros((P, NCOLS), np.float32)

    def put(name, a):
        at, n = COLS[name]
        t[:, at:at + n] = a

    def vec(a):
        return a.reshape(-1, P).T

    put("c", vec(i["c"][0]))
    put("c2", vec(i["c_2"][0]))
    put("final_g", vec(i["final_norm_g_2"]))
    for l in range(LAYERS):
        first, m = l < DEPTH, l % DEPTH
        put(("b_ada", l), vec(i["b_ada" if first else "ada_b_2"][m]))
        put(("g1", l), vec(i["norm1_g" if first else "norm_mix_g_2"][m]))
        put(("g2", l), vec(i["norm2_g" if first else "norm_ffn_g_2"][m]))
    for l in range(DEPTH):
        put(("gq", l), np.tile(i["q_norm_g"][l], 2)[:, None])
        put(("gk", l), np.tile(i["k_norm_g"][l], 2)[:, None])
        put(("cw", l), vec(i["conv_w"][l].reshape(-1)))
        put(("og", l), vec(i["out_norm_g"][l]))
        put(("sb", l), i["sgu_b"][l].T)
        put(("sink", l), i["attn_sink"][l][None, :])
    put("lcw", vec(i["lru_conv_w_2"][0].reshape(-1)))
    put("lcb", vec(i["lru_conv_b_2"][0]))
    put("lbr", vec(i["lru_b_r_2"][0].reshape(-1)))
    put("lbi", vec(i["lru_b_i_2"][0].reshape(-1)))
    put("lam", vec(i["lru_lambda_2"][0]))
    put("rw", i["router_w_2"].reshape(KT, P, EXPERTS).transpose(1, 0, 2).reshape(P, -1))
    put("rb", i["router_bias_2"][None, :])
    return t


def _first_const(i):
    dist = np.clip(np.arange(P)[:, None] + P - np.arange(T)[None, :], 0, P - 1)
    bias = i["rel_bias"][_t5_buckets()[dist]].transpose(0, 2, 1).reshape(P, -1)
    t = np.empty((DEPTH, P, FIRST_CONST), np.float32)
    t[:, :, 0:2048] = bias
    t[:, :, 2048:2560] = i["sgu_w"].transpose(0, 3, 1, 2).reshape(DEPTH, P, 512)
    return t


def _gla_const(i):
    t = np.zeros((P, GLA_CONST), np.float32)
    t[:, L2["bg"]:L2["bg"] + 512] = i["gla_b_gate_2"][0]
    t[:, L2["ng"]:L2["ng"] + 256] = i["gla_norm_g_2"][0]
    t[0:GRANK, L2["wgu"]:L2["wgu"] + 512] = i["gla_w_gate_up_2"][0]
    t[:, L2["wa"]:L2["wa"] + 128] = i["gla_w_in_2"][0][:, 3072:].reshape(KT, P, GRANK).transpose(
        1, 0, 2).reshape(P, -1)
    return t


def kernel(**inputs):
    import concourse.bacc as bacc
    from concourse.bass_utils import run_bass_kernel_spmd

    i = {k: np.asarray(v) for k, v in inputs.items()}
    arrays = {
        "x_t": np.ascontiguousarray(i["x"][0].T),
        "stream": _stream(i),
        "ada": _ada(i),
        "small": _small(i),
        "first_const": _first_const(i),
        "gla_const": _gla_const(i),
    }
    nc = bacc.Bacc("TRN2", target_bir_lowering=False, num_devices=1)
    args = [nc.dram_tensor(k, a.shape, F32, kind="ExternalInput").ap() for k, a in arrays.items()]
    args.append(nc.dram_tensor("out_t", (D, T), F32, kind="ExternalOutput").ap())
    program(nc, *args)
    r = run_bass_kernel_spmd(nc, [arrays], core_ids=[0])
    return np.ascontiguousarray(r.results[0]["out_t"].T)[None]
```

```python
from contextlib import ExitStack

import numpy as np

import concourse.bass as bass
from concourse import mybir

P = 128
D = 1024
KT = D // P
T = 256
TB = T // P
DEPTH = 2
LAYERS = 2 * DEPTH
EPS = 1e-6
NEG = -1e30

F32 = mybir.dt.float32
F32R = mybir.dt.float32r
BF16 = mybir.dt.bfloat16
U32 = mybir.dt.uint32
ALU = mybir.AluOpType
ACT = mybir.ActivationFunctionType
AX = mybir.AxisListType.X

HEADS, KVH, HD = 8, 2, 64
BUCKETS, MAX_DIST = 32, 128
PH, TOPK, NKEYS = 8, 16, 128
EXPERTS, FE = 16, 512
GH, GDK, GDV, CHUNK, GRANK = 4, 128, 256, 64, 16
CONV2 = 4

SLOT = 16 * P
RING = 2
TURN = 4
BANKS = 4
ADA_RING = 2
QUARTERS = 4
QT_TILES = NKEYS // QUARTERS
QT_SLOTS = QT_TILES // 2
LATE = QT_SLOTS // 2
GROUP = 512 // QT_TILES
EXP_SLOTS = 6


def plan():
    slot, unit, s, u = {}, {}, 0, 0

    def stage(name, slots, units):
        nonlocal s, u
        slot[name], unit[name] = s, u
        s += slots
        u += units

    for l in range(LAYERS):
        stage(("norm", 2 * l), 0, 1)
        stage(("mod", l), 0, 1)
        if l < DEPTH:
            stage(("q", l), 2, 2)
            stage(("kv", l), 1, 1)
            stage(("sgu", l), 2, 2)
            stage(("conv", l), 3, 3)
            stage(("qkT", l), 0, 3)
            if l == 0:
                stage(("mod_next", l), 0, 1)
            stage(("scores", l), 0, 6)
            stage(("conv_sum", l), 0, 1)
            stage(("mix", l), 0, 1)
            stage(("PT", l), 0, 6)
            stage(("PV", l), 0, 2)
            stage(("sguT", l), 0, 1)
            stage(("attnT", l), 0, 2)
            if l == 0:
                stage(("mod_rest", l), 0, 1)
        elif l == DEPTH:
            stage(("gq", l), 2, 2)
            stage(("alr", l), 0, 1)
            stage(("z", l), 0, 2)
            stage(("gk", l), 2, 2)
            stage(("gv", l), 4, 4)
            stage(("gg", l), 4, 4)
            stage(("decay", l), 0, 2)
            stage(("gamma", l), 0, 1)
            stage(("kvs", l), 0, 8)
            stage(("oT", l), 0, 4)
        else:
            stage(("lru_g", l), 4, 4)
            stage(("lru_x", l), 4, 4)
            stage(("lru_r", l), 1, 4)
            stage(("lru_i", l), 1, 4)
        stage(("out", l), 4, 4)
        stage(("norm", 2 * l + 1), 0, 1)
        if l < DEPTH:
            stage(("pq", l), 8, 8)
            stage(("keys", l), 1, 8)
            stage(("down", l, 0), QT_SLOTS, QT_SLOTS)
            stage(("down", l, 1), QT_SLOTS, LATE)
            stage(("idxT", l), 0, 2)
            stage(("late", l), 0, 3 * LATE)
            stage(("up", l, 0), QT_SLOTS, QT_SLOTS)
            stage(("down", l, 2), QT_SLOTS, QT_SLOTS)
            stage(("up", l, 1), QT_SLOTS, QT_SLOTS)
            stage(("down", l, 3), QT_SLOTS, QT_SLOTS)
            stage(("up", l, 2), QT_SLOTS, QT_SLOTS)
            stage(("up", l, 3), QT_SLOTS, 0)
        else:
            stage(("router", l), 0, 1)
            stage(("combT", l), 0, 1)
            stage(("comb", l), 0, 8)
            stage(("experts", l), EXPERTS * EXP_SLOTS, EXPERTS * 4)
    stage(("norm", 2 * LAYERS), 0, 1)
    slot["end"] = s
    assert s % RING == 0
    return slot, unit


SLOT_OF, UNIT_OF = plan()

COLS = {}


def _cols():
    n = 0
    for name, w in (
        [("c", 8), ("c2", 8), ("final_g", 8)]
        + [((k, l), w) for l in range(LAYERS) for k, w in (("b_ada", 48), ("g1", 8), ("g2", 8))]
        + [((k, l), w) for l in range(DEPTH)
           for k, w in (("gq", 1), ("gk", 1), ("cw", 6), ("og", 8), ("sb", 4), ("sink", 8))]
        + [("lcw", 32), ("lcb", 8), ("lbr", 8), ("lbi", 8), ("lam", 8), ("rw", 128), ("rb", 16)]
    ):
        COLS[name] = (n, w)
        n += w
    COLS["end"] = (n, 0)


_cols()
NCOLS = COLS["end"][0]

ROOM = 24576
ACT0, ACT1, TOP = 0, 8192, 16384
MT, SQ, H = ACT1, ACT1 + 2048, ACT1 + 6144
CAND, HOT = TOP + 4096, TOP + 6144
ADA_AT = (2560, 4608, 6656, 12288, 14336, 18432, 20480, 22528)
FIRST = 2 * len(ADA_AT)
ADA_AT_2 = (8192, 12288, 18432, 20480)
SECOND = 2 * 2 * len(ADA_AT_2)
SPLIT = 8 * QT_SLOTS
L1 = dict(bias=0, sgw=2048, qk=2560, v=3840, suv=4096, cb=5120, cc=5632, z=6144, yc=6660, kT=7172,
          vn=7428, lg=12288, pp=14336, pT=16384, qT=19456, ya=20480, ys=21504, sq2=22016, sq3=22528,
          rc=23552, tmp=23808)
FIRST_CONST = 2560
GLA_CONST = 512 + 256 + 512 + 128
L2 = dict(bg=0, ng=512, wgu=768, wa=1280, qT=1408, k=2432, v=3456, gs=5504, alr=7552,
          lg=12288, e=13312, kd=14336, S=16384, o=18432, osq=20480, gam=22528, zz=22560)
L3 = dict(gate=0, xp=2048, xc=4120, r=18432, i=12288, a=14336, t=16384, m=18432, b=12288, hs=20480)
MOE = dict(cb=8192, he=0, si=2048, cT=12288)


def program(nc, x, w, ada, small, first_const, gla_const, out):
    with ExitStack() as ctx:
        def sb(name, shape, dt=F32):
            return ctx.enter_context(nc.sbuf_tensor(name, shape, dt))

        def sem(name):
            return ctx.enter_context(nc.semaphore(name))

        ring = sb("ring", [P, RING, SLOT])
        ada_ring = sb("ada_ring", [P, ADA_RING, D])
        xT = sb("xT", [P, KT, T])
        w_hi, w_lo = sb("w_hi", [P, RING, SLOT], F32R), sb("w_lo", [P, RING, SLOT], F32R)
        h_hi, h_lo = sb("h_hi", [P, KT, T], F32R), sb("h_lo", [P, KT, T], F32R)
        a_hi, a_lo = sb("a_hi", [P, 2, 512], F32R), sb("a_lo", [P, 2, 512], F32R)
        arena = sb("arena", [P, ROOM])
        cols = sb("cols", [P, NCOLS])
        mod = sb("mod", [P, 48])
        gain = sb("gain", [P, 2, KT])
        cact = sb("cact", [P, 2, KT])
        rstd = sb("rstd", [P, T])
        ident = sb("ident", [P, P])
        iota = sb("iota", [P, TOPK])
        steps_of = sb("steps_of", [P, P, GROUP], BF16)
        ones = sb("ones", [P, P])
        one = sb("one", [P, 1])
        zeros = sb("zeros", [P, 512], BF16)
        st = sb("st", [P, 6, 32])
        tv = sb("tv", [P, 16, TOPK])
        ti = sb("ti", [P, 16, TOPK], U32)
        tf = sb("tf", [P, 16, TOPK])
        bv = sb("bv", [P, PH, TOPK])
        bp = sb("bp", [P, 3, PH * TOPK], U32)
        bf = sb("bf", [P, 2, PH * TOPK])
        pick = sb("pick", [P, 3, TB, P])
        pickT = sb("pickT", [P, 2, T], BF16)
        gateT = sb("gateT", [P, 3, T], BF16)
        psr = sb("psr", [P, 16])
        sel = tf[:, :, :].rearrange("p (r a) k -> p r (a k)", a=2)
        seli = ti[:, 0:2, 0:8]
        later = sb("later", [P, P])
        chunk_of = sb("chunk_of", [P, 2])

        unit = [ctx.enter_context(nc.psum_tensor(f"unit{i}", [P, 512], F32)) for i in range(BANKS)]
        acc = [ctx.enter_context(nc.psum_tensor(f"acc{i}", [P, 512], F32)) for i in range(4)]

        slot_landed = [sem(f"slot_landed{i}") for i in range(RING)]
        slot_read = [sem(f"slot_read{i}") for i in range(RING)]
        ada_landed = [sem(f"ada_landed{i}") for i in range(ADA_RING)]
        ada0_landed = [sem(f"ada0_landed{i}") for i in range(len(ADA_AT))]
        batch_landed = [[sem(f"batch{b}_landed{i}") for i in range(len(ADA_AT_2))] for b in range(2)]
        ada0_done = sem("ada0_done")
        ada_done = sem("ada_done")
        half_made = [sem(f"half_made{i}") for i in range(RING)]
        half_read = sem("half_read")
        hi_made, acc_read, a_hi_made, a_made = (
            sem("hi_made"), sem("acc_read"), sem("a_hi_made"), sem("a_made"))
        h_hi_made, h_made, he_made = sem("h_hi_made"), sem("h_made"), sem("he_made")
        unit_full = [sem(f"unit_full{i}") for i in range(BANKS)]
        unit_taken = [sem(f"unit_taken{i}") for i in range(BANKS)]
        dve_step, act_step, pool_step = sem("dve_step"), sem("act_step"), sem("pool_step")
        x_landed, cols_landed, const_landed = sem("x_landed"), sem("cols_landed"), sem("const_landed")
        consts_made = sem("consts_made")
        c_ready = sem("c_ready")
        x_ready, sq_ready, std_ready, h_ready = (
            sem("x_ready"), sem("sq_ready"), sem("std_ready"), sem("h_ready"))
        acc_full, o_full = sem("acc_full"), sem("o_full")
        bias_masked = sem("bias_masked")
        qk_var, qk_std, qk_ready = sem("qk_var"), sem("qk_std"), sem("qk_ready")
        yc_ready, yc_sq, yc_std = sem("yc_ready"), sem("yc_sq"), sem("yc_std")
        vn_var, vn_std, vn_ready = sem("vn_var"), sem("vn_std"), sem("vn_ready")
        lg_ready, exp_done = sem("lg_ready"), sem("exp_done")
        ys_var, ys_std, ys_ready = sem("ys_var"), sem("ys_std"), sem("ys_ready")
        ya_var, ya_std, ya_ready = sem("ya_var"), sem("ya_std"), sem("ya_ready")
        m_ready = sem("m_ready")
        best_ready, gate_exp, pick_ready = sem("best_ready"), sem("gate_exp"), sem("pick_ready")
        hot_ready = sem("hot_ready")
        z_ready, soft_done, la_ready, kd_ready = (
            sem("z_ready"), sem("soft_done"), sem("la_ready"), sem("kd_ready"))
        o_var, o_std, o_ready = sem("o_var"), sem("o_std"), sem("o_ready")
        xc_ready, lam_abs, lam_exp, lam_ready = sem("xc_ready"), sem("lam_abs"), sem("lam_exp"), sem("lam_ready")
        tanh_done, m_sq, m_root = sem("tanh_done"), sem("m_sq"), sem("m_root")
        comb_ready = sem("comb_ready")
        stored = sem("stored")

        def room(at, *shape):
            n = int(np.prod(shape))
            v = arena[:, at:at + n]
            if len(shape) == 2:
                v = v.rearrange("p (a b) -> p a b", b=shape[1])
            elif len(shape) == 3:
                v = v.rearrange("p (a b c) -> p a b c", b=shape[1], c=shape[2])
            return v

        def spread(a, axis, shape):
            return a.unsqueeze(axis).broadcast_to(shape)

        def col(name, i=None):
            at, n = COLS[name]
            return cols[:, at:at + n] if i is None else cols[:, at + i:at + i + 1]

        mT = room(MT, KT, T)
        sq = room(SQ, KT, T)
        hT = room(H, KT, T)
        ada_sum = arena[:, TOP:TOP + 6 * D]
        ada_rest = w_lo[:, 0, :].bitcast(F32)
        ohi = room(HOT, 1024).bitcast(BF16).rearrange("p (i t) -> p i t", t=GROUP)
        ohj = room(HOT + 1024, 768).bitcast(BF16).rearrange("p (c j t) -> p c j t", c=3, t=GROUP)
        eqj = room(HOT + 1792, 256).bitcast(BF16).rearrange("p (j t) -> p j t", t=GROUP)

        class Steps:

            def __init__(self, eng, s):
                self.eng, self.sem, self.n, self.base = eng, s, 0, 0

            def __call__(self, ins):
                self.n += 1
                ins.then_inc(self.sem, 1)

            def sync(self, back=0):
                self.eng.wait_ge(self.sem, self.base + (self.n - back))

            def enter(self, it, per):
                self.base, self.per, self.at = it * per, per, self.n

            def leave(self, times):
                assert self.n - self.at == self.per, self.n - self.at
                self.base = 0
                self.n = self.at + self.per * times

        def upto(base, it, step):
            return base if it is None else it * step + base

        def wait_full(eng, u, it=None, per=0):
            eng.wait_ge(unit_full[u % BANKS], upto(u // BANKS + 1, it, per // BANKS))

        def wait_taken(eng, u, it=None, per=0):
            eng.wait_ge(unit_taken[u % BANKS], upto(u // BANKS + 1, it, per // BANKS))

        def bank(u):
            return unit[u % BANKS]

        def wait_slot(eng, n, it=None, turn=TURN):
            eng.wait_ge(slot_landed[n % RING], upto(16 * (n // RING + 1), it, 16 * turn // RING))

        def split_index(n):
            for l in range(LAYERS):
                n0 = SLOT_OF[("down", l, 0) if l < DEPTH else ("experts", l)]
                size = SPLIT if l < DEPTH else EXPERTS * EXP_SLOTS
                if n0 <= n < n0 + size:
                    return min(l, DEPTH) * SPLIT + max(l - DEPTH, 0) * size + n - n0
            raise ValueError(n)

        def half_of(n, half):
            return n % RING, slice(half * (SLOT // 2), (half + 1) * (SLOT // 2))

        def hi_part(act, n, half, it=None, turn=TURN):
            wait_slot(act, n, it, turn)
            i, c = half_of(n, half)
            nc.scalar.activation(w_hi[:, i, c], ring[:, i, c], ACT.Copy).then_inc(hi_made, 1)

        def lo_part(eng, ns, n, half, it=None, turn=TURN):
            eng.wait_ge(hi_made, upto(2 * split_index(n) + half + 1, it, 2 * turn))
            i, c = half_of(n, half)
            ns.tensor_tensor(w_lo[:, i, c], ring[:, i, c], w_hi[:, i, c].bitcast(F32),
                             ALU.subtract).then_inc((slot_read if half else half_made)[i], 1)

        def a_rest(eng, ns, count, it, step, a, src):
            eng.wait_ge(a_hi_made, upto(count, it, step))
            ns.tensor_tensor(a_lo[:, a, :], src, a_hi[:, a, :].bitcast(F32), ALU.subtract).then_inc(a_made, 1)

        def wait_half_read(eng, n, it=None, turn=TURN):
            eng.wait_ge(half_read, upto(split_index(n) + 1, it, turn))

        def hidden_base(l):
            return DEPTH * QUARTERS * QT_SLOTS + 2 * EXPERTS * (l - DEPTH)

        stages = [("down", 0, None), ("down", 1, 0), ("up", 0, 1), ("down", 2, None), ("up", 1, 2),
                  ("down", 3, None), ("up", 2, 3), ("up", 3, None)]
        def down_unit(l, q, s):
            return UNIT_OF["down", l, q] + s if q != 1 or s < LATE else UNIT_OF["late", l] + 3 * (s - LATE)

        def down_units(q, s):
            return TURN * 3 if q == 1 and s >= LATE else TURN

        def gate_unit(l, gq, g):
            if gq == 0:
                return down_unit(l, 1, LATE + g // 2) + 1 + g % 2
            return UNIT_OF["up", l, gq - 1] + g

        block = ctx.enter_context(nc.Block())

        @block.sync
        def _(sp):
            sp.dma_start(cols[:, :], small).then_inc(cols_landed, 16)
            sp.dma_start(xT[:, :, :], x.rearrange("(k p) t -> p k t", p=P)).then_inc(x_landed, 16)
            first = ada[0].rearrange("(n a) p d -> n p a d", a=2)
            for i, at in enumerate(ADA_AT):
                sp.dma_start(room(at, 2, D), first[i]).then_inc(ada0_landed[i], 16)
            for n in range(RING):
                sp.dma_start(ring[:, n, :], w[n]).then_inc(slot_landed[n], 16)
            sp.wait_ge(ada0_done, FIRST // 2)
            for i, at in enumerate(ADA_AT_2):
                sp.dma_start(room(at, 2, D), first[FIRST // 2 + i]).then_inc(batch_landed[0][i], 16)
            for n in range(RING, TURN):
                sp.wait_ge(slot_read[n % RING], n // RING)
                sp.dma_start(ring[:, n % RING, :], w[n]).then_inc(slot_landed[n % RING], 16)
            with sp.Fori(1, SLOT_OF["end"] // TURN) as it:
                for s in range(TURN):
                    sp.wait_ge(slot_read[s % RING], it * (TURN // RING) + s // RING)
                    sp.dma_start(ring[:, s % RING, :], w[it * TURN + s]).then_inc(slot_landed[s % RING], 16)
            sp.wait_ge(h_ready, 2 * LAYERS + 1)
            sp.dma_start(out.rearrange("(k p) t -> p k t", p=P), hT[:, :, :]).then_inc(stored, 16)
            sp.wait_ge(stored, 16)

        @block.gpsimd
        def _(pool):
            g = nc.gpsimd
            steps = Steps(pool, pool_step)

            flat = ada.rearrange("l a p d -> (l a) p d")

            def ada_load(piece, s):
                pool.dma_start(ada_ring[:, s, :], flat[piece]).then_inc(ada_landed[s], 16)

            def ada_piece(l, turn, s, it, load=True):
                c = cact[:, l // DEPTH, :]
                base = turn + ((48 - FIRST - SECOND) // ADA_RING + 48 // ADA_RING * (l - 1) if l else 0)
                pool.wait_ge(ada_landed[s], upto(16 * (base + 1), it, 16))
                piece = ada_ring[:, s, :]
                p3 = piece.rearrange("p (k d) -> p k d", d=P)
                steps(g.tensor_tensor(p3, p3, spread(c, 2, [P, KT, P]), ALU.mult))
                for n in (512, 256):
                    steps.sync()
                    steps(g.tensor_tensor(piece[:, 0:n], piece[:, 0:n], piece[:, n:2 * n], ALU.add))
                steps.sync()
                at = (turn * ADA_RING + s) * P
                at = slice(at, at + P) if it is None else bass.ds(it * (ADA_RING * P) + at, P)
                g.tensor_tensor((ada_sum if l else ada_rest)[:, at], piece[:, 0:P],
                                piece[:, P:2 * P], ALU.add).then_inc(ada_done, 1)
                if load:
                    pool.wait_ge(ada_done, upto(base * ADA_RING + s + 1, it, ADA_RING))
                    ada_load(upto(FIRST + SECOND + (base + 1) * ADA_RING + s, it, ADA_RING), s)

            def ada_loop(l, turns, first=0):
                last = l + 1 == LAYERS
                with pool.Fori(0, turns - last) as it:
                    steps.enter(it, ADA_RING * 3)
                    for s in range(ADA_RING):
                        ada_piece(l, first, s, it)
                steps.leave(turns - last)
                if last:
                    for s in range(ADA_RING):
                        ada_piece(l, turns - 1, s, None, False)

            def ada_and_rests(l):
                turns = QT_SLOTS // TURN
                assert len(stages[2:]) * turns * ADA_RING == 48
                for i, (kind, q, _) in enumerate(stages[2:]):
                    up = kind == "up"
                    act_q = arena[:, (q % 2) * 8192:(q % 2 + 1) * 8192]
                    base = QT_SLOTS * (QUARTERS * l + q)

                    def turn(it, first, last):
                        for s in range(first, first + TURN):
                            if up and not (last and s >= QT_SLOTS - 2):
                                src = act_q[:, (s + 2) * 512:(s + 3) * 512] if it is None else (
                                    act_q[:, bass.ds(it * (TURN * 512) + (s + 2) * 512, 512)])
                                a_rest(pool, g, base + s + 3, it, TURN, s % 2, src)
                            if s % 2:
                                ada_piece(l + 1, i * turns + first // TURN, s % TURN // 2, it)

                    if up:
                        for s in range(2):
                            a_rest(pool, g, base + s + 1, None, 0, s, act_q[:, s * 512:(s + 1) * 512])
                    with pool.Fori(0, turns - up) as it:
                        steps.enter(it, ADA_RING * 3)
                        turn(it, 0, False)
                    steps.leave(turns - up)
                    if up:
                        turn(None, QT_SLOTS - TURN, True)

            def take_apart(l):
                n = SLOT_OF["down", l, 0]
                for s in range(2):
                    for half in range(2):
                        lo_part(pool, g, n + s, half)
                with pool.Fori(0, 2 * QT_SLOTS // TURN) as it:
                    for s in range(TURN):
                        for half in range(2):
                            lo_part(pool, g, n + 2 + s, half, it)

            steps(g.memset(ident[:, :], 0.0))
            steps(g.memset(later[:, :], 1.0 / 16.0))
            steps(g.memset(chunk_of[:, :], 1.0 / 16.0))
            steps(g.memset(ones[:, :], 1.0 / D))
            steps(g.memset(one[:, :], 1.0))
            steps(g.iota(iota[:, :], pattern=[[1, TOPK]], base=0, channel_multiplier=0,
                         allow_small_or_imprecise_dtypes=True))
            steps(g.iota(steps_of[:, :, :], pattern=[[1, P], [0, GROUP]], base=0, channel_multiplier=0,
                         allow_small_or_imprecise_dtypes=True))
            steps.sync()
            steps(g.affine_select(out=ident[:, :], in_=ident[:, :], compare_op=ALU.not_equal,
                                  fill=1.0, base=0, pattern=[[-1, P]], channel_multiplier=1))
            steps(g.affine_select(out=later[:, :], in_=later[:, :], compare_op=ALU.is_gt,
                                  fill=0.0, base=0, pattern=[[-1, P]], channel_multiplier=1))
            steps(g.affine_select(out=chunk_of[:, 0:1], in_=chunk_of[:, 0:1], compare_op=ALU.is_ge,
                                  fill=0.0, base=CHUNK - 1, pattern=[[0, 1]], channel_multiplier=-1))
            steps(g.affine_select(out=chunk_of[:, 1:2], in_=chunk_of[:, 1:2], compare_op=ALU.is_ge,
                                  fill=0.0, base=-CHUNK, pattern=[[0, 1]], channel_multiplier=1))
            steps.sync()
            steps(g.memset(later[CHUNK:P, 0:CHUNK], 0.0))
            steps.sync()
            g.memset(zeros[:, :], 0.0).then_inc(consts_made, 1)

            def first_masks(l):
                pool.wait_ge(const_landed, 16 * (l + 1))
                b = room(L1["bias"], HEADS, T)
                steps(g.affine_select(out=b, in_=b, compare_op=ALU.is_ge, fill=NEG, base=P,
                                      pattern=[[0, HEADS], [-1, T]], channel_multiplier=1))
                steps.sync()
                steps(g.affine_select(out=b, in_=b, compare_op=ALU.is_gt, fill=NEG, base=0,
                                      pattern=[[0, HEADS], [1, T]], channel_multiplier=-1))
                steps.sync()
                wv = room(L1["sgw"], 4, P)
                g.affine_select(out=wv, in_=wv, compare_op=ALU.is_ge, fill=0.0, base=0,
                                pattern=[[0, 4], [1, P]], channel_multiplier=-1).then_inc(bias_masked, 1)

            pool.dma_start(arena[:, 0:FIRST_CONST], first_const[0]).then_inc(const_landed, 16)
            for s in range(ADA_RING):
                ada_load(FIRST + SECOND + s, s)
            first_masks(0)
            pool.wait_ge(c_ready, 1)
            for l in range(LAYERS):
                if l:
                    pool.wait_ge(x_ready, 2 * l)
                if 0 < l < DEPTH:
                    pool.dma_start(arena[:, 0:FIRST_CONST], first_const[l]).then_inc(const_landed, 16)
                    first_masks(l)
                elif l == DEPTH:
                    pool.dma_start(arena[:, 0:GLA_CONST], gla_const).then_inc(const_landed, 16)
                if l == 0:
                    turns = (48 - FIRST - SECOND) // ADA_RING
                    n = len(ADA_AT_2)
                    ada_loop(0, 2)
                    pool.wait_ge(ada0_done, FIRST // 2 + n)
                    for i, at in enumerate(ADA_AT_2):
                        pool.dma_start(room(at, 2, D), ada[0].rearrange("(n a) p d -> n p a d", a=2)[
                            FIRST // 2 + n + i]).then_inc(batch_landed[1][i], 16)
                    ada_loop(0, turns - 2, 2)
                if l < DEPTH:
                    take_apart(l)
                    pool.wait_ge(pick_ready, l + 1)
                    ada_and_rests(l)
                elif l + 1 < LAYERS:
                    pool.wait_ge(x_ready, 2 * l + 1)
                    ada_loop(l + 1, 48 // ADA_RING)

        @block.tensor
        def _(pe):
            mm = nc.tensor.matmul

            def open_bank(u, it=None, per=0):
                if u >= BANKS:
                    wait_taken(pe, u - BANKS, it, per)

            def slot_mms(n, mms, ends=(), after=True):
                wait_slot(pe, n)
                ends = dict(ends)
                for i, (o, a, b, start, stop) in enumerate(mms):
                    ins = mm(o, a, b, start=start, stop=stop, skip_group_check=True)
                    if i == 0 and after:
                        ins.then_inc(slot_read[(n - 1) % RING], 1)
                    if i in ends:
                        ins.then_inc(ends[i], 1)

            def tile(n, i):
                return ring[:, n % RING, i * P:(i + 1) * P]

            def feature_slot(n, u, act, after=True):
                open_bank(u)
                mms = [(bank(u)[:, j * T:(j + 1) * T], tile(n, j * KT + k), act[:, k, :], k == 0, k == KT - 1)
                       for j in range(2) for k in range(KT)]
                slot_mms(n, mms, {15: unit_full[u % BANKS]}, after)

            def token_slots(n, u, act, after=True):
                for b in range(TB):
                    open_bank(u + b)
                for s in range(2):
                    mms = [(bank(u + b)[:, :], act[:, 4 * s + k, b * P:(b + 1) * P],
                            ring[:, (n + s) % RING, k * 512:(k + 1) * 512], s + k == 0, s == 1 and k == 3)
                           for b in range(TB) for k in range(4)]
                    slot_mms(n + s, mms, {3: unit_full[u % BANKS], 7: unit_full[(u + 1) % BANKS]} if s else {},
                             after or s > 0)

            def products(o, n, i, hi, lo, start, stop):
                a, b = w_hi[:, n % RING, i * P:(i + 1) * P], w_lo[:, n % RING, i * P:(i + 1) * P]
                mm(o, a, hi, start=start, stop=False, skip_group_check=True)
                mm(o, a, lo, start=False, stop=False, skip_group_check=True)
                return mm(o, b, hi, start=False, stop=stop, skip_group_check=True)

            def wait_parts(n, half, it=None, turn=TURN):
                if half:
                    pe.wait_ge(slot_read[n % RING], upto(n // RING + 1, it, turn // RING))
                else:
                    pe.wait_ge(half_made[n % RING], upto(split_index(n) // RING + 1, it, turn // RING))

            def split_unit(n, u, it, per, turn=TURN, between=None):
                open_bank(u, it, per)
                for j in range(2):
                    wait_parts(n, j, it, turn)
                    for k in range(KT):
                        ins = products(bank(u)[:, j * T:(j + 1) * T], n, j * KT + k, h_hi[:, k, :], h_lo[:, k, :],
                                       k == 0, k == KT - 1)
                    if j == 0:
                        ins.then_inc(half_read, 1)
                        if between:
                            between()
                ins.then_inc(unit_full[u % BANKS], 1)

            def split_sum(n, a, it, turn=TURN):
                for j in range(2):
                    wait_parts(n, j, it, turn)
                    for d in range(KT):
                        ins = products(acc[d // 2][:, (d % 2) * T:(d % 2 + 1) * T], n, j * KT + d,
                                       a_hi[:, a, j * T:(j + 1) * T], a_lo[:, a, j * T:(j + 1) * T], False, False)
                    ins.then_inc(acc_read if j else half_read, 1)

            def transposes(u, srcs):
                open_bank(u)
                for i, a in enumerate(srcs):
                    ins = nc.tensor.transpose(bank(u)[:, i * P:(i + 1) * P], a, ident[:, :])
                ins.then_inc(unit_full[u % BANKS], 1)

            def norm(i):
                u = UNIT_OF["norm", i]
                open_bank(u)
                for k in range(KT):
                    if k % (KT // 2) == 0:
                        pe.wait_ge(sq_ready, 2 * i + 2 * k // KT + 1)
                    ins = mm(bank(u)[:, 0:T], ones[:, :], sq[:, k, :], start=k == 0, stop=k == KT - 1)
                    if k == 0 and i % 2 and i > 2 * DEPTH:
                        ins.then_inc(slot_read[(SLOT_OF["experts", i // 2] - 1) % RING], 1)
                ins.then_inc(unit_full[u % BANKS], 1)

            def mod_sums(u, sums, first, n):
                open_bank(u)
                for i in range(n):
                    ins = mm(bank(u)[:, first + i:first + i + 1], sums[:, i * P:(i + 1) * P], one[:, :],
                             start=True, stop=True)
                ins.then_inc(unit_full[u % BANKS], 1)

            def mods(l):
                if l:
                    pe.wait_ge(ada_done, 48 * (l + 1) - FIRST - SECOND)
                    mod_sums(UNIT_OF["mod", l], ada_sum, 0, 48)
                else:
                    pe.wait_ge(ada0_done, len(ADA_AT))
                    mod_sums(UNIT_OF["mod", l], ada_sum, 0, FIRST)

            def out_proj(l):
                if l == 0:
                    pe.wait_ge(ada_done, 48 - FIRST - SECOND)
                    mod_sums(UNIT_OF["mod_rest", 0], ada_rest, FIRST + SECOND, 48 - FIRST - SECOND)
                pe.wait_ge(m_ready, l + 1)
                for s in range(4):
                    feature_slot(SLOT_OF["out", l] + s, UNIT_OF["out", l] + s, mT)

            def clear_acc(n=None):
                for b in range(4):
                    ins = mm(acc[b][:, :], zeros[:, 0:P], zeros[:, :], start=True, stop=False,
                             skip_group_check=True)
                    if b == 0 and n is not None:
                        ins.then_inc(slot_read[n % RING], 1)

            def first_mixer(l):
                pe.wait_ge(h_ready, 2 * l + 1)
                token_slots(SLOT_OF["q", l], UNIT_OF["q", l], hT, False)
                n, u = SLOT_OF["kv", l], UNIT_OF["kv", l]
                open_bank(u)
                slot_mms(n, [(bank(u)[:, b * 256:(b + 1) * 256], hT[:, k, b * P:(b + 1) * P],
                              ring[:, n % RING, k * 256:(k + 1) * 256], k == 0, k == KT - 1)
                             for b in range(TB) for k in range(KT)], {15: unit_full[u % BANKS]})
                token_slots(SLOT_OF["sgu", l], UNIT_OF["sgu", l], hT)
                for s in range(3):
                    feature_slot(SLOT_OF["conv", l] + s, UNIT_OF["conv", l] + s, hT)
                qk = room(L1["qk"], TB, 640)
                pe.wait_ge(qk_ready, l + 1)
                u = UNIT_OF["qkT", l]
                transposes(u, [qk[:, b, 512:640] for b in range(TB)])
                for b in range(TB):
                    transposes(u + 1 + b, [qk[:, b, i * P:(i + 1) * P] for i in range(4)])
                if l == 0:
                    pe.wait_ge(ada0_done, (FIRST + SECOND) // 2)
                    mod_sums(UNIT_OF["mod_next", 0], ada_sum, FIRST, SECOND)
                qT, kT = room(L1["qT"], TB, 4, P), room(L1["kT"], T)
                u = UNIT_OF["scores", l]
                wait_taken(pe, UNIT_OF["qkT", l])
                for b in range(TB):
                    wait_taken(pe, UNIT_OF["qkT", l] + 1 + b)
                    nk = P * (b + 1)
                    per = 512 // nk
                    for c in range(HEADS // per):
                        open_bank(u)
                        for h in range(per):
                            j, i = divmod(c * per + h, 4)
                            ins = mm(bank(u)[:, h * nk:(h + 1) * nk], qT[64 * j:64 * j + 64, b, i, :],
                                     kT[64 * j:64 * j + 64, 0:nk], start=True, stop=True)
                        ins.then_inc(unit_full[u % BANKS], 1)
                        u += 1
                u = UNIT_OF["conv_sum", l]
                pe.wait_ge(yc_sq, l + 1)
                open_bank(u)
                s2 = room(L1["sq2"], 2, T)
                for k in range(2):
                    ins = mm(bank(u)[:, 0:T], ones[:, :], s2[:, k, :], start=k == 0, stop=k == 1)
                ins.then_inc(unit_full[u % BANKS], 1)
                u = UNIT_OF["mix", l]
                pe.wait_ge(vn_ready, l + 1)
                pe.wait_ge(bias_masked, l + 1)
                open_bank(u)
                sgw, vn = room(L1["sgw"], 4, P), room(L1["vn"], TB, 256)
                for b in range(TB):
                    for g in range(4):
                        ins = mm(bank(u)[:, b * 256 + g * 64:b * 256 + (g + 1) * 64], sgw[:, g, :],
                                 vn[:, b, g * 64:(g + 1) * 64], start=True, stop=True)
                ins.then_inc(unit_full[u % BANKS], 1)
                pp, pT = room(L1["pp"], HEADS, T), room(L1["pT"], 24, P)
                v = room(L1["v"], TB, P)
                u = UNIT_OF["PT", l]
                for b in range(TB):
                    pe.wait_ge(exp_done, 2 * l + b + 1)
                    flat = [pp[:, h, s * P:(s + 1) * P] for h in range(HEADS) for s in range(b + 1)]
                    for c in range(2 * (b + 1)):
                        transposes(u, flat[4 * c:4 * c + 4])
                        u += 1
                u = UNIT_OF["PV", l]
                for b in range(TB):
                    for c in range(2 * (b + 1)):
                        wait_taken(pe, UNIT_OF["PT", l] + 2 * b + c)
                    open_bank(u)
                    for h in range(HEADS):
                        for s in range(b + 1):
                            ins = mm(bank(u)[:, h * 64:(h + 1) * 64],
                                     pT[:, 8 * b + h * (b + 1) + s, :],
                                     v[:, s, h // 4 * 64:(h // 4 + 1) * 64], start=s == 0, stop=s == b)
                    ins.then_inc(unit_full[u % BANKS], 1)
                    u += 1
                ys, ya = room(L1["ys"], TB, 256), room(L1["ya"], TB, 512)
                pe.wait_ge(ys_ready, l + 1)
                transposes(UNIT_OF["sguT", l], [ys[:, b, i * P:(i + 1) * P] for i in range(2) for b in range(TB)])
                pe.wait_ge(ya_ready, l + 1)
                for b in range(TB):
                    transposes(UNIT_OF["attnT", l] + b, [ya[:, b, i * P:(i + 1) * P] for i in range(4)])

            def gates(l, gq, g, it, groups, per):
                u = gate_unit(l, gq, g)
                open_bank(u, it, per)
                pe.wait_ge(hot_ready, upto((T // GROUP) * (QUARTERS * l + gq) + g + 1, it, groups))
                for t in range(GROUP):
                    for c in range(3):
                        ins = mm(bank(u)[:, t * QT_TILES:(t + 1) * QT_TILES], ohi[:, :, t], ohj[:, c, :, t],
                                 start=c == 0, stop=c == 2)
                ins.then_inc(unit_full[u % BANKS], 1)

            def down(l, q):
                n = SLOT_OF["down", l, q]
                with pe.Fori(0, QT_SLOTS // TURN) as it:
                    for s in range(TURN):
                        split_unit(n + s, down_unit(l, q, s), it, TURN)

            def up(l, q):
                n = SLOT_OF["up", l, q]
                with pe.Fori(0, QT_SLOTS // TURN) as it:
                    for s in range(TURN):
                        pe.wait_ge(a_made, it * TURN + (QT_SLOTS * (QUARTERS * l + q) + s + 1))
                        split_sum(n + s, s % 2, it)
                        if q < QUARTERS - 1:
                            gates(l, q + 1, s, it, TURN, TURN)

            def peer(l):
                pe.wait_ge(h_ready, 2 * l + 2)
                for s in range(8):
                    feature_slot(SLOT_OF["pq", l] + s, UNIT_OF["pq", l] + s, hT)
                n, u = SLOT_OF["keys", l], UNIT_OF["keys", l]
                qT = room(ACT1, 16, T)
                for b in range(BANKS):
                    wait_taken(pe, UNIT_OF["pq", l] + 7 - b)
                wait_slot(pe, n)
                for b in range(TB):
                    for c in range(4):
                        open_bank(u)
                        for i in range(4):
                            g = 4 * c + i
                            ins = mm(bank(u)[:, i * P:(i + 1) * P], qT[:, g, b * P:(b + 1) * P], tile(n, g),
                                     start=True, stop=True)
                            if b + c + i == 0:
                                ins.then_inc(slot_read[(n - 1) % RING], 1)
                        ins.then_inc(unit_full[u % BANKS], 1)
                        u += 1
                clear_acc(n)
                pe.wait_ge(h_made, l + 1)
                down(l, 0)
                picks_and_down(l)
                for kind, q, _ in stages[2:]:
                    (down if kind == "down" else up)(l, q)
                end_acc()

            def picks_and_down(l):
                n = SLOT_OF["down", l, 1]
                with pe.Fori(0, LATE // TURN) as it:
                    for s in range(TURN):
                        split_unit(n + s, down_unit(l, 1, s), it, TURN)
                pe.wait_ge(pick_ready, l + 1)
                u = UNIT_OF["idxT", l]
                transposes(u, [pick[:, a, b, :] for a in range(2) for b in range(TB)])
                transposes(u + 1, [pick[:, 2, b, :] for b in range(TB)])
                per = down_units(1, LATE)
                with pe.Fori(0, LATE // TURN) as it:
                    for s in range(LATE, LATE + TURN):
                        g = 2 * (s - LATE)
                        split_unit(n + s, down_unit(l, 1, s), it, per,
                                   between=lambda: gates(l, 0, g, it, 2 * TURN, per))
                        gates(l, 0, g + 1, it, 2 * TURN, per)

            def end_acc():
                for b in range(4):
                    ins = mm(acc[b][:, :], zeros[:, 0:P], zeros[:, :], start=False, stop=True,
                             skip_group_check=True)
                ins.then_inc(acc_full, 1)

            def gla(l):
                pe.wait_ge(h_ready, 2 * l + 1)
                for s in range(2):
                    feature_slot(SLOT_OF["gq", l] + s, UNIT_OF["gq", l] + s, hT, s > 0)
                pe.wait_ge(const_landed, 16 * (DEPTH + 1))
                wa = room(L2["wa"], KT, GRANK)
                u = UNIT_OF["alr", l]
                open_bank(u)
                for k in range(KT):
                    ins = mm(bank(u)[0:GRANK, 0:T], wa[:, k, :], hT[:, k, :], start=k == 0, stop=k == KT - 1)
                ins.then_inc(unit_full[u % BANKS], 1)
                wait_taken(pe, u)
                alr = arena[0:GRANK, L2["alr"]:L2["alr"] + T]
                u = UNIT_OF["z", l]
                for b in range(TB):
                    open_bank(u + b)
                    mm(bank(u + b)[:, :], alr[:, b * P:(b + 1) * P],
                       arena[0:GRANK, L2["wgu"]:L2["wgu"] + 512], start=True, stop=True).then_inc(
                           unit_full[(u + b) % BANKS], 1)
                token_slots(SLOT_OF["gk", l], UNIT_OF["gk", l], hT)
                for c in range(2):
                    token_slots(SLOT_OF["gv", l] + 2 * c, UNIT_OF["gv", l] + 2 * c, hT)
                for c in range(2):
                    token_slots(SLOT_OF["gg", l] + 2 * c, UNIT_OF["gg", l] + 2 * c, hT)
                la = room(L2["zz"], TB, 512)
                pe.wait_ge(la_ready, 1)
                u = UNIT_OF["decay", l]
                for b in range(TB):
                    open_bank(u + b)
                    mm(bank(u + b)[:, :], later[:, :], la[:, b, :], start=True, stop=True).then_inc(
                        unit_full[(u + b) % BANKS], 1)
                u = UNIT_OF["gamma", l]
                open_bank(u)
                for h in range(GH):
                    for b in range(TB):
                        ins = mm(bank(u)[:, h * 4 + 2 * b:h * 4 + 2 * b + 2], la[:, b, h * GDK:(h + 1) * GDK],
                                 chunk_of[:, :], start=True, stop=True)
                ins.then_inc(unit_full[u % BANKS], 1)
                kd, v = room(L2["kd"], TB, 512), room(L2["v"], TB, 1024)
                S, qT = room(L2["S"], 2, GH, GDV), room(L2["qT"], GH, T)
                pe.wait_ge(kd_ready, 1)
                u = UNIT_OF["kvs", l]

                def kvs(c):
                    b, r = c // 2, CHUNK * (c % 2)
                    for a in range(2):
                        open_bank(u + 2 * c + a)
                        for h in range(2 * a, 2 * a + 2):
                            ins = mm(bank(u + 2 * c + a)[:, (h % 2) * GDV:(h % 2 + 1) * GDV],
                                     kd[r:r + CHUNK, b, h * GDK:(h + 1) * GDK],
                                     v[r:r + CHUNK, b, h * GDV:(h + 1) * GDV], start=True, stop=True)
                        ins.then_inc(unit_full[(u + 2 * c + a) % BANKS], 1)

                def outs(c):
                    b, r = c // 2, CHUNK * (c % 2)
                    wait_taken(pe, u + 2 * c)
                    wait_taken(pe, u + 2 * c + 1)
                    for h in range(GH):
                        ins = mm(acc[2 * b + h // 2][r:r + CHUNK, (h % 2) * GDV:(h % 2 + 1) * GDV],
                                 qT[:, h, c * CHUNK:(c + 1) * CHUNK], S[:, c % 2, h, :],
                                 start=True, stop=True, skip_group_check=True)
                    ins.then_inc(o_full, 1)

                kvs(0)
                for c in range(T // CHUNK):
                    if c + 1 < T // CHUNK:
                        kvs(c + 1)
                    outs(c)
                o = room(L2["o"], TB, 1024)
                pe.wait_ge(o_ready, 1)
                u = UNIT_OF["oT", l]
                for b in range(TB):
                    for c in range(2):
                        transposes(u, [o[:, b, (4 * c + i) * P:(4 * c + i + 1) * P] for i in range(4)])
                        u += 1

            def lru(l):
                pe.wait_ge(h_ready, 2 * l + 1)
                for name in ("lru_g", "lru_x"):
                    for s in range(4):
                        feature_slot(SLOT_OF[name, l] + s, UNIT_OF[name, l] + s, hT, name == "lru_x" or s > 0)
                xc = room(L3["xc"], KT, T)
                pe.wait_ge(xc_ready, 1)
                for name in ("lru_r", "lru_i"):
                    n, u = SLOT_OF[name, l], UNIT_OF[name, l]
                    wait_slot(pe, n)
                    for blk in range(4):
                        open_bank(u + blk)
                        for j in range(2):
                            for k in range(2):
                                ins = mm(bank(u + blk)[:, j * T:(j + 1) * T], tile(n, blk * 4 + j * 2 + k),
                                         xc[:, 2 * blk + k, :], start=k == 0, stop=k == 1)
                                if blk + j + k == 0:
                                    ins.then_inc(slot_read[(n - 1) % RING], 1)
                        ins.then_inc(unit_full[(u + blk) % BANKS], 1)

            def moe(l):
                pe.wait_ge(h_ready, 2 * l + 2)
                u = UNIT_OF["router", l]
                at, _ = COLS["rw"]
                open_bank(u)
                for b in range(TB):
                    for k in range(KT):
                        ins = mm(bank(u)[:, b * 16:(b + 1) * 16], hT[:, k, b * P:(b + 1) * P],
                                 cols[:, at + 16 * k:at + 16 * (k + 1)], start=k == 0, stop=k == KT - 1)
                ins.then_inc(unit_full[u % BANKS], 1)
                pe.wait_ge(comb_ready, l - DEPTH + 1)
                u = UNIT_OF["combT", l]
                open_bank(u)
                for b in range(TB):
                    ins = nc.tensor.transpose(bank(u)[0:16, b * P:(b + 1) * P], sel[:, 7, b * 16:(b + 1) * 16],
                                              ident[:, :])
                ins.then_inc(unit_full[u % BANKS], 1)
                wait_taken(pe, u)
                cT = arena[0:16, MOE["cT"]:MOE["cT"] + T]
                u = UNIT_OF["comb", l]
                for e in range(EXPERTS):
                    if e % 2 == 0:
                        open_bank(u)
                    ins = mm(bank(u)[:, (e % 2) * T:(e % 2 + 1) * T], ident[0:16, e:e + 1].broadcast_to([16, P]), cT,
                             start=True, stop=True)
                    if e % 2:
                        ins.then_inc(unit_full[u % BANKS], 1)
                        u += 1
                clear_acc()
                n, u = SLOT_OF["experts", l], UNIT_OF["experts", l]
                pe.wait_ge(h_made, l + 1)
                turn = 2 * EXP_SLOTS
                with pe.Fori(0, EXPERTS // 2) as it:
                    for e in range(2):
                        m, ue = n + EXP_SLOTS * e, u + 4 * e
                        for s in range(4):
                            split_unit(m + s, ue + s, it, 8, turn)
                        for s in range(2):
                            pe.wait_ge(a_made, it * 4 + (hidden_base(l) + 2 * e + s + 1))
                            split_sum(m + 4 + s, s, it, turn)
                end_acc()

            pe.wait_ge(consts_made, 1)
            pe.wait_ge(cols_landed, 16)
            for l in range(LAYERS):
                norm(2 * l)
                mods(l)
                (first_mixer if l < DEPTH else gla if l == DEPTH else lru)(l)
                out_proj(l)
                norm(2 * l + 1)
                (peer if l < DEPTH else moe)(l)
            norm(2 * LAYERS)

        @block.scalar
        def _(act):
            steps = Steps(act, act_step)
            af = nc.scalar.activation

            def take(u, o, i, func=ACT.Copy, it=None, per=0, **kw):
                wait_full(act, u, it, per)
                af(o, i, func, **kw).then_inc(unit_taken[u % BANKS], 1)

            def norm(i):
                if i:
                    act.wait_ge(x_ready, i)
                else:
                    act.wait_ge(x_landed, 16)
                for half in range(2):
                    k = slice(half * (KT // 2), (half + 1) * (KT // 2))
                    af(sq[:, k, :], xT[:, k, :], ACT.Square).then_inc(sq_ready, 1)
                wait_taken(act, UNIT_OF["norm", i])
                af(rstd[:, :], rstd[:, :], ACT.Sqrt).then_inc(std_ready, 1)

            def first_mixer(l):
                qk, v = room(L1["qk"], TB, 640), room(L1["v"], TB, P)
                for b in range(TB):
                    u = UNIT_OF["q", l] + b
                    take(u, qk[:, b, 0:512], bank(u)[:, :])
                u = UNIT_OF["kv", l]
                kv = bank(u)[:, :].rearrange("p (b c) -> p b c", b=TB)
                wait_full(act, u)
                steps(af(qk[:, :, 512:640], kv[:, :, 0:P], ACT.Copy))
                take(u, v, kv[:, :, P:2 * P])
                suv = room(L1["suv"], TB, 512)
                for b in range(TB):
                    u = UNIT_OF["sgu", l] + b
                    take(u, suv[:, b, :], bank(u)[:, :])
                for i, name in enumerate(("cb", "cc")):
                    u = UNIT_OF["conv", l] + i
                    take(u, room(L1[name], 512), bank(u)[:, :])
                act.wait_ge(qk_var, l + 1)
                af(st[:, 0, 0:20], st[:, 0, 0:20], ACT.Sqrt).then_inc(qk_std, 1)
                act.wait_ge(vn_var, l + 1)
                af(st[:, 2, 0:8], st[:, 2, 0:8], ACT.Sqrt).then_inc(vn_std, 1)
                act.wait_ge(yc_ready, l + 1)
                af(room(L1["sq2"], 512), room(L1["yc"], 512), ACT.Square).then_inc(yc_sq, 1)
                pp, pT = room(L1["pp"], HEADS, T), room(L1["pT"], 24, P)
                for b in range(TB):
                    nk = P * (b + 1)
                    lg = room((SQ, L1["lg"])[b], HEADS, T)
                    act.wait_ge(lg_ready, 2 * l + b + 1)
                    if b:
                        wait_full(act, UNIT_OF["PT", l] + 1)
                    for h in range(HEADS):
                        steps(af(pp[:, h, 0:nk], lg[:, h, 0:nk], ACT.Exp, bias=st[:, 3, 8 * b + h:8 * b + h + 1],
                                 accum_out=st[:, 4, 8 * b + h:8 * b + h + 1]))
                    af(st[:, 5, 8 * b:8 * b + 8], st[:, 5, 8 * b:8 * b + 8], ACT.Exp).then_inc(exp_done, 1)
                    for c in range(2 * (b + 1)):
                        u = UNIT_OF["PT", l] + 2 * b + c
                        k = 8 * b + 4 * c
                        take(u, pT[:, k:k + 4, :], bank(u)[:, :].rearrange("p (a b) -> p a b", b=P))
                wait_taken(act, UNIT_OF["conv_sum", l])
                af(room(L1["rc"], T), room(L1["rc"], T), ACT.Sqrt).then_inc(yc_std, 1)
                act.wait_ge(ys_var, l + 1)
                af(st[:, 1, 20:22], st[:, 1, 20:22], ACT.Sqrt).then_inc(ys_std, 1)
                act.wait_ge(ya_var, l + 1)
                af(st[:, 1, 24:26], st[:, 1, 24:26], ACT.Sqrt).then_inc(ya_std, 1)

            def h_parts():
                af(h_hi[:, :, :], hT[:, :, :], ACT.Copy).then_inc(h_hi_made, 1)

            def a_part(a, src):
                af(a_hi[:, a, :], src, ACT.Copy).then_inc(a_hi_made, 1)

            def load_function(f):
                steps.sync()
                steps(af(psr[:, 14:15], one[:, :], f))

            def stage(l, kind, q):
                n = SLOT_OF[kind, l, q]
                act_q = arena[:, (q % 2) * 8192:(q % 2 + 1) * 8192]
                end = n + QT_SLOTS == SLOT_OF["up", l, 3] + QT_SLOTS

                def slot(s, it, last):
                    ahead = not (end and last and s >= QT_SLOTS - 2)
                    if ahead:
                        wait_half_read(act, n + s, it)
                        hi_part(act, n + s + 2, 0, it)
                    if kind == "down":
                        u, per = down_unit(l, q, s), down_units(q, s)
                        wait_full(act, u, it, per)
                    else:
                        act.wait_ge(acc_read, upto(QT_SLOTS * (QUARTERS * l + q) + s + 1, it, TURN))
                    if ahead:
                        hi_part(act, n + s + 2, 1, it)
                    if kind == "up" and not (last and s >= QT_SLOTS - 2):
                        at = (s + 2) * 512 if it is None else bass.ds(it * (TURN * 512) + (s + 2) * 512, 512)
                        a_part(s % 2, act_q[:, at:at + 512] if it is None else act_q[:, at])
                    if kind == "down":
                        take(u, act_q[:, bass.ds(it * (TURN * 512) + s * 512, 512)], bank(u)[:, :], ACT.Gelu,
                             it, per)

                if kind == "down":
                    for first in (0, LATE):
                        with act.Fori(0, LATE // TURN) as it:
                            steps.enter(it, 1)
                            load_function(ACT.Gelu)
                            for s in range(first, first + TURN):
                                slot(s, it, False)
                        steps.leave(LATE // TURN)
                        if q == 0:
                            b = first // LATE
                            act.wait_ge(best_ready, 2 * l + b + 1)
                            af(pick[:, 2, b, :], pick[:, 2, b, :], ACT.Exp).then_inc(gate_exp, 1)
                else:
                    wait_taken(act, gate_unit(l, q, T // GROUP - 1))
                    for s in range(2):
                        a_part(s, act_q[:, s * 512:(s + 1) * 512])
                    with act.Fori(0, QT_SLOTS // TURN - 1) as it:
                        for s in range(TURN):
                            slot(s, it, False)
                    for s in range(QT_SLOTS - TURN, QT_SLOTS):
                        slot(s, None, True)

            def peer(l):
                act.wait_ge(h_ready, 2 * l + 2)
                h_parts()
                qT = room(ACT1, 16, T)
                for s in range(8):
                    u = UNIT_OF["pq", l] + s
                    take(u, qT[:, 2 * s:2 * s + 2, :], bank(u)[:, :].rearrange("p (a b) -> p a b", b=T))
                S = room(TOP, TB, 16 * P)
                for b in range(TB):
                    for c in range(4):
                        u = UNIT_OF["keys", l] + 4 * b + c
                        take(u, S[:, b, c * 512:(c + 1) * 512], bank(u)[:, :])
                for s in range(2):
                    for half in range(2):
                        hi_part(act, SLOT_OF["down", l, 0] + s, half)
                for kind, q, _ in stages:
                    stage(l, kind, q)

            def gla(l):
                qT = room(L2["qT"], GH, T)
                for s in range(2):
                    u = UNIT_OF["gq", l] + s
                    take(u, qT[:, 2 * s:2 * s + 2, :], bank(u)[:, :].rearrange("p (a b) -> p a b", b=T),
                         scale=float(GDK) ** -0.5)
                u = UNIT_OF["alr", l]
                take(u, arena[0:GRANK, L2["alr"]:L2["alr"] + T], bank(u)[0:GRANK, 0:T])
                e = room(L2["e"], 1024)
                act.wait_ge(z_ready, 1)
                steps(af(e, e, ACT.Exp, scale=-1.0))
                steps.sync()
                af(e, e, ACT.Ln, bias=1.0).then_inc(soft_done, 1)
                k, v, gs = room(L2["k"], TB, 512), room(L2["v"], TB, 1024), room(L2["gs"], TB, 1024)
                for b in range(TB):
                    u = UNIT_OF["gk", l] + b
                    take(u, k[:, b, :], bank(u)[:, :])
                for name, o, f in (("gv", v, ACT.Copy), ("gg", gs, ACT.Silu)):
                    for c in range(2):
                        for b in range(TB):
                            u = UNIT_OF[name, l] + 2 * c + b
                            take(u, o[:, b, c * 512:(c + 1) * 512], bank(u)[:, :], f)
                for b in range(TB):
                    u = UNIT_OF["decay", l] + b
                    take(u, room(L2["lg"], TB, 512)[:, b, :], bank(u)[:, :], ACT.Exp)
                u = UNIT_OF["gamma", l]
                take(u, room(L2["gam"], 16), bank(u)[:, 0:16], ACT.Exp)
                act.wait_ge(o_var, 1)
                af(st[:, 0, 0:8], st[:, 0, 0:8], ACT.Sqrt).then_inc(o_std, 1)

            def lru(l):
                gate = room(L3["gate"], KT, T)
                act.wait_ge(lam_abs, 1)
                af(st[:, 0, 0:8], st[:, 0, 8:16], ACT.Exp, scale=-1.0).then_inc(lam_exp, 1)
                for s in range(4):
                    u = UNIT_OF["lru_g", l] + s
                    take(u, gate[:, 2 * s:2 * s + 2, :], bank(u)[:, :].rearrange("p (a b) -> p a b", b=T),
                         ACT.Gelu_apprx_tanh)
                xp = room(L3["xp"], KT, T + CONV2 - 1)
                for s in range(4):
                    u = UNIT_OF["lru_x", l] + s
                    take(u, xp[:, 2 * s:2 * s + 2, CONV2 - 1:], bank(u)[:, :].rearrange("p (a b) -> p a b", b=T))
                for name, o, bias in (("lru_r", "r", "lbr"), ("lru_i", "i", "lbi")):
                    ov = room(L3[o], KT, T)
                    for blk in range(4):
                        u = UNIT_OF[name, l] + blk
                        wait_full(act, u)
                        steps(af(ov[:, 2 * blk, :], bank(u)[:, 0:T], ACT.Sigmoid, bias=col(bias, 2 * blk)))
                        take(u, ov[:, 2 * blk + 1, :], bank(u)[:, T:2 * T], ACT.Sigmoid, bias=col(bias, 2 * blk + 1))
                r, t, a = room(L3["r"], KT, T), room(L3["t"], KT, T), room(L3["a"], KT, T)
                act.wait_ge(lam_ready, 1)
                for b in range(4):
                    wait_taken(act, UNIT_OF["lru_r", l] + b)
                steps.sync()
                for k in range(KT):
                    steps(af(t[:, k, :], r[:, k, :], ACT.Tanh, scale=st[:, 1, k:k + 1]))
                for k in range(KT):
                    ins = af(a[:, k, :], r[:, k, :], ACT.Exp, scale=st[:, 1, k:k + 1])
                    if k < KT - 1:
                        steps(ins)
                ins.then_inc(tanh_done, 1)
                act.wait_ge(m_sq, 1)
                af(room(L3["m"], 2048), room(L3["m"], 2048), ACT.Sqrt).then_inc(m_root, 1)

            def moe(l):
                act.wait_ge(h_ready, 2 * l + 2)
                h_parts()
                u = UNIT_OF["router", l]
                take(u, sel[:, 0, :], bank(u)[:, 0:32], ACT.Sigmoid)
                for s in range(2):
                    for half in range(2):
                        hi_part(act, SLOT_OF["experts", l] + s, half)
                u = UNIT_OF["combT", l]
                take(u, arena[0:16, MOE["cT"]:MOE["cT"] + T], bank(u)[0:16, 0:T])
                cb = room(MOE["cb"], EXPERTS, T)
                for c in range(8):
                    u = UNIT_OF["comb", l] + c
                    take(u, cb[:, 2 * c:2 * c + 2, :], bank(u)[:, :].rearrange("p (a b) -> p a b", b=T))
                si = room(MOE["si"], 2, 512)
                u = UNIT_OF["experts", l]
                n = SLOT_OF["experts", l]
                he = room(MOE["he"], 2, 512)
                turn = 2 * EXP_SLOTS

                def experts(it, last):
                    for e in range(2):
                        m = n + EXP_SLOTS * e
                        for s in range(4):
                            us = u + 4 * e + s
                            wait_half_read(act, m + s, it, turn)
                            hi_part(act, m + s + 2, 0, it, turn)
                            wait_full(act, us, it, 8)
                            hi_part(act, m + s + 2, 1, it, turn)
                            if s % 2 == 0:
                                wait_taken(act, us - 3, it, 8)
                                take(us, si[:, s // 2, :], bank(us)[:, :], ACT.Silu, it, 8)
                            if s >= 2:
                                act.wait_ge(he_made, it * 4 + (2 * EXPERTS * (l - DEPTH) + 2 * e + s - 1))
                                a_part(s - 2, he[:, s - 2, :])
                        for s in range(2):
                            if not (last and e == 1):
                                wait_half_read(act, m + 4 + s, it, turn)
                                hi_part(act, m + EXP_SLOTS + s, 0, it, turn)
                                act.wait_ge(acc_read, it * 4 + (hidden_base(l) + 2 * e + s + 1))
                                hi_part(act, m + EXP_SLOTS + s, 1, it, turn)

                with act.Fori(0, EXPERTS // 2 - 1) as it:
                    steps.enter(it, 1)
                    load_function(ACT.Silu)
                    experts(it, False)
                steps.leave(EXPERTS // 2 - 1)
                with act.Fori(EXPERTS // 2 - 1, EXPERTS // 2) as it:
                    experts(it, True)

            act.wait_ge(cols_landed, 16)
            af(cact[:, :, :], cols[:, 0:16].rearrange("p (a b) -> p a b", b=KT), ACT.Silu).then_inc(c_ready, 1)
            for l in range(LAYERS):
                norm(2 * l)
                (first_mixer if l < DEPTH else gla if l == DEPTH else lru)(l)
                norm(2 * l + 1)
                (peer if l < DEPTH else moe)(l)
            norm(2 * LAYERS)

        @block.vector
        def _(dve):
            v = nc.vector
            steps = Steps(dve, dve_step)
            ts, tt, stt = v.tensor_scalar, v.tensor_tensor, v.scalar_tensor_tensor

            def took(ins, u):
                ins.then_inc(unit_taken[u % BANKS], 1)

            def ada_pairs(rooms, landed, sums):
                c = cact[:, 0, :]
                for pair in range(0, len(rooms), 2):
                    for k in range(KT):
                        for i in range(pair, pair + 2):
                            if k == 0:
                                dve.wait_ge(landed[i], 16)
                            o = sums[:, i * 256:(i + 1) * 256].rearrange("p (a c) -> p a c", c=P)
                            a = rooms[i][:, :, k * P:(k + 1) * P]
                            if k == 0:
                                ins = ts(o, a, c[:, 0:1], None, ALU.mult)
                            else:
                                steps.sync(1 if k < KT - 1 else 1 - i % 2)
                                ins = stt(o, a, c[:, k:k + 1], o, ALU.mult, ALU.add)
                            if k < KT - 1:
                                steps(ins)
                            else:
                                ins.then_inc(ada0_done, 1)

            def ada_batch(b):
                ada_pairs([room(at, 2, D) for at in ADA_AT_2], batch_landed[b],
                          ada_sum[:, b * D:(b + 1) * D])

            def gain_of(i, l, g):
                steps(stt(gain[:, i, :], mod[:, 8 + 24 * i:16 + 24 * i], 1.0, col((g, l)), ALU.add, ALU.mult))
                steps.sync()

            def take_mods(u, l, first, end):
                wait_full(dve, u)
                at, _ = COLS["b_ada", l]
                took(tt(mod[:, first:end], bank(u)[:, first:end], cols[:, at + first:at + end], ALU.add), u)
                wait_taken(dve, u)

            def mods(l):
                if l:
                    dve.wait_ge(x_ready, 2 * l)
                take_mods(UNIT_OF["mod", l], l, 0, 48 if l else FIRST)
                gain_of(0, l, "g1")
                if l:
                    gain_of(1, l, "g2")

            def norm(i):
                u = UNIT_OF["norm", i]
                wait_full(dve, u)
                took(ts(rstd[:, :], bank(u)[:, 0:T], EPS, None, ALU.add), u)
                dve.wait_ge(std_ready, i + 1)
                steps(v.reciprocal(rstd[:, :], rstd[:, :]))
                steps.sync()
                steps(tt(hT[:, :, :], xT[:, :, :], spread(rstd[:, :], 1, [P, KT, T]), ALU.mult))
                steps.sync()
                if i % 2 == 0 and i < 2 * LAYERS:
                    mods(i // 2)
                for k in range(KT):
                    if i < 2 * LAYERS:
                        sh = (i % 2) * 24 + k
                        ins = ts(hT[:, k, :], hT[:, k, :], gain[:, i % 2, k:k + 1], mod[:, sh:sh + 1],
                                 ALU.mult, ALU.add)
                    else:
                        ins = ts(hT[:, k, :], hT[:, k, :], col("final_g", k), None, ALU.mult)
                    if k < KT - 1:
                        steps(ins)
                ins.then_inc(h_ready, 1)

            def residual(l):
                if l == 0:
                    take_mods(UNIT_OF["mod_rest", 0], 0, FIRST + SECOND, 48)
                    gain_of(1, 0, "g2")
                for s in range(4):
                    u = UNIT_OF["out", l] + s
                    wait_full(dve, u)
                    for j in range(2):
                        d = 2 * s + j
                        ins = stt(xT[:, d, :], bank(u)[:, j * T:(j + 1) * T], mod[:, 16 + d:17 + d],
                                  xT[:, d, :], ALU.mult, ALU.add)
                        if j:
                            took(ins, u)
                        else:
                            steps(ins)
                for s in range(4):
                    wait_taken(dve, UNIT_OF["out", l] + s)
                v.memset(psr[:, 15:16], 0.0).then_inc(x_ready, 1)

            def acc_residual(l):
                dve.wait_ge(acc_full, l + 1)
                for d in range(KT):
                    ins = stt(xT[:, d, :], acc[d // 2][:, (d % 2) * T:(d % 2 + 1) * T],
                              mod[:, 40 + d:41 + d], xT[:, d, :], ALU.mult, ALU.add)
                    if d < KT - 1:
                        steps(ins)
                ins.then_inc(x_ready, 1)

            def var(o, i, scale):
                return ts(o, i, scale, EPS, ALU.mult, ALU.add)

            def first_mixer(l):
                qk, suv = room(L1["qk"], TB, 640), room(L1["suv"], TB, 512)
                s3 = room(L1["sq3"], 1024)
                og = col(("og", l))
                if l == 0:
                    ada_batch(0)
                wait_taken(dve, UNIT_OF["q", l])
                wait_taken(dve, UNIT_OF["q", l] + 1)
                wait_taken(dve, UNIT_OF["kv", l])
                qsq = room(SQ, TB * 640)
                qf = room(L1["qk"], TB * 640)
                steps(tt(qsq, qf, qf, ALU.mult))
                steps.sync()
                rs = st[:, 0, 0:20]
                steps(v.tensor_reduce(rs, room(SQ, 20, HD), AX, ALU.add))
                steps.sync()
                var(rs, rs, 1.0 / HD).then_inc(qk_var, 1)
                for b in range(TB):
                    wait_taken(dve, UNIT_OF["sgu", l] + b)
                vn = room(L1["vn"], TB, 256)
                vn3 = room(L1["vn"], TB * 4, 64)
                mu = st[:, 2, 8:16]
                for b in range(TB):
                    steps(v.tensor_reduce(st[:, 2, 8 + 4 * b:12 + 4 * b],
                                          suv[:, b, 256:512].rearrange("p (g c) -> p g c", c=64), AX, ALU.add))
                steps.sync()
                steps(ts(mu, mu, 1.0 / 64, None, ALU.mult))
                steps.sync()
                for b in range(TB):
                    steps(tt(vn[:, b, :].rearrange("p (g c) -> p g c", c=64),
                             suv[:, b, 256:512].rearrange("p (g c) -> p g c", c=64),
                             spread(st[:, 2, 8 + 4 * b:12 + 4 * b], 2, [P, 4, 64]), ALU.subtract))
                steps.sync()
                vf = room(L1["vn"], 512)
                steps(tt(s3[:, 0:512], vf, vf, ALU.mult))
                steps.sync()
                steps(v.tensor_reduce(st[:, 2, 0:8], room(L1["sq3"], 8, 64), AX, ALU.add))
                steps.sync()
                var(st[:, 2, 0:8], st[:, 2, 0:8], 1.0 / 64).then_inc(vn_var, 1)
                dve.wait_ge(qk_std, l + 1)
                steps(v.reciprocal(rs, rs))
                steps.sync()
                q3 = room(L1["qk"], 20, HD)
                tt(q3, q3, spread(rs, 2, [P, 20, HD]), ALU.mult).then_inc(qk_ready, 1)
                dve.wait_ge(vn_std, l + 1)
                steps(v.reciprocal(st[:, 2, 0:8], st[:, 2, 0:8]))
                steps.sync()
                tt(vn3, vn3, spread(st[:, 2, 0:8], 2, [P, 8, 64]), ALU.mult).then_inc(vn_ready, 1)
                if l == 0:
                    ada_batch(1)
                z, cc = room(L1["z"], 2, T + 2), room(L1["cc"], 2, T)
                yc, cb = room(L1["yc"], 2, T), room(L1["cb"], 2, T)
                steps(v.memset(z[:, :, 0:2], 0.0))
                u = UNIT_OF["conv", l]
                wait_taken(dve, u)
                wait_taken(dve, u + 1)
                wait_full(dve, u + 2)
                took(tt(z[:, :, 2:], cc, bank(u + 2)[:, :].rearrange("p (a b) -> p a b", b=T), ALU.mult), u + 2)
                wait_taken(dve, u + 2)
                steps.sync()
                for j in range(3):
                    for k in range(2):
                        w_j = col(("cw", l), 2 * j + k)
                        if j == 0:
                            steps(ts(yc[:, k, :], z[:, k, 0:T], w_j, None, ALU.mult))
                        else:
                            steps.sync(1)
                            steps(stt(yc[:, k, :], z[:, k, j:j + T], w_j, yc[:, k, :], ALU.mult, ALU.add))
                steps.sync()
                tt(yc, yc, cb, ALU.mult).then_inc(yc_ready, 1)
                u = UNIT_OF["qkT", l]
                wait_full(dve, u)
                took(ts(room(L1["kT"], T), bank(u)[:, 0:T], col(("gk", l)), None, ALU.mult), u)
                for b in range(TB):
                    wait_full(dve, u + 1 + b)
                    took(ts(room(L1["qT"], TB, 512)[:, b, :], bank(u + 1 + b)[:, :], col(("gq", l)),
                            float(HD) ** -0.5, ALU.mult, ALU.mult), u + 1 + b)
                if l == 0:
                    take_mods(UNIT_OF["mod_next", 0], 0, FIRST, FIRST + SECOND)
                dve.wait_ge(bias_masked, l + 1)
                bias = room(L1["bias"], HEADS, T)
                sink = col(("sink", l))
                u = UNIT_OF["scores", l]
                for b in range(TB):
                    nk = P * (b + 1)
                    per = 512 // nk
                    lg = room((SQ, L1["lg"])[b], HEADS, T)
                    for c in range(HEADS // per):
                        wait_full(dve, u)
                        took(tt(lg[:, c * per:(c + 1) * per, 0:nk],
                                bank(u)[:, :].rearrange("p (h s) -> p h s", s=nk),
                                bias[:, c * per:(c + 1) * per, T - nk:T], ALU.add), u)
                        u += 1
                    for c in range(min(BANKS, HEADS // per)):
                        wait_taken(dve, u - 1 - c)
                    top = st[:, 2, 16 + 8 * b:24 + 8 * b]
                    steps(v.tensor_reduce(top, lg[:, :, 0:nk], AX, ALU.max))
                    steps.sync()
                    steps(tt(top, top, sink, ALU.max))
                    steps.sync()
                    steps(tt(st[:, 5, 8 * b:8 * b + 8], sink, top, ALU.subtract))
                    ts(st[:, 3, 8 * b:8 * b + 8], top, -1.0, None, ALU.mult).then_inc(lg_ready, 1)
                u = UNIT_OF["conv_sum", l]
                wait_full(dve, u)
                took(ts(room(L1["rc"], T), bank(u)[:, 0:T], float(D) / 256, EPS, ALU.mult, ALU.add), u)
                u = UNIT_OF["mix", l]
                wait_full(dve, u)
                ys = room(L1["ys"], TB, 256)
                for b in range(TB):
                    ins = tt(ys[:, b, :].rearrange("p (g c) -> p g c", c=64),
                             bank(u)[:, b * 256:(b + 1) * 256].rearrange("p (g c) -> p g c", c=64),
                             spread(col(("sb", l)), 2, [P, 4, 64]), ALU.add)
                    if b:
                        took(ins, u)
                    else:
                        steps(ins)
                wait_taken(dve, u)
                steps(tt(ys, ys, suv[:, :, 0:256], ALU.mult))
                steps.sync()
                for b in range(TB):
                    steps(v.tensor_tensor_reduce(out=s3[:, b * 256:(b + 1) * 256], in0=ys[:, b, :],
                                                 in1=ys[:, b, :], scale=1.0, scalar=0.0, op0=ALU.mult,
                                                 op1=ALU.add, accum_out=st[:, 1, 20 + b:21 + b]))
                steps.sync()
                var(st[:, 1, 20:22], st[:, 1, 20:22], 1.0 / 256).then_inc(ys_var, 1)
                ya = room(L1["ya"], TB, 512)
                for b in range(TB):
                    dve.wait_ge(exp_done, 2 * l + b + 1)
                    den = st[:, 4, 8 * b:8 * b + 8]
                    steps(tt(den, den, st[:, 5, 8 * b:8 * b + 8], ALU.add))
                    steps.sync()
                    steps(v.reciprocal(den, den))
                    steps.sync()
                    u = UNIT_OF["PV", l] + b
                    wait_full(dve, u)
                    took(tt(ya[:, b, :].rearrange("p (h c) -> p h c", c=64),
                            bank(u)[:, :].rearrange("p (h c) -> p h c", c=64),
                            spread(den, 2, [P, HEADS, 64]), ALU.mult), u)
                    wait_taken(dve, u)
                    steps(v.tensor_tensor_reduce(out=s3[:, 0:512], in0=ya[:, b, :],
                                                 in1=ya[:, b, :], scale=1.0, scalar=0.0, op0=ALU.mult,
                                                 op1=ALU.add, accum_out=st[:, 1, 24 + b:25 + b]))
                    steps.sync()
                var(st[:, 1, 24:26], st[:, 1, 24:26], 1.0 / 512).then_inc(ya_var, 1)
                dve.wait_ge(ys_std, l + 1)
                steps(v.reciprocal(st[:, 1, 20:22], st[:, 1, 20:22]))
                steps.sync()
                tt(ys, ys, spread(st[:, 1, 20:22], 2, [P, TB, 256]), ALU.mult).then_inc(ys_ready, 1)
                dve.wait_ge(ya_std, l + 1)
                steps(v.reciprocal(st[:, 1, 24:26], st[:, 1, 24:26]))
                steps.sync()
                tt(ya, ya, spread(st[:, 1, 24:26], 2, [P, TB, 512]), ALU.mult).then_inc(ya_ready, 1)
                rc = room(L1["rc"], T)
                dve.wait_ge(yc_std, l + 1)
                steps(v.reciprocal(rc, rc))
                steps.sync()
                for k in range(2):
                    steps(stt(mT[:, 4 + k, :], yc[:, k, :], og[:, 4 + k:5 + k], rc, ALU.mult, ALU.mult))
                u = UNIT_OF["sguT", l]
                wait_full(dve, u)
                took(tt(mT[:, 6:8, :], bank(u)[:, :].rearrange("p (a b) -> p a b", b=T),
                        spread(og[:, 6:8], 2, [P, 2, T]), ALU.mult), u)
                for b in range(TB):
                    u = UNIT_OF["attnT", l] + b
                    wait_full(dve, u)
                    took(tt(mT[:, 0:4, b * P:(b + 1) * P], bank(u)[:, :].rearrange("p (a b) -> p a b", b=P),
                            spread(og[:, 0:4], 2, [P, 4, P]), ALU.mult), u)
                v.memset(psr[:, 14:15], 0.0).then_inc(m_ready, 1)

            def best(b, l):
                S = room(TOP, TB, 16, P)
                work = S[:, b, :, :]
                for c in range(4):
                    wait_taken(dve, UNIT_OF["keys", l] + 4 * b + c)
                for g in range(16):
                    steps(v.max(tv[:, g, 0:8], S[:, b, g, :]))
                steps.sync()
                for g in range(16):
                    steps(v.max_index(ti[:, g, 0:8], tv[:, g, 0:8], S[:, b, g, :]))
                steps.sync()
                for g in range(16):
                    steps(v.match_replace(work[:, g, :], tv[:, g, 0:8], S[:, b, g, :], -3e38))
                steps.sync()
                for g in range(16):
                    steps(v.max(tv[:, g, 8:16], work[:, g, :]))
                steps.sync()
                for g in range(16):
                    steps(v.max_index(ti[:, g, 8:16], tv[:, g, 8:16], work[:, g, :]))
                steps.sync()
                steps(v.tensor_copy(tf[:, :, :], ti[:, :, :]))
                cand = room(CAND, PH, TOPK * TOPK)
                c4 = cand.rearrange("p h (a b) -> p h a b", b=TOPK)
                half = tv[:, :, :].rearrange("p (h s) a -> p h s a", s=2)
                steps(tt(c4, half[:, :, 0, :].unsqueeze(3).broadcast_to([P, PH, TOPK, TOPK]),
                         half[:, :, 1, :].unsqueeze(2).broadcast_to([P, PH, TOPK, TOPK]), ALU.add))
                steps.sync()
                bp3 = bp[:, 0, :].rearrange("p (h k) -> p h k", k=TOPK)
                for h in range(PH):
                    steps(v.max(bv[:, h, 0:8], cand[:, h, :]))
                steps.sync()
                for h in range(PH):
                    steps(v.max_index(bp3[:, h, 0:8], bv[:, h, 0:8], cand[:, h, :]))
                steps.sync()
                for h in range(PH):
                    steps(v.match_replace(cand[:, h, :], bv[:, h, 0:8], cand[:, h, :], -3e38))
                steps.sync()
                for h in range(PH):
                    steps(v.max(bv[:, h, 8:16], cand[:, h, :]))
                steps.sync()
                for h in range(PH):
                    steps(v.max_index(bp3[:, h, 8:16], bv[:, h, 8:16], cand[:, h, :]))
                g3 = pick[:, 2, b, :].rearrange("p (h k) -> p h k", k=TOPK)
                tt(g3, bv[:, :, :], bv[:, :, 0:1].broadcast_to([P, PH, TOPK]), ALU.subtract).then_inc(best_ready, 1)
                steps.sync()
                steps(ts(bp[:, 1, :], bp[:, 0, :], 4, None, ALU.logical_shift_right))
                steps(ts(bp[:, 2, :], bp[:, 0, :], TOPK - 1, None, ALU.bitwise_and))
                steps.sync()
                steps(v.tensor_copy(bf[:, :, :], bp[:, 1:3, :]))
                steps.sync()
                tfh = tf[:, :, :].rearrange("p (h s) a -> p h s a", s=2)
                eq = room(TOP + b * 2048, PH, TOPK, TOPK)
                for s in range(2):
                    steps(tt(eq, iota[:, 0:TOPK].unsqueeze(1).broadcast_to([P, PH * TOPK, TOPK]).rearrange(
                        "p (h k) a -> p h k a", h=PH),
                        bf[:, s, :].rearrange("p (h k) -> p h k", h=PH).unsqueeze(3).broadcast_to(
                            [P, PH, TOPK, TOPK]), ALU.is_equal))
                    steps.sync()
                    steps(tt(eq, eq, tfh[:, :, s, :].unsqueeze(2).broadcast_to([P, PH, TOPK, TOPK]), ALU.mult))
                    steps.sync()
                    steps(v.tensor_reduce(pick[:, s, b, :], eq.rearrange("p h k a -> p (h k) a"), AX, ALU.add))
                    steps.sync()

            def weigh(b, l):
                g3 = pick[:, 2, b, :].rearrange("p (h k) -> p h k", k=TOPK)
                dve.wait_ge(gate_exp, 2 * l + b + 1)
                steps(v.tensor_reduce(psr[:, 0:8], g3, AX, ALU.add))
                steps.sync()
                steps(v.reciprocal(psr[:, 0:8], psr[:, 0:8]))
                steps.sync()
                steps(tt(g3, g3, spread(psr[:, 0:8], 2, [P, PH, TOPK]), ALU.mult))
                steps.sync()

            def take_h_apart(l):
                dve.wait_ge(h_hi_made, l + 1)
                tt(h_lo[:, :, :], hT, h_hi[:, :, :].bitcast(F32), ALU.subtract).then_inc(h_made, 1)

            def build(l, gq, g, it, groups):
                at = pickT[:, :, bass.ds(it * (groups * GROUP) + g * GROUP, GROUP)] if it is not None else (
                    pickT[:, :, g * GROUP:(g + 1) * GROUP])
                gt = gateT[:, :, bass.ds(it * (groups * GROUP) + g * GROUP, GROUP)] if it is not None else (
                    gateT[:, :, g * GROUP:(g + 1) * GROUP])
                steps(tt(ohi, steps_of[:, :, :], spread(at[:, 0, :], 1, [P, P, GROUP]), ALU.is_equal))
                steps(tt(eqj, steps_of[:, gq * QT_TILES:(gq + 1) * QT_TILES, :],
                         spread(at[:, 1, :], 1, [P, QT_TILES, GROUP]), ALU.is_equal))
                steps.sync()
                tt(ohj, spread(eqj, 1, [P, 3, QT_TILES, GROUP]), spread(gt, 2, [P, 3, QT_TILES, GROUP]),
                   ALU.mult).then_inc(hot_ready, 1)

            def gate(l, gq, g, it, groups, per):
                u = gate_unit(l, gq, g)
                wait_full(dve, u, it, per)
                a = arena[:, (gq % 2) * 8192:(gq % 2 + 1) * 8192].rearrange("p (j t) -> p t j", t=T)
                a = (a[:, bass.ds(it * (groups * GROUP) + g * GROUP, GROUP), :] if it is not None else
                     a[:, g * GROUP:(g + 1) * GROUP, :])
                took(tt(a, a, bank(u)[:, :].rearrange("p (t j) -> p t j", j=QT_TILES), ALU.mult), u)

            def take_rest(n, it=None, turn=TURN):
                for half in range(2):
                    lo_part(dve, v, n, half, it, turn)

            def stage(l, kind, q, gq):
                n = SLOT_OF[kind, l, q]
                end = kind == "up" and q == QUARTERS - 1
                if gq is not None:
                    wait_taken(dve, down_unit(l, gq, QT_SLOTS - 1))

                def slot(s, it, last):
                    ahead = not (end and last and s >= QT_SLOTS - 2)
                    if ahead:
                        lo_part(dve, v, n + s + 2, 0, it)
                    if gq is not None:
                        wait_full(dve, gate_unit(l, gq, s), it, TURN)
                        if not (last and s == QT_SLOTS - 1):
                            build(l, gq, s + 1, it, TURN)
                        gate(l, gq, s, it, TURN, TURN)
                    if ahead:
                        lo_part(dve, v, n + s + 2, 1, it)

                if kind == "down":
                    with dve.Fori(0, QT_SLOTS // TURN) as it:
                        for s in range(TURN):
                            slot(s, it, False)
                    return
                if gq is not None:
                    build(l, gq, 0, None, 0)
                with dve.Fori(0, QT_SLOTS // TURN - 1) as it:
                    steps.enter(it, 0 if gq is None else 2 * TURN)
                    for s in range(TURN):
                        slot(s, it, False)
                steps.leave(QT_SLOTS // TURN - 1)
                for s in range(QT_SLOTS - TURN, QT_SLOTS):
                    slot(s, None, True)

            def peer(l):
                take_h_apart(l)
                for b in range(TB):
                    best(b, l)
                for b in range(TB):
                    weigh(b, l)
                v.memset(psr[:, 13:14], 0.0).then_inc(pick_ready, 1)
                u = UNIT_OF["idxT", l]
                wait_full(dve, u)
                took(v.tensor_copy(pickT[:, :, :], bank(u)[:, :].rearrange("p (a b) -> p a b", b=T)), u)
                wait_full(dve, u + 1)
                rest = rstd[:, :]
                steps(v.tensor_copy(gateT[:, 0, :], bank(u + 1)[:, 0:T]))
                steps.sync()
                took(tt(rest, bank(u + 1)[:, 0:T], gateT[:, 0, :], ALU.subtract), u + 1)
                wait_taken(dve, u + 1)
                steps(v.tensor_copy(gateT[:, 1, :], rest))
                steps.sync()
                steps(tt(rest, rest, gateT[:, 1, :], ALU.subtract))
                steps.sync()
                steps(v.tensor_copy(gateT[:, 2, :], rest))
                steps.sync()
                wait_taken(dve, u)
                wait_taken(dve, down_unit(l, 0, QT_SLOTS - 1))
                groups, turns = 2 * TURN, LATE // TURN

                def late(g, it, last):
                    wait_full(dve, gate_unit(l, 0, g), it, 3 * TURN)
                    if not last:
                        build(l, 0, g + 1, it, groups)
                    gate(l, 0, g, it, groups, 3 * TURN)

                build(l, 0, 0, None, 0)
                with dve.Fori(0, turns - 1) as it:
                    steps.enter(it, 2 * groups)
                    for g in range(groups):
                        late(g, it, False)
                steps.leave(turns - 1)
                for g in range(groups * (turns - 1), groups * turns):
                    late(g, None, g == groups * turns - 1)
                for kind, q, gq in stages[2:]:
                    stage(l, kind, q, gq)
                acc_residual(l)

            def gla(l):
                zz, e = room(L2["zz"], TB, 512), room(L2["e"], TB, 512)
                dve.wait_ge(const_landed, 16 * (DEPTH + 1))
                u = UNIT_OF["z", l]
                for b in range(TB):
                    wait_full(dve, u + b)
                    took(tt(zz[:, b, :], bank(u + b)[:, :], room(L2["bg"], 512), ALU.add), u + b)
                for b in range(TB):
                    wait_taken(dve, u + b)
                stt(e, zz, -1.0, zz, ALU.mult, ALU.max).then_inc(z_ready, 1)
                steps(ts(zz, zz, 0.0, None, ALU.min))
                dve.wait_ge(soft_done, 1)
                steps.sync()
                tt(zz, zz, e, ALU.subtract).then_inc(la_ready, 1)
                gs = room(L2["gs"], TB * GH, GDV)
                for i in range(4):
                    wait_taken(dve, UNIT_OF["gg", l] + i)
                steps(tt(gs, gs, spread(room(L2["ng"], GDV), 1, [P, TB * GH, GDV]), ALU.mult))
                kd = room(L2["kd"], 1024)
                for b in range(TB):
                    wait_taken(dve, UNIT_OF["decay", l] + b)
                    wait_taken(dve, UNIT_OF["gk", l] + b)
                tt(kd, room(L2["k"], 1024), room(L2["lg"], 1024), ALU.mult).then_inc(kd_ready, 1)
                S, gam = room(L2["S"], 2, GH, GDV), room(L2["gam"], 16)
                wait_taken(dve, UNIT_OF["gamma", l])
                u = UNIT_OF["kvs", l]
                for c in range(T // CHUNK):
                    if c >= 2:
                        dve.wait_ge(o_full, c - 1)
                    for a in range(2):
                        ua = u + 2 * c + a
                        wait_full(dve, ua)
                        if c == 0:
                            took(v.tensor_copy(S[:, 0, 2 * a:2 * a + 2, :],
                                               bank(ua)[:, :].rearrange("p (a b) -> p a b", b=GDV)), ua)
                        else:
                            for h in range(2 * a, 2 * a + 2):
                                ins = stt(S[:, c % 2, h, :], S[:, (c - 1) % 2, h, :],
                                          gam[:, 4 * h + c:4 * h + c + 1],
                                          bank(ua)[:, (h % 2) * GDV:(h % 2 + 1) * GDV], ALU.mult, ALU.add)
                                if h % 2:
                                    took(ins, ua)
                                else:
                                    steps(ins)
                    wait_taken(dve, u + 2 * c)
                    wait_taken(dve, u + 2 * c + 1)
                o, osq = room(L2["o"], TB, 1024), room(L2["osq"], 2048)
                of = room(L2["o"], 2048)
                for b in range(TB):
                    dve.wait_ge(o_full, 2 * b + 2)
                    for a in range(2):
                        steps(v.tensor_copy(o[:, b, a * 512:(a + 1) * 512], acc[2 * b + a][:, :]))
                steps.sync()
                steps(tt(osq, of, of, ALU.mult))
                steps.sync()
                rs = st[:, 0, 0:8]
                steps(v.tensor_reduce(rs, room(L2["osq"], 8, GDV), AX, ALU.add))
                steps.sync()
                var(rs, rs, 1.0 / GDV).then_inc(o_var, 1)
                steps(tt(of, of, room(L2["gs"], 2048), ALU.mult))
                dve.wait_ge(o_std, 1)
                steps(v.reciprocal(rs, rs))
                steps.sync()
                o3 = room(L2["o"], 8, GDV)
                tt(o3, o3, spread(rs, 2, [P, 8, GDV]), ALU.mult).then_inc(o_ready, 1)
                u = UNIT_OF["oT", l]
                for b in range(TB):
                    for c in range(2):
                        wait_full(dve, u)
                        took(v.tensor_copy(mT[:, 4 * c:4 * c + 4, b * P:(b + 1) * P],
                                           bank(u)[:, :].rearrange("p (a b) -> p a b", b=P)), u)
                        u += 1
                v.memset(psr[:, 14:15], 0.0).then_inc(m_ready, 1)

            def lru(l):
                lam, s, s2, p = col("lam"), st[:, 2, 0:8], st[:, 2, 8:16], st[:, 2, 16:24]
                stt(st[:, 0, 8:16], lam, -1.0, lam, ALU.mult, ALU.max).then_inc(lam_abs, 1)
                xp = room(L3["xp"], KT, T + CONV2 - 1)
                steps(v.memset(xp[:, :, 0:CONV2 - 1], 0.0))
                dve.wait_ge(lam_exp, 1)
                steps(ts(s, st[:, 0, 0:8], 2.0, None, ALU.add))
                steps.sync()
                steps(v.reciprocal(s, s))
                steps.sync()
                steps(tt(s, s, st[:, 0, 0:8], ALU.mult))
                steps.sync()
                steps(tt(s2, s, s, ALU.mult))
                steps.sync()
                steps(ts(p, s2, 1.0 / 15, 1.0 / 13, ALU.mult, ALU.add))
                for n in (11, 9, 7, 5, 3, 1):
                    steps.sync()
                    steps(tt(p, p, s2, ALU.mult))
                    steps.sync()
                    steps(ts(p, p, 1.0 / n, None, ALU.add))
                steps.sync()
                steps(tt(p, p, s, ALU.mult))
                steps(ts(s2, lam, -1.0, 0.0, ALU.mult, ALU.max))
                steps.sync()
                steps(stt(p, p, 2.0, s2, ALU.mult, ALU.add))
                steps.sync()
                ts(st[:, 1, 0:8], p, -8.0, None, ALU.mult).then_inc(lam_ready, 1)
                xc = room(L3["xc"], KT, T)
                for i in range(4):
                    wait_taken(dve, UNIT_OF["lru_x", l] + i)
                    for j in range(CONV2):
                        for k in range(2 * i, 2 * i + 2):
                            w_j = col("lcw", 8 * j + k)
                            if j == 0:
                                steps(ts(xc[:, k, :], xp[:, k, 0:T], w_j, col("lcb", k), ALU.mult, ALU.add))
                                continue
                            steps.sync(1)
                            ins = stt(xc[:, k, :], xp[:, k, j:j + T], w_j, xc[:, k, :], ALU.mult, ALU.add)
                            if j == CONV2 - 1 and k == KT - 1:
                                ins.then_inc(xc_ready, 1)
                            else:
                                steps(ins)
                a, i_, t, m = (room(L3[n], 2048) for n in ("a", "i", "t", "m"))
                b_, hs = room(L3["b"], KT, T), room(L3["hs"], KT, T)
                dve.wait_ge(xc_ready, 1)
                for n in range(4):
                    wait_taken(dve, UNIT_OF["lru_i", l] + n)
                steps(tt(room(L3["b"], 2048), room(L3["xc"], 2048), i_, ALU.mult))
                dve.wait_ge(tanh_done, 1)
                steps(tt(m, a, a, ALU.mult))
                steps.sync()
                steps(stt(m, m, 1.0, t, ALU.add, ALU.mult))
                steps.sync()
                ts(m, m, -1.0, 1e-34, ALU.mult, ALU.max).then_inc(m_sq, 1)
                dve.wait_ge(m_root, 1)
                steps(tt(room(L3["b"], 2048), room(L3["b"], 2048), m, ALU.mult))
                steps.sync()
                a3 = room(L3["a"], KT, T)
                for k in range(KT):
                    steps(v.tensor_tensor_scan(hs[:, k, :], a3[:, k, :], b_[:, k, :], 0.0, ALU.mult, ALU.add))
                steps.sync()
                for n in range(4):
                    wait_taken(dve, UNIT_OF["lru_g", l] + n)
                tt(mT, hs, room(L3["gate"], KT, T), ALU.mult).then_inc(m_ready, 1)

            def route(l):
                u = UNIT_OF["router", l]
                wait_taken(dve, u)
                scores, biased = sel[:, 0, :], sel[:, 1, :]
                steps(tt(biased.rearrange("p (b e) -> p b e", b=TB), scores.rearrange("p (b e) -> p b e", b=TB),
                         spread(col("rb"), 1, [P, TB, EXPERTS]), ALU.add))
                steps.sync()
                x4 = biased.rearrange("p (g e) -> p g e", e=4)
                r2, r3 = sel[:, 2, :], sel[:, 3, :]
                for i, (e, op) in enumerate(((0, ALU.max), (0, ALU.min), (2, ALU.max), (2, ALU.min))):
                    steps(tt(r2[:, 8 * i:8 * i + 8], x4[:, :, e], x4[:, :, e + 1], op))
                steps.sync()
                steps(tt(r3[:, 0:8], r2[:, 0:8], r2[:, 16:24], ALU.max))
                steps(tt(r3[:, 8:16], r2[:, 0:8], r2[:, 16:24], ALU.min))
                steps(tt(r3[:, 16:24], r2[:, 8:16], r2[:, 24:32], ALU.max))
                steps(v.memset(sel[:, 4, 0:16], NEG))
                steps.sync()
                steps(tt(r3[:, 24:32], r3[:, 8:16], r3[:, 16:24], ALU.max))
                steps.sync()
                gs = sel[:, 4, 0:16].rearrange("p (b e) -> p b e", b=TB)
                steps(tt(gs[:, :, 0:4], r3[:, 0:8].rearrange("p (b e) -> p b e", b=TB),
                         r3[:, 24:32].rearrange("p (b e) -> p b e", b=TB), ALU.add))
                steps.sync()
                top = sel[:, 5, :]
                for b in range(TB):
                    steps(v.max(top[:, 8 * b:8 * b + 8], gs[:, b, :]))
                steps.sync()
                for b in range(TB):
                    steps(v.max_index(seli[:, b, :], top[:, 8 * b:8 * b + 8], gs[:, b, :]))
                steps.sync()
                steps(v.tensor_copy(top[:, 16:18], seli[:, :, 0]))
                steps.sync()
                pickg = sel[:, 6, :]
                for b in range(TB):
                    steps(ts(pickg[:, 4 * b:4 * b + 4], iota[:, 0:4], top[:, 16 + b:17 + b], None, ALU.is_equal))
                steps.sync()
                steps(ts(pickg[:, 8:16], pickg[:, 0:8], 1.0, -NEG, ALU.subtract, ALU.mult))
                steps(tt(r2.rearrange("p (g e) -> p g e", e=4), x4, spread(pickg[:, 0:8], 2, [P, 8, 4]), ALU.mult))
                steps.sync()
                steps(tt(r2.rearrange("p (g e) -> p g e", e=4), r2.rearrange("p (g e) -> p g e", e=4),
                         spread(pickg[:, 8:16], 2, [P, 8, 4]), ALU.add))
                steps.sync()
                for b in range(TB):
                    steps(v.max(top[:, 8 * b:8 * b + 8], r2[:, 16 * b:16 * b + 16]))
                steps.sync()
                for b in range(TB):
                    steps(v.max_index(seli[:, b, :], top[:, 8 * b:8 * b + 8], r2[:, 16 * b:16 * b + 16]))
                steps.sync()
                steps(v.tensor_copy(top[:, 16:20].rearrange("p (b e) -> p b e", b=TB), seli[:, :, 0:2]))
                steps.sync()
                for b in range(TB):
                    steps(ts(r3[:, 16 * b:16 * b + 16], iota[:, 0:16], top[:, 16 + 2 * b:17 + 2 * b], None,
                             ALU.is_equal))
                steps.sync()
                for b in range(TB):
                    steps(stt(r3[:, 16 * b:16 * b + 16], iota[:, 0:16], top[:, 17 + 2 * b:18 + 2 * b],
                              r3[:, 16 * b:16 * b + 16], ALU.is_equal, ALU.add))
                steps.sync()
                steps(tt(r3, r3, scores, ALU.mult))
                steps.sync()
                r3b = r3.rearrange("p (b e) -> p b e", b=TB)
                steps(v.tensor_reduce(top[:, 20:22], r3b, AX, ALU.add))
                steps.sync()
                steps(v.reciprocal(top[:, 20:22], top[:, 20:22]))
                steps.sync()
                tt(sel[:, 7, :].rearrange("p (b e) -> p b e", b=TB), r3b,
                   spread(top[:, 20:22], 2, [P, TB, EXPERTS]), ALU.mult).then_inc(comb_ready, 1)

            def moe(l):
                route(l)
                take_h_apart(l)
                for s in range(2):
                    take_rest(SLOT_OF["experts", l] + s)
                for c in range(BANKS):
                    wait_taken(dve, UNIT_OF["comb", l] + 7 - c)
                u = UNIT_OF["experts", l]
                he, si = room(MOE["he"], 2, 512), room(MOE["si"], 2, 512)
                cb = arena[:, MOE["cb"]:MOE["cb"] + EXPERTS * T]
                n = SLOT_OF["experts", l]
                turn = 2 * EXP_SLOTS

                def hidden(e, s, it):
                    ug = u + 4 * e + 2 * s
                    wait_taken(dve, ug, it, 8)
                    wait_full(dve, ug + 1, it, 8)
                    took(tt(he[:, s, :], si[:, s, :], bank(ug + 1)[:, :], ALU.mult), ug + 1)
                    wait_taken(dve, ug + 1, it, 8)
                    h2 = he[:, s, :].rearrange("p (a b) -> p a b", b=T)
                    c = cb[:, bass.ds(it * (2 * T) + e * T, T)]
                    tt(h2, h2, spread(c, 1, [P, 2, T]), ALU.mult).then_inc(he_made, 1)

                def experts(it, last):
                    for e in range(2):
                        m = n + EXP_SLOTS * e
                        base = hidden_base(l) + 2 * e
                        take_rest(m + 2, it, turn)
                        take_rest(m + 3, it, turn)
                        hidden(e, 0, it)
                        take_rest(m + 4, it, turn)
                        a_rest(dve, v, base + 1, it, 4, 0, he[:, 0, :])
                        take_rest(m + 5, it, turn)
                        hidden(e, 1, it)
                        a_rest(dve, v, base + 2, it, 4, 1, he[:, 1, :])
                        for s in range(2):
                            if not (last and e == 1):
                                take_rest(m + EXP_SLOTS + s, it, turn)

                with dve.Fori(0, EXPERTS // 2 - 1) as it:
                    experts(it, False)
                with dve.Fori(EXPERTS // 2 - 1, EXPERTS // 2) as it:
                    experts(it, True)
                acc_residual(l)

            dve.wait_ge(consts_made, 1)
            dve.wait_ge(cols_landed, 16)
            dve.wait_ge(x_landed, 16)
            dve.wait_ge(c_ready, 1)
            ada_pairs([room(at, 2, D) for at in ADA_AT], ada0_landed, ada_sum)
            for l in range(LAYERS):
                norm(2 * l)
                (first_mixer if l < DEPTH else gla if l == DEPTH else lru)(l)
                residual(l)
                norm(2 * l + 1)
                (peer if l < DEPTH else moe)(l)
            norm(2 * LAYERS)


def _t5_buckets():
    d = np.arange(P)
    exact = BUCKETS // 2
    ratio = np.log(np.maximum(d, 1).astype(np.float32) / np.float32(exact)) / np.float32(
        np.log(MAX_DIST / exact))
    large = np.minimum(exact + (ratio * np.float32(BUCKETS - exact)).astype(np.int32), BUCKETS - 1)
    return np.where(d < exact, d, large)


def _tiles(a):
    n = a.shape[1] // 256
    return a.reshape(KT, P, n, 2, P).transpose(2, 1, 3, 0, 4).reshape(n, P, SLOT)


def _rows(a):
    m = a.shape[1] // 512
    return a.reshape(2, 4, P, m, 512).transpose(3, 0, 2, 1, 4).reshape(2 * m, P, SLOT)


def _stream(i):
    w = np.empty((SLOT_OF["end"], P, SLOT), np.float32)

    def put(name, a):
        w[SLOT_OF[name]:SLOT_OF[name] + len(a)] = a

    q_order = np.concatenate([np.arange(HD) + HD * ((h % 2) * 4 + h // 2) for h in range(HEADS)])
    for l in range(DEPTH):
        a = i["w_in"][l]
        put(("q", l), _rows(a[:, q_order]))
        put(("kv", l), a[:, 512:768].reshape(KT, P, 256).transpose(1, 0, 2).reshape(1, P, SLOT))
        put(("sgu", l), _rows(a[:, 1536:2048]))
        put(("conv", l), _tiles(a[:, 768:1536]))
        put(("out", l), _tiles(i["w_out"][l]))
        put(("pq", l), _tiles(i["peer_wq"][l]))
        put(("keys", l), i["peer_sub_keys"][l].transpose(3, 0, 1, 2).reshape(1, P, SLOT))
        down = i["peer_down"][l].reshape(P, 64, 2, KT, P).transpose(1, 4, 2, 3, 0).reshape(64, P, SLOT)
        up = i["peer_up"][l].reshape(P, 64, SLOT).transpose(1, 0, 2)
        for q in range(QUARTERS):
            put(("down", l, q), down[q * QT_SLOTS:(q + 1) * QT_SLOTS])
            put(("up", l, q), up[q * QT_SLOTS:(q + 1) * QT_SLOTS])
        m = DEPTH + l
        gate, up_, dn = i["moe_w_gate_2"][l], i["moe_w_up_2"][l], i["moe_w_down_2"][l]
        ex = np.empty((EXPERTS, EXP_SLOTS, P, SLOT), np.float32)
        for e in range(EXPERTS):
            ex[e, 0:4:2] = _tiles(gate[e])
            ex[e, 1:4:2] = _tiles(up_[e])
            ex[e, 4:6] = dn[e].reshape(2, 2, P, D).transpose(0, 2, 1, 3).reshape(2, P, SLOT)
        put(("experts", m), ex.reshape(EXPERTS * EXP_SLOTS, P, SLOT))
    l = DEPTH
    a = i["gla_w_in_2"][0]
    put(("gq", l), _tiles(a[:, 0:512]))
    put(("gk", l), _rows(a[:, 512:1024]))
    put(("gv", l), _rows(a[:, 1024:2048]))
    put(("gg", l), _rows(a[:, 2048:3072]))
    put(("out", l), _tiles(i["gla_w_out_2"][0]))
    l = DEPTH + 1
    a = i["lru_w_in_2"][0]
    put(("lru_g", l), _tiles(a[:, 0:D]))
    put(("lru_x", l), _tiles(a[:, D:2 * D]))
    for name, key in (("lru_r", "lru_w_r_2"), ("lru_i", "lru_w_i_2")):
        put((name, l), i[key][0].reshape(4, 2, P, 2, P).transpose(2, 0, 3, 1, 4).reshape(1, P, SLOT))
    put(("out", l), _tiles(i["lru_w_out_2"][0]))
    return w


def _ada(i):
    a = np.concatenate([i["w_ada"], i["ada_w_2"]])
    return np.ascontiguousarray(a.reshape(LAYERS, KT, P, 48, P).transpose(0, 3, 2, 1, 4).reshape(
        LAYERS, 48, P, D))


def _small(i):
    t = np.zeros((P, NCOLS), np.float32)

    def put(name, a):
        at, n = COLS[name]
        t[:, at:at + n] = a

    def vec(a):
        return a.reshape(-1, P).T

    put("c", vec(i["c"][0]))
    put("c2", vec(i["c_2"][0]))
    put("final_g", vec(i["final_norm_g_2"]))
    for l in range(LAYERS):
        first, m = l < DEPTH, l % DEPTH
        put(("b_ada", l), vec(i["b_ada" if first else "ada_b_2"][m]))
        put(("g1", l), vec(i["norm1_g" if first else "norm_mix_g_2"][m]))
        put(("g2", l), vec(i["norm2_g" if first else "norm_ffn_g_2"][m]))
    for l in range(DEPTH):
        put(("gq", l), np.tile(i["q_norm_g"][l], 2)[:, None])
        put(("gk", l), np.tile(i["k_norm_g"][l], 2)[:, None])
        put(("cw", l), vec(i["conv_w"][l].reshape(-1)))
        put(("og", l), vec(i["out_norm_g"][l]))
        put(("sb", l), i["sgu_b"][l].T)
        put(("sink", l), i["attn_sink"][l][None, :])
    put("lcw", vec(i["lru_conv_w_2"][0].reshape(-1)))
    put("lcb", vec(i["lru_conv_b_2"][0]))
    put("lbr", vec(i["lru_b_r_2"][0].reshape(-1)))
    put("lbi", vec(i["lru_b_i_2"][0].reshape(-1)))
    put("lam", vec(i["lru_lambda_2"][0]))
    put("rw", i["router_w_2"].reshape(KT, P, EXPERTS).transpose(1, 0, 2).reshape(P, -1))
    put("rb", i["router_bias_2"][None, :])
    return t


def _first_const(i):
    dist = np.clip(np.arange(P)[:, None] + P - np.arange(T)[None, :], 0, P - 1)
    bias = i["rel_bias"][_t5_buckets()[dist]].transpose(0, 2, 1).reshape(P, -1)
    t = np.empty((DEPTH, P, FIRST_CONST), np.float32)
    t[:, :, 0:2048] = bias
    t[:, :, 2048:2560] = i["sgu_w"].transpose(0, 3, 1, 2).reshape(DEPTH, P, 512)
    return t


def _gla_const(i):
    t = np.zeros((P, GLA_CONST), np.float32)
    t[:, L2["bg"]:L2["bg"] + 512] = i["gla_b_gate_2"][0]
    t[:, L2["ng"]:L2["ng"] + 256] = i["gla_norm_g_2"][0]
    t[0:GRANK, L2["wgu"]:L2["wgu"] + 512] = i["gla_w_gate_up_2"][0]
    t[:, L2["wa"]:L2["wa"] + 128] = i["gla_w_in_2"][0][:, 3072:].reshape(KT, P, GRANK).transpose(
        1, 0, 2).reshape(P, -1)
    return t


def kernel(**inputs):
    import concourse.bacc as bacc
    from concourse.bass_utils import run_bass_kernel_spmd

    i = {k: np.asarray(v) for k, v in inputs.items()}
    arrays = {
        "x_t": np.ascontiguousarray(i["x"][0].T),
        "stream": _stream(i),
        "ada": _ada(i),
        "small": _small(i),
        "first_const": _first_const(i),
        "gla_const": _gla_const(i),
    }
    nc = bacc.Bacc("TRN2", target_bir_lowering=False, num_devices=1)
    args = [nc.dram_tensor(k, a.shape, F32, kind="ExternalInput").ap() for k, a in arrays.items()]
    args.append(nc.dram_tensor("out_t", (D, T), F32, kind="ExternalOutput").ap())
    program(nc, *args)
    r = run_bass_kernel_spmd(nc, [arrays], core_ids=[0])
    return np.ascontiguousarray(r.results[0]["out_t"].T)[None]
```
